# Optimizing a Trainium2 kernel written in Bass

```python
import jax, jax.numpy as jnp
from jax import lax
import numpy as np

D_MODEL = 1024
BATCH = 1
SEQ = 1024
DEPTH = 1

N_MEM = 256
DN_HEADS = 4
DN_HEAD_DIM = 128
DN_CONV = 4
DN_CHUNK = 64
SA_HEADS = 4
SA_HEAD_DIM = 64
SA_KV_RANK = 128
IDX_HEADS = 8
IDX_DIM = 64
IDX_TOPK_MAX = 256
QBLOCK = 128
MEM_HEADS = 4
MEM_HEAD_DIM = 64

DN_WIDTH = DN_HEADS * DN_HEAD_DIM
SA_WIDTH = SA_HEADS * SA_HEAD_DIM
MEM_WIDTH = MEM_HEADS * MEM_HEAD_DIM
MIX_WIDTH = DN_WIDTH + SA_WIDTH + MEM_WIDTH

IN_SPLITS = (
    DN_WIDTH, DN_WIDTH, DN_WIDTH, DN_WIDTH, DN_HEADS, DN_HEADS,
    SA_WIDTH, SA_KV_RANK, SA_WIDTH, IDX_HEADS * IDX_DIM, IDX_DIM, IDX_HEADS,
    MEM_WIDTH, MEM_WIDTH,
)
IN_WIDTH = sum(IN_SPLITS)

DEEPNORM_ALPHA = (2.0 * DEPTH) ** 0.25
DEEPNORM_BETA = (8.0 * DEPTH) ** -0.25
LN_EPS = 1e-5
RMS_EPS = 1e-6

kernel_name = 'hybrid_deltanet_dsa_memory_deepnorm'

def _split_points(widths):
    pts, acc = [], 0
    for w in widths[:-1]:
        acc += w
        pts.append(acc)
    return pts

def _alibi_slopes(n):
    return np.array([2.0 ** (-8.0 * (i + 1) / n) for i in range(n)], dtype=np.float32)

def _rmsnorm_f32(x, w):
    xf = x.astype(jnp.float32)
    return xf * lax.rsqrt(jnp.mean(xf * xf, axis=-1, keepdims=True) + RMS_EPS) * w.astype(jnp.float32)

def _l2norm(x):
    return x * lax.rsqrt(jnp.sum(x * x, axis=-1, keepdims=True) + RMS_EPS)

def _layernorm(x, g, b):
    xf = x.astype(jnp.float32)
    mu = jnp.mean(xf, axis=-1, keepdims=True)
    var = jnp.mean(jnp.square(xf - mu), axis=-1, keepdims=True)
    y = (xf - mu) * lax.rsqrt(var + LN_EPS) * g.astype(jnp.float32) + b.astype(jnp.float32)
    return y.astype(x.dtype)

def _short_conv(x, w):
    return lax.conv_general_dilated(
        x, w[:, None, :].astype(x.dtype), window_strides=(1,), padding=[(DN_CONV - 1, 0)],
        dimension_numbers=('NWC', 'WIO', 'NWC'), feature_group_count=x.shape[-1])

def _gated_delta_rule(q, k, v, g, beta):
    B_, S_, H, Dk = q.shape
    Dv = v.shape[-1]
    C = DN_CHUNK
    N = S_ // C
    q = _l2norm(q) * (Dk ** -0.5)
    k = _l2norm(k)

    def chunks(t):
        return t.reshape(B_, N, C, H, t.shape[-1]).transpose(0, 3, 1, 2, 4)

    q, k, v = chunks(q), chunks(k), chunks(v)
    beta = beta.reshape(B_, N, C, H).transpose(0, 3, 1, 2)
    g = jnp.cumsum(g.reshape(B_, N, C, H).transpose(0, 3, 1, 2), axis=-1)
    causal = jnp.tril(jnp.ones((C, C), dtype=bool))
    strict = jnp.tril(jnp.ones((C, C), dtype=bool), -1)
    decay = jnp.exp(jnp.where(causal, g[..., :, None] - g[..., None, :], -jnp.inf))
    k_beta = k * beta[..., None]
    lower = jnp.where(strict, jnp.einsum('bhncd,bhnsd->bhncs', k_beta, k) * decay, 0.0)
    m = lower + jnp.eye(C, dtype=jnp.float32)
    rhs = jnp.concatenate([v * beta[..., None], k_beta * jnp.exp(g)[..., None]], axis=-1)
    sol = lax.linalg.triangular_solve(m, rhs, left_side=True, lower=True)
    u, w = sol[..., :Dv], sol[..., Dv:]
    attn = jnp.where(causal, jnp.einsum('bhncd,bhnsd->bhncs', q, k) * decay, 0.0)
    g_last = g[..., -1:]
    k_dec = k * jnp.exp(g_last - g)[..., None]
    q_dec = q * jnp.exp(g)[..., None]
    xs = tuple(jnp.moveaxis(t, 2, 0) for t in (q_dec, k_dec, u, w, attn, jnp.exp(g_last)))

    def step(state, inp):
        qg, kd, u_i, w_i, a_i, gl = inp
        v_new = u_i - jnp.einsum('bhcd,bhde->bhce', w_i, state)
        o = jnp.einsum('bhcd,bhde->bhce', qg, state) + jnp.einsum('bhcs,bhse->bhce', a_i, v_new)
        state = state * gl[..., None] + jnp.einsum('bhcd,bhce->bhde', kd, v_new)
        return state, o

    s0 = jnp.zeros((B_, H, Dk, Dv), jnp.float32)
    _, o = lax.scan(step, s0, xs)
    return jnp.moveaxis(o, 0, 2).transpose(0, 2, 3, 1, 4).reshape(B_, S_, H, Dv)

def _dsa_attention(q_abs, ckv, q_idx, k_idx, w_idx, slopes):
    B_, S_ = ckv.shape[:2]
    topk = min(IDX_TOPK_MAX, S_ // 4)
    nb = S_ // QBLOCK
    key_pos = jnp.arange(S_)

    def blocks(t):
        return jnp.moveaxis(t.reshape(B_, nb, QBLOCK, *t.shape[2:]), 1, 0)

    def one_block(args):
        qa, qi, wi, blk = args
        t = blk * QBLOCK + jnp.arange(QBLOCK)
        logits = jnp.einsum('bqjd,bsd->bqjs', qi, k_idx).astype(jnp.float32) * (IDX_DIM ** -0.5)
        score = jnp.einsum('bqjs,bqj->bqs', jax.nn.relu(logits),
                           wi.astype(jnp.float32) * (IDX_HEADS ** -0.5))
        causal = key_pos[None, :] <= t[:, None]
        score = jnp.where(causal[None], score, -jnp.inf)
        _, idx = lax.top_k(score, topk)
        c_sel = jax.vmap(lambda c, i: c[i])(ckv, idx)
        valid = idx <= t[None, :, None]
        dist = (t[None, :, None] - idx).astype(jnp.float32)
        s = jnp.einsum('bqhr,bqkr->bqhk', qa, c_sel).astype(jnp.float32) * (SA_HEAD_DIM ** -0.5)
        s = s - slopes[None, None, :, None] * dist[:, :, None, :]
        s = jnp.where(valid[:, :, None, :], s, -jnp.inf)
        p = jax.nn.softmax(s, axis=-1).astype(ckv.dtype)
        return jnp.einsum('bqhk,bqkr->bqhr', p, c_sel)

    out = lax.map(one_block, (blocks(q_abs), blocks(q_idx), blocks(w_idx), jnp.arange(nb)))
    return jnp.moveaxis(out, 0, 1).reshape(B_, S_, *out.shape[3:])

def setup_inputs(seed: int = 0) -> dict:
    key = jax.random.key(seed)
    ks = jax.random.split(key, 14)
    nrm = jax.random.normal
    x = nrm(ks[0], (BATCH, SEQ, D_MODEL), jnp.float32)
    mem = nrm(ks[1], (BATCH, N_MEM, D_MODEL), jnp.float32)
    w_in = nrm(ks[2], (DEPTH, D_MODEL, IN_WIDTH), jnp.float32) * D_MODEL ** -0.5
    v0 = 2 * DN_WIDTH
    w_in = w_in.at[:, :, v0:v0 + DN_WIDTH].multiply(DEEPNORM_BETA)
    conv_w = nrm(ks[3], (DEPTH, DN_CONV, 3 * DN_WIDTH), jnp.float32) * DN_CONV ** -0.5
    dn_a_log = jnp.log(jax.random.uniform(ks[4], (DEPTH, DN_HEADS), jnp.float32, 1.0, 16.0))
    dt = jnp.exp(jax.random.uniform(ks[5], (DEPTH, DN_HEADS), jnp.float32,
                                    float(np.log(1e-3)), float(np.log(1e-1))))
    dn_dt_bias = dt + jnp.log(-jnp.expm1(-dt))
    dn_norm_w = 1.0 + 0.02 * nrm(ks[6], (DEPTH, DN_HEAD_DIM), jnp.float32)
    kv_norm_w = 1.0 + 0.02 * nrm(ks[7], (DEPTH, SA_KV_RANK), jnp.float32)
    w_uk = nrm(ks[8], (DEPTH, SA_HEADS, SA_KV_RANK, SA_HEAD_DIM), jnp.float32) * SA_KV_RANK ** -0.5
    w_uv = nrm(ks[9], (DEPTH, SA_HEADS, SA_KV_RANK, SA_HEAD_DIM), jnp.float32) * (SA_KV_RANK ** -0.5 * DEEPNORM_BETA)
    w_mem_kv = nrm(ks[10], (DEPTH, D_MODEL, 2 * MEM_WIDTH), jnp.float32) * D_MODEL ** -0.5
    w_mem_kv = w_mem_kv.at[:, :, MEM_WIDTH:].multiply(DEEPNORM_BETA)
    w_out = nrm(ks[11], (DEPTH, MIX_WIDTH, D_MODEL), jnp.float32) * (MIX_WIDTH ** -0.5 * DEEPNORM_BETA)
    ln_g = 1.0 + 0.02 * nrm(ks[12], (DEPTH, D_MODEL), jnp.float32)
    ln_b = 0.02 * nrm(ks[13], (DEPTH, D_MODEL), jnp.float32)
    return {'x': x, 'mem': mem, 'w_in': w_in, 'conv_w': conv_w, 'dn_a_log': dn_a_log,
            'dn_dt_bias': dn_dt_bias, 'dn_norm_w': dn_norm_w, 'kv_norm_w': kv_norm_w,
            'w_uk': w_uk, 'w_uv': w_uv, 'w_mem_kv': w_mem_kv, 'w_out': w_out,
            'ln_g': ln_g, 'ln_b': ln_b}

def reference(x, mem, w_in, conv_w, dn_a_log, dn_dt_bias, dn_norm_w, kv_norm_w,
              w_uk, w_uv, w_mem_kv, w_out, ln_g, ln_b):
    B_, S_, _ = x.shape
    dt = x.dtype
    f32 = jnp.float32
    slopes = jnp.asarray(_alibi_slopes(SA_HEADS))
    pts = _split_points(IN_SPLITS)
    for l in range(DEPTH):
        h = x @ w_in[l]
        (q_a, k_a, v_a, z_a, b_a, a_a,
         q_s, ckv, z_s, q_i, k_i, w_i,
         q_m, z_m) = jnp.split(h, pts, axis=-1)

        qkv = jax.nn.silu(_short_conv(jnp.concatenate([q_a, k_a, v_a], axis=-1), conv_w[l])).astype(f32)
        qa, ka, va = [t.reshape(B_, S_, DN_HEADS, DN_HEAD_DIM) for t in jnp.split(qkv, 3, axis=-1)]
        beta = jax.nn.sigmoid(b_a.astype(f32))
        g = -jnp.exp(dn_a_log[l].astype(f32)) * jax.nn.softplus(a_a.astype(f32) + dn_dt_bias[l].astype(f32))
        o_a = _gated_delta_rule(qa, ka, va, g, beta)
        o_a = _rmsnorm_f32(o_a, dn_norm_w[l]) * jax.nn.silu(z_a.astype(f32).reshape(B_, S_, DN_HEADS, DN_HEAD_DIM))
        o_a = o_a.reshape(B_, S_, DN_WIDTH).astype(dt)

        q_abs = jnp.einsum('bshd,hrd->bshr', q_s.reshape(B_, S_, SA_HEADS, SA_HEAD_DIM), w_uk[l])
        c = _rmsnorm_f32(ckv, kv_norm_w[l]).astype(dt)
        lat = _dsa_attention(q_abs, c, q_i.reshape(B_, S_, IDX_HEADS, IDX_DIM), k_i, w_i, slopes)
        o_s = jnp.einsum('bshr,hrd->bshd', lat, w_uv[l]).reshape(B_, S_, SA_WIDTH)
        o_s = (o_s.astype(f32) * jax.nn.silu(z_s.astype(f32))).astype(dt)

        kv_m = mem @ w_mem_kv[l]
        k_m = kv_m[..., :MEM_WIDTH].reshape(B_, N_MEM, MEM_HEADS, MEM_HEAD_DIM)
        v_m = kv_m[..., MEM_WIDTH:].reshape(B_, N_MEM, MEM_HEADS, MEM_HEAD_DIM)
        s_m = jnp.einsum('bshd,bmhd->bhsm', q_m.reshape(B_, S_, MEM_HEADS, MEM_HEAD_DIM), k_m).astype(f32)
        p_m = jax.nn.softmax(s_m * (MEM_HEAD_DIM ** -0.5), axis=-1).astype(v_m.dtype)
        o_m = jnp.einsum('bhsm,bmhd->bshd', p_m, v_m).reshape(B_, S_, MEM_WIDTH)
        o_m = (o_m.astype(f32) * jax.nn.silu(z_m.astype(f32))).astype(dt)

        y = jnp.concatenate([o_a, o_s, o_m], axis=-1) @ w_out[l]
        x = _layernorm(DEEPNORM_ALPHA * x + y, ln_g[l], ln_b[l])
    return x


_drawn_inputs = setup_inputs


def setup_inputs(seed=0):
    import zlib

    import numpy as np

    out = dict(_drawn_inputs(seed))
    spreads = {}
    factors = {'mem': 6.608,
     'dn_a_log': 2.915,
     'dn_norm_w': 59.472,
     'kv_norm_w': 26.665,
     'w_uk': 2.796,
     'w_mem_kv': 5.886,
     'ln_g': 8.359,
     'ln_b': 7.939}
    for name, (base, spread) in spreads.items():
        noise = np.random.default_rng([zlib.crc32(name.encode()), seed]).standard_normal(out[name].shape)
        drawn = base * np.exp(spread * noise) if base else spread * noise
        out[name] = __import__('jax').numpy.asarray(drawn.astype(out[name].dtype))
    for name, factor in factors.items():
        out[name] = (out[name] * factor).astype(out[name].dtype)
    return out
```

```python
from contextlib import ExitStack

import numpy as np

import concourse.bass as bass
from concourse import mybir

P = 128
SEQ, DM = 1024, 1024
NB = SEQ // P
KT = DM // P
NMEM = 256
DNH, DND = 4, 128
SAH, SAD, RANK = 4, 64, 128
IXH, IXD = 8, 64
TOPK = 256
DNW = DNH * DND
OFF, acc_ = {}, 0
for name_, width_ in (("qa", DNW), ("ka", DNW), ("va", DNW), ("za", DNW), ("ba", DNH), ("aa", DNH), ("qs", 256),
                      ("ckv", RANK), ("zs", 256), ("qi", IXH * IXD), ("ki", IXD), ("wi", IXH), ("qm", 256), ("zm", 256)):
    OFF[name_] = acc_
    acc_ += width_
ALPHA = 2.0 ** 0.25
LN_EPS, RMS_EPS = 1e-5, 1e-6
SLOPES = [2.0 ** (-8.0 * (i + 1) / SAH) for i in range(SAH)]
BIG = 1.0e30
TAKEN = -3.0e38
NLEV = 7
F32 = mybir.dt.float32
ALU = mybir.AluOpType
ACT = mybir.ActivationFunctionType
AX = mybir.AxisListType.X
C_ID, C_TRI, C_NEG, C_CAUS, C_ONE, C_LEV, C_KT = 0, 128, 256, 384, 512, 640, 640 + NLEV * 128
C_ALL = C_KT + SEQ


def shape_constants():
    c = np.zeros((P, C_ALL), np.float32)
    p, f = np.arange(P)[:, None], np.arange(P)[None, :]
    c[:, C_ID:C_ID + P] = p == f
    c[:, C_TRI:C_TRI + P] = p <= f
    c[:, C_NEG:C_NEG + P] = np.where(p <= f, 0.0, -BIG)
    c[:, C_CAUS:C_CAUS + P] = np.where(f <= p, 0.0, -BIG)
    c[:, C_ONE:C_ONE + P] = 1.0
    for i in range(NLEV):
        s = 1 << i
        c[:, C_LEV + i * P:C_LEV + (i + 1) * P] = (p // (2 * s) == f // (2 * s)) & (p % (2 * s) < s) & (f % (2 * s) >= s)
    c[:, C_KT:] = np.arange(SEQ)[None, :] - p - (SEQ - P)
    return c


def idx_chunks(b):
    w = (b + 1) * P
    return [(0, w)] if w <= 512 else [(0, w // 2), (w // 2, w)]


def score_at(b):
    return sum((i + 1) * P for i in range(2, b))


SCORE_W = score_at(NB)


def make_plan():
    plan = []
    add = plan.append
    rounds = [(b, r) for b in range(2, NB) for r in range(TOPK // 8)]

    def topk(n=1):
        for _ in range(n):
            if rounds:
                add(("topk", *rounds.pop(0)))

    for i in range(2 * NB):
        add(("xT", i))
    for t in range(2):
        add(("kiT", t))
    for b in range(NB):
        add(("small", b))
    add(("wis",))
    for m in range(4):
        for t in range(2):
            add(("qiT", m, t))
    for b in range(2, NB):
        for c in range(len(idx_chunks(b))):
            for j in range(IXH):
                add(("idx", b, j, c))
    add(("cwT",))
    add(("wukT",))
    add(("gates",))
    for m in range(2):
        for t in range(2):
            add(("qsT", m, t))
            topk()
    for m in range(2):
        for t in range(2):
            add(("qmT", m, t))
            topk()
    for i in range(4):
        add(("memT", i))
    add(("kmT",))
    add(("vm",))
    topk(2)
    for i in range(2):
        add(("cT", i))

    def slices(h):
        return [("proj", h, part, t, s) for part in (1, 0, 2) for t in range(2) for s in range(4)]

    for i, e in enumerate(slices(0)):
        add(e)
        if i % 2:
            topk()
    zs = [("z", b, half, s) for b in range(NB) for half in range(2) for s in range(4)]
    for h in range(DNH):
        nxt = slices(h + 1) if h + 1 < DNH else list(zs)
        per = len(nxt) // 24

        def fill():
            for _ in range(per if len(nxt) >= per else len(nxt)):
                add(nxt.pop(0))
            topk(2)

        add(("ss", h, 1))
        add(("ss", h, 0))
        for a in range(2):
            add(("tok", h, a, 1))
            add(("tok", h, a, 0))
            add(("tok", h, a, 2))
        add(("GB", h, 0))
        add(("GB", h, 1))
        for a in range(2):
            for w in range(4):
                add(("bT", h, a, w))
            fill()
        for a in range(2):
            add(("U", h, a))
            add(("At", h, a))
        fill()
        for a in range(2):
            add(("lv1", h, a))
        fill()
        for s in range(1, NLEV):
            for a in range(2):
                add(("M", h, a, s))
            fill()
            for a in range(2):
                add(("XY", h, a, s))
            fill()
        for a in range(2):
            add(("nw", h, a))
        for b in range(NB):
            add(("scanV", h, b))
            fill()
            add(("scanS", h, b))
        while nxt:
            fill()
    topk(999)
    add(("finals",))
    for b in range(NB):
        add(("dm", b))
        add(("qabs", b))
        for h in range(SAH):
            for c in range(len(idx_chunks(b))):
                add(("sc", b, h, c))
        for i in range(2):
            add(("msc", b, i))
        if b:
            add(("mixT", b - 1, 0))
            add(("mixT", b - 1, 1))
            add(("y", b - 1, 0))
            add(("y", b - 1, 1))
        for k in range(b + 1):
            add(("pT", b, k))
            if k:
                add(("lat", b, k - 1))
        add(("lat", b, b))
        add(("mpT", b, 0))
        add(("mpT", b, 1))
        add(("o", b))
    for i in range(2):
        add(("mixT", NB - 1, i))
    for i in range(2):
        add(("y", NB - 1, i))
    return plan


POOL_OF = {"xT": "P", "kiT": "P", "small": "P", "qiT": "P", "idx": "L", "cwT": "P", "wukT": "P", "gates": "P",
           "qsT": "P", "qmT": "P", "memT": "P", "kmT": "P", "vm": "P", "cT": "P", "ss": "D", "tok": "D", "GB": "D",
           "bT": "D", "U": "D", "At": "D", "lv1": "D", "M": "D", "XY": "D", "nw": "D", "sc": "L",
           "msc": "D", "mixT": "P", "y": "P", "pT": "D", "lat": "P", "mpT": "D", "o": "P"}


def tiles_of(e):
    k = e[0]
    if k == "proj":
        return [("P", ("proj", *e[1:4]))] if e[4] == 0 else []
    if k == "z":
        return [("PL"[e[2]], ("z", e[1], e[2]))] if e[3] == 0 else []
    if k == "lat":
        return [("P", ("lat", e[1]))] if e[2] == 0 else []
    if k == "qabs":
        return [("P", (*e, 0)), ("P", (*e, 1))]
    if k == "scanV":
        return [("D", ("V", e[1], e[2]))]
    if k == "scanS":
        return [("D", ("S", e[1], e[2]))] * (e[2] < NB - 1) + [("D", ("O", e[1], e[2]))]
    return [(POOL_OF[k], e)] if k in POOL_OF else []


def weight_loads():
    loads = [("ki", [("w_in", OFF["ki"], 64, 0), ("w_in", OFF["ki"], 64, 64), ("w_in", OFF["ckv"], 128, 128)]),
             ("small", [("w_in", OFF["ba"], 8, 0), ("w_in", OFF["wi"], 8, 8)]),
             ("qi0", [("w_in", OFF["qi"], 256, 0)]), ("qi1", [("w_in", OFF["qi"] + 256, 256, 0)]),
             ("qs", [("w_in", OFF["qs"], 256, 0)]), ("qm", [("w_in", OFF["qm"], 256, 0)]),
             ("mk", [("w_mem_kv", 0, 256, 0)]), ("mv", [("w_mem_kv", 256, 256, 0)])]
    for h in range(DNH):
        loads.append((f"kq{h}", [("w_in", OFF["ka"] + h * P, P, 0), ("w_in", OFF["qa"] + h * P, P, P)]))
        loads.append((f"v{h}", [("w_in", OFF["va"] + h * P, P, 0)]))
    loads += [("z0", [("w_in", OFF["za"], 256, 0)]), ("z1", [("w_in", OFF["za"] + 256, 256, 0)]),
              ("z2", [("w_in", OFF["zs"], 256, 0)]), ("z3", [("w_in", OFF["zm"], 256, 0)])]
    return loads


def build(nc, x, mem, w_in, conv_w, dn_a_log, dn_dt_bias, dn_norm_w, kv_norm_w, w_uk, w_uv, w_mem_kv, w_out,
          ln_g, ln_b, consts, out, plan=None):
    plan = plan or make_plan()
    ctx = ExitStack()
    with ctx:
        def sb(name, cols):
            return ctx.enter_context(nc.sbuf_tensor(name, [P, cols], F32))

        def sem(name):
            return ctx.enter_context(nc.semaphore(name))

        cst = sb("cst", C_ALL)
        xT_ = sb("xT", NB * KT * P)
        ring = sb("ring", 4 * 2048)
        idx_ = sb("idxq", 4 * SEQ)
        score = sb("score", SCORE_W)
        small = sb("small", NB * 144)
        cT = sb("cT", SEQ)
        qmT = sb("qmT", 2 * SEQ)
        qsT = sb("qsT", 2 * SEQ)
        hbuf = sb("hbuf", 3 + SEQ)
        qkvT = sb("qkvT", 3 * SEQ)
        kmT = sb("kmT", 2 * NMEM)
        vm = sb("vm", 2 * NMEM)
        wukT = sb("wukT", 2 * RANK)
        wuv = sb("wuv", SAH * SAD)
        arena = sb("arena", 24 * 512)
        cw = sb("cw", 48)
        rows = sb("rows", 128 + 128 + 8)
        sc32 = sb("sc32", 14 * 32)
        hsc = sb("hsc", 16 + 16 + 6 * 8)
        dn_s = sb("dn_s", 2 * 128)
        vnew = sb("vnew", 2 * 128)
        wis_ = sb("wis", 64)
        misc = sb("misc", 64)
        mx8 = sb("mx8", 8)
        junk = sb("junk", 128)

        ident = cst[:, C_ID:C_ID + P]
        tri = cst[:, C_TRI:C_TRI + P]
        ones = cst[:, C_ONE:C_ONE + P]
        xT = xT_[:, :].rearrange("p (b k t) -> p b k t", b=NB, k=KT)
        zg = xT_[:, :].rearrange("p (b c) -> p b c", b=NB)
        slots = ring[:, :].rearrange("p (s k n) -> p s k n", s=4, k=KT)
        wout = ring[:, :].rearrange("p (k n) -> p k n", k=KT)
        qiT = idx_[:, :].rearrange("p (m t) -> p m t", m=4)
        oall = idx_[:, :].rearrange("p (b h d) -> p b h d", b=NB, h=DNH)
        sm = small[:, :].rearrange("p (b c) -> p b c", b=NB)
        qmTv = qmT[:, :].rearrange("p (m t) -> p m t", m=2)
        qsTv = qsT[:, :].rearrange("p (m t) -> p m t", m=2)
        qkv = qkvT[:, :].rearrange("p (a t) -> p a t", a=3)
        wis = wis_[:, :].rearrange("p (b j) -> p b j", b=NB)
        kvw, nrmw = rows[:, 0:128], rows[:, 128:256]
        alog, dtb = rows[:, 256:260], rows[:, 260:264]
        kiT = arena[:, 0:1024]
        rbuf = [arena[:, 1024 + i * 512:1536 + i * 512] for i in range(3)]
        memnat = arena[:, 3072:5120].rearrange("p (m c) -> p m c", m=2)
        memT = arena[:, 5120:7168].rearrange("p (k t) -> p k t", k=KT)
        wuknat = arena[:, 7168:7424]
        cwnat = arena[:, 7424:7552]
        xnat = [score[:, i * 1024:(i + 1) * 1024] for i in range(4)]

        def row(a, i):
            return arena[:, (12 * a + i) * 512:(12 * a + i + 1) * 512]

        def blk(ap, i):
            return ap[:, i * P:(i + 1) * P]

        R_KHAT, R_KB, R_QHAT, R_QDEC, R_KBG, R_KD, R_VB, R_KHATT, R_KBT, R_QHATT, R_QDECT, R_DEC = range(12)
        R_UO, R_M1, R_NW, R_X, R_U, R_ATT, R_Y, R_DARG = (0, 1), 2, 0, 7, 8, 9, 11, 11

        def av(at, n):
            return arena[:, at:at + n]

        xs = av(0, 4096).rearrange("p (h n) -> p h n", h=SAH)
        pTb = [av(4096 + i * 512, 512) for i in range(3)]
        latT = av(5632, 512)
        qab = av(6144, 512)
        mp = av(6656, 1024)
        mpT = [av(7680 + i * 512, 512) for i in range(2)]
        mix = av(8704, 1024)
        mixT = [av(9728 + i * 512, 512) for i in range(2)]
        yres = av(10752, 1024)
        otmp = av(11776, 512)
        lng, lnb = qkvT[:, 0:1024], qkvT[:, 1024:2048]
        xres = qkvT[:, 2048:3072]
        dm01 = hbuf[:, 0:384]
        dmx = hbuf[:, 384:896]
        (s_beta, s_y, s_neg, s_g, s_G, s_Gt, s_nG, s_dG, s_eG, s_eD, s_gl, s_oss, s_orn, s_tmp) = (
            sc32[:, i * 32:(i + 1) * 32] for i in range(14))
        css, crs = misc[:, 0:8], misc[:, 8:16]
        eps_rms, eps_ln, one1 = misc[:, 16:17], misc[:, 17:18], misc[:, 18:19]
        mxp, nmx = misc[:, 20:28], misc[:, 28:32]
        sums, rinv = misc[:, 32:40], misc[:, 40:48]
        mmx = misc[:, 48:52]
        bst, mv, rstd, ealog = hsc[:, 0:12], hsc[:, 12:14], hsc[:, 14:15], misc[:, 52:56]
        rs_k, rs_q = hsc[:, 16:24], hsc[:, 24:32]
        sc_of = {n: hsc[:, 32 + 8 * i:40 + 8 * i] for i, n in enumerate(("kb", "kbg", "kd", "q", "qd"))}

        pools = {"P": (0, 1), "L": (2, 3), "D": (4, 5, 6, 7)}
        banks = [ctx.enter_context(nc.psum_tensor(f"bank{i}", [P, 512], F32)) for i in range(8)]
        filled_sem = [sem(f"filled{i}") for i in range(8)]
        released_sem = [sem(f"released{i}") for i in range(8)]
        bank_of, use_of, count = {}, {}, {k: 0 for k in pools}
        for e in plan:
            for pool, key in tiles_of(e):
                n = count[pool]
                bank_of[key] = pools[pool][n % len(pools[pool])]
                use_of[key] = n // len(pools[pool]) + 1
                count[pool] += 1

        def ps(key):
            return banks[bank_of[key]]

        def vacated(key):
            return released_sem[bank_of[key]], use_of[key] - 1

        def first(key):
            return use_of[key] == 1

        def filled(key):
            return filled_sem[bank_of[key]], use_of[key]

        def released(key):
            return released_sem[bank_of[key]], use_of[key]

        def fill_of(key):
            return filled_sem[bank_of[key]]

        def release_of(key):
            return released_sem[bank_of[key]]

        small_constants_set = sem("small_constants_set")
        gate_steps_by_dve = sem("gate_steps_by_dve")
        scores_summed = sem("scores_summed")
        conv_done = sem("conv_done")
        head_max_ready = sem("head_max_ready")
        mem_max_ready = sem("mem_max_ready")
        attention_gated = sem("attention_gated")
        ln_stats_ready = sem("ln_stats_ready")
        ln_scaled = sem("ln_scaled")
        silu_done = sem("silu_done")
        squares_ready = sem("squares_ready")
        inverse_norms_ready = sem("inverse_norms_ready")
        decays_ready = sem("decays_ready")
        exps_ready = sem("exps_ready")
        gate_steps_by_act = sem("gate_steps_by_act")
        output_norms_ready = sem("output_norms_ready")
        ln_rstd_ready = sem("ln_rstd_ready")
        level_masked = sem("level_masked")
        y_started = sem("y_started")
        deltanet_gated = sem("deltanet_gated")
        row_finished = sem("row_finished")
        order = {}
        seen = {}
        for e in plan:
            seen[e[0]] = seen.get(e[0], 0) + 1
            order[e] = seen[e[0]]

        loads = weight_loads()
        load_at = {n: i for i, (n, _) in enumerate(loads)}
        loaded_sem = [sem(f"loaded{i}") for i in range(4)]
        last_use = {"ki": ("small", NB - 1), "small": ("small", NB - 1), "qi0": ("qiT", 1, 1), "qi1": ("qiT", 3, 1),
                    "qs": ("qsT", 1, 1), "qm": ("qmT", 1, 1), "mk": ("kmT",), "mv": ("vm",)}
        for h in range(DNH):
            last_use[f"kq{h}"] = ("proj", h, 0, 1)
            last_use[f"v{h}"] = ("proj", h, 2, 1)
        load_need = {}
        total = [0] * 4
        for i, (n, pieces) in enumerate(loads):
            total[i % 4] += 16 * len(pieces)
            load_need[n] = total[i % 4]
        x_sem = [sem(f"x_loaded{i}") for i in range(4)]
        c_sem = sem("consts_loaded")
        m_sem = sem("mem_loaded")
        r_sem = sem("rows_loaded")
        w_sem = sem("wout_loaded")
        xr_sem = sem("xres_loaded")
        ln_sem = sem("lnrows_loaded")
        st_sem = sem("stored")

        def slot(name):
            return slots[:, load_at[name] % 4]

        def weights(pe, name):
            pe.wait_ge(loaded_sem[load_at[name] % 4], load_need[name])

        block = ctx.enter_context(nc.Block())

        @block.sync
        def _(sp):
            xv = x.rearrange("a (b p) c -> (a b) p c", p=P)
            ov = out.rearrange("a (b p) c -> (a b) p c", p=P)
            src = {"w_in": w_in.rearrange("a (k p) n -> p (a k) n", p=P),
                   "w_mem_kv": w_mem_kv.rearrange("a (k p) n -> p (a k) n", p=P)}
            sp.dma_start(cst[:, :], consts).then_inc(c_sem, 16)
            for b in range(4):
                sp.dma_start(xnat[b], xv[b]).then_inc(x_sem[b], 16)

            def load(i):
                if i >= 4:
                    sp.wait_ge(*filled(last_use[loads[i - 4][0]]))
                for t, col, w, at in loads[i][1]:
                    sp.dma_start(slots[:, i % 4, :, at:at + w], src[t][:, :, col:col + w]).then_inc(loaded_sem[i % 4], 16)

            load(0)
            load(1)
            for b in range(4, NB):
                sp.wait_ge(*filled(("xT", 2 * (b - 4) + 1)))
                sp.dma_start(xnat[b - 4], xv[b]).then_inc(x_sem[b - 4], 16)
            load(2)
            load(3)
            sp.dma_start(wuknat.rearrange("p (h d) -> p h d", h=SAH), w_uk.rearrange("a h r d -> r (a h) d")).then_inc(m_sem, 16)
            sp.dma_start(cwnat[0:48, :], conv_w.rearrange("a j (c p) -> (a j c) p", p=P)).then_inc(m_sem, 16)
            sp.dma_start(memnat, mem.rearrange("a (m p) c -> p (a m) c", p=P)).then_inc(m_sem, 16)
            sp.dma_start(wuv[:, :].rearrange("p (h d) -> p h d", h=SAH), w_uv.rearrange("a h r d -> r (a h) d")).then_inc(m_sem, 16)
            for dst, s in ((kvw, kv_norm_w), (nrmw, dn_norm_w), (alog, dn_a_log), (dtb, dn_dt_bias)):
                sp.dma_start(dst, s.broadcast_to([P, dst.shape[1]])).then_inc(r_sem, 16)
            for i in range(4, len(loads)):
                load(i)
            if ("finals",) not in order:
                return
            sp.wait_ge(*filled(("z", NB - 1, 0)))
            sp.wait_ge(*filled(("z", NB - 1, 1)))
            sp.dma_start(wout, w_out.rearrange("a (k p) n -> p (a k) n", p=P)).then_inc(w_sem, 16)
            for part in range(3):
                sp.wait_ge(*filled(("tok", DNH - 1, 1, part)))
            sp.dma_start(lng, ln_g.broadcast_to([P, DM])).then_inc(ln_sem, 16)
            sp.dma_start(lnb, ln_b.broadcast_to([P, DM])).then_inc(ln_sem, 16)
            for b in range(NB):
                if b:
                    sp.wait_ge(*released(("y", b - 1, 0)))
                    sp.wait_ge(*released(("y", b - 1, 1)))
                sp.dma_start(xres, xv[b]).then_inc(xr_sem, 16)
                if b:
                    sp.wait_ge(row_finished, b)
                    sp.dma_start(ov[b - 1], yres).then_inc(st_sem, 16)
            sp.wait_ge(row_finished, NB)
            sp.dma_start(ov[NB - 1], yres).then_inc(st_sem, 16)
            sp.wait_ge(st_sem, 16 * NB)

        @block.tensor
        def _(pe):
            def group(dst, pairs):
                for i, (w, r) in enumerate(pairs):
                    last = nc.tensor.matmul(dst, w, r, start=(i == 0), stop=(i == len(pairs) - 1))
                return last

            def tp(dst, src, n=P):
                return nc.tensor.transpose(dst, src, ident[0:n, 0:n])

            pe.wait_ge(c_sem, 16)
            for e in plan:
                k = e[0]
                if k == "xT":
                    b, half = e[1] // 2, e[1] % 2
                    if half == 0:
                        pe.wait_ge(x_sem[b % 4], 16 * (b // 4 + 1))
                    if not first(e):
                        pe.wait_ge(*vacated(e))
                    for i in range(4):
                        c = 4 * half + i
                        last = tp(ps(e)[:, i * P:(i + 1) * P], xnat[b % 4][:, c * P:(c + 1) * P])
                    last.then_inc(fill_of(e), 1)
                elif k == "kiT":
                    t = e[1]
                    if t == 0:
                        weights(pe, "ki")
                        pe.wait_ge(*released(("xT", 2 * NB - 2)))
                        pe.wait_ge(*released(("xT", 2 * NB - 1)))
                    if not first(e):
                        pe.wait_ge(*vacated(e))
                    group(ps(e)[:, :], [(slot("ki")[:, c, 0:P], xT[:, 4 * t:4 * t + 4, c, :]) for c in range(KT)]).then_inc(fill_of(e), 1)
                elif k == "small":
                    b = e[1]
                    if b == 0:
                        weights(pe, "small")
                    if not first(e):
                        pe.wait_ge(*vacated(e))
                    group(ps(e)[:, 0:P], [(xT[:, b, c, :], slot("ki")[:, c, P:2 * P]) for c in range(KT)])
                    group(ps(e)[:, P:144], [(xT[:, b, c, :], slot("small")[:, c, 0:16]) for c in range(KT)]).then_inc(fill_of(e), 1)
                elif k in ("qiT", "qsT", "qmT"):
                    m, t = e[1], e[2]
                    name = f"qi{m // 2}" if k == "qiT" else k[:2]
                    if t == 0:
                        weights(pe, name)
                    if not first(e):
                        pe.wait_ge(*vacated(e))
                    mc = (m % 2) * P
                    group(ps(e)[:, :], [(slot(name)[:, c, mc:mc + P], xT[:, 4 * t:4 * t + 4, c, :]) for c in range(KT)]).then_inc(fill_of(e), 1)
                elif k == "idx":
                    b, j, c = e[1:]
                    if (j, c) == (0, 0):
                        if b == 2:
                            pe.wait_ge(*released(("kiT", 0)))
                            pe.wait_ge(*released(("kiT", 1)))
                            for m in range(4):
                                for t in range(2):
                                    pe.wait_ge(*released(("qiT", m, t)))
                    lo, hi = idx_chunks(b)[c]
                    p0 = 64 * (j % 2)
                    if not first(e):
                        pe.wait_ge(*vacated(e))
                    group(ps(e)[:, 0:hi - lo], [(qiT[p0:p0 + 64, j // 2, b * P:(b + 1) * P], kiT[p0:p0 + 64, lo:hi])]).then_inc(fill_of(e), 1)
                elif k == "cwT":
                    pe.wait_ge(m_sem, 64)
                    if not first(e):
                        pe.wait_ge(*vacated(e))
                    tp(ps(e)[:, 0:48], cwnat[0:48, :], 48).then_inc(fill_of(e), 1)
                elif k == "wukT":
                    if not first(e):
                        pe.wait_ge(*vacated(e))
                    tp(ps(e)[:, 0:P], wuknat[:, 0:P])
                    tp(ps(e)[:, P:2 * P], wuknat[:, P:2 * P]).then_inc(fill_of(e), 1)
                elif k == "gates":
                    if not first(e):
                        pe.wait_ge(*vacated(e))
                    pe.wait_ge(gate_steps_by_dve, 2)
                    nc.tensor.matmul(ps(e)[:, 0:32], tri, s_g, start=True, stop=True)
                    nc.tensor.matmul(ps(e)[:, 32:64], ones, s_g, start=True, stop=True).then_inc(fill_of(e), 1)
                elif k == "memT":
                    m, half = e[1] // 2, e[1] % 2
                    if not first(e):
                        pe.wait_ge(*vacated(e))
                    for i in range(4):
                        c = 4 * half + i
                        last = tp(ps(e)[:, i * P:(i + 1) * P], memnat[:, m, c * P:(c + 1) * P])
                    last.then_inc(fill_of(e), 1)
                elif k == "kmT":
                    weights(pe, "mk")
                    for i in range(4):
                        pe.wait_ge(*released(("memT", i)))
                    if not first(e):
                        pe.wait_ge(*vacated(e))
                    for m in range(2):
                        last = group(ps(e)[:, m * 256:(m + 1) * 256],
                                     [(slot("mk")[:, c, m * P:(m + 1) * P], memT[:, c, :]) for c in range(KT)])
                    last.then_inc(fill_of(e), 1)
                elif k == "vm":
                    weights(pe, "mv")
                    if not first(e):
                        pe.wait_ge(*vacated(e))
                    for m in range(2):
                        last = group(ps(e)[:, m * 256:(m + 1) * 256],
                                     [(memT[:, c, m * P:(m + 1) * P], slot("mv")[:, c, :]) for c in range(KT)])
                    last.then_inc(fill_of(e), 1)
                elif k == "cT":
                    pe.wait_ge(gate_steps_by_dve, 3)
                    if not first(e):
                        pe.wait_ge(*vacated(e))
                    for i in range(4):
                        last = tp(ps(e)[:, i * P:(i + 1) * P], sm[:, 4 * e[1] + i, 0:P])
                    last.then_inc(fill_of(e), 1)
                elif k == "proj":
                    h, part, t, s = e[1:]
                    key = ("proj", h, part, t)
                    name = f"v{h}" if part == 2 else f"kq{h}"
                    at = P if part == 0 else 0
                    if s == 0:
                        if t == 0:
                            weights(pe, name)
                        if not first(key):
                            pe.wait_ge(*vacated(key))
                    for c in (2 * s, 2 * s + 1):
                        last = nc.tensor.matmul(ps(key)[:, :], slot(name)[:, c, at:at + P], xT[:, 4 * t:4 * t + 4, c, :],
                                                start=(c == 0), stop=(c == KT - 1))
                    if s == 3:
                        last.then_inc(fill_of(key), 1)
                elif k == "z":
                    b, half, s = e[1:]
                    key = ("z", b, half)
                    if s == 0:
                        if b == 0:
                            weights(pe, f"z{2 * half}")
                            weights(pe, f"z{2 * half + 1}")
                        if not first(key):
                            pe.wait_ge(*vacated(key))
                    q = s // 2
                    for c in range(4 * (s % 2), 4 * (s % 2) + 4):
                        last = nc.tensor.matmul(ps(key)[:, q * 256:(q + 1) * 256], xT[:, b, c, :], slot(f"z{2 * half + q}")[:, c, :],
                                                start=(c == 0), stop=(c == KT - 1))
                    if s == 3:
                        last.then_inc(fill_of(key), 1)
                elif k == "ss":
                    h, part = e[1:]
                    pe.wait_ge(squares_ready, order[e])
                    if not first(e):
                        pe.wait_ge(*vacated(e))
                    sq = arena[:, (0 if part else 1024):(1024 if part else 2048)]
                    for b in range(NB):
                        last = nc.tensor.matmul(ps(e)[:, b:b + 1], sq[:, b * P:(b + 1) * P], ones[:, 0:1], start=True, stop=True)
                    last.then_inc(fill_of(e), 1)
                elif k == "tok":
                    h, a, part = e[1:]
                    if part == 2:
                        pe.wait_ge(silu_done, 3 * h + 3)
                    if not first(e):
                        pe.wait_ge(*vacated(e))
                    for i in range(4):
                        last = tp(ps(e)[:, i * P:(i + 1) * P], qkv[:, part, (4 * a + i) * P:(4 * a + i + 1) * P])
                    last.then_inc(fill_of(e), 1)
                elif k == "bT":
                    h, a, w = e[1:]
                    pe.wait_ge(*released(("tok", h, a, 1 if w < 2 else 0)))
                    if not first(e):
                        pe.wait_ge(*vacated(e))
                    src = row(a, (R_KHAT, R_KB, R_QHAT, R_QDEC)[w])
                    for i in range(4):
                        last = tp(ps(e)[:, i * P:(i + 1) * P], blk(src, i))
                    last.then_inc(fill_of(e), 1)
                elif k == "GB":
                    h, a = e[1:]
                    if not first(e):
                        pe.wait_ge(*vacated(e))
                    for i in range(4):
                        col = h * NB + 4 * a + i
                        last = nc.tensor.matmul(ps(e)[:, i * P:(i + 1) * P], s_g[:, col:col + 1].broadcast_to([P, P]), tri, start=True, stop=True)
                    last.then_inc(fill_of(e), 1)
                elif k in ("U", "At"):
                    h, a = e[1:]
                    pe.wait_ge(*released(("bT", h, a, 0)))
                    pe.wait_ge(*released(("bT", h, a, 1 if k == "U" else 2)))
                    if not first(e):
                        pe.wait_ge(*vacated(e))
                    other = row(a, R_KBT if k == "U" else R_QHATT)
                    for i in range(4):
                        last = nc.tensor.matmul(ps(e)[:, i * P:(i + 1) * P], blk(row(a, R_KHATT), i), blk(other, i), start=True, stop=True)
                    last.then_inc(fill_of(e), 1)
                elif k == "lv1":
                    h, a = e[1:]
                    pe.wait_ge(level_masked, ((h * NLEV) + 0) * 2 + a + 1)
                    if not first(e):
                        pe.wait_ge(*vacated(e))
                    for i in range(4):
                        last = tp(ps(e)[:, i * P:(i + 1) * P], blk(row(a, R_UO[0]), i))
                    last.then_inc(fill_of(e), 1)
                elif k == "M":
                    h, a, s = e[1:]
                    pe.wait_ge(level_masked, (h * NLEV + s) * 2 + a + 1)
                    if s == 1:
                        pe.wait_ge(*released(("lv1", h, a)))
                    else:
                        pe.wait_ge(*released(("XY", h, a, s - 1)))
                    if not first(e):
                        pe.wait_ge(*vacated(e))
                    for i in range(4):
                        last = nc.tensor.matmul(ps(e)[:, i * P:(i + 1) * P], blk(row(a, R_UO[s % 2]), i), blk(row(a, R_X), i), start=True, stop=True)
                    last.then_inc(fill_of(e), 1)
                elif k == "XY":
                    h, a, s = e[1:]
                    pe.wait_ge(*released(("M", h, a, s)))
                    pe.wait_ge(y_started, 2 * h + a + 1)
                    if not first(e):
                        pe.wait_ge(*vacated(e))
                    w = 1 << s
                    for i in range(4):
                        m1 = blk(row(a, R_M1), i)
                        if s < NLEV - 1:
                            last = nc.tensor.matmul(ps(e)[:, i * 64:(i + 1) * 64], blk(row(a, R_Y), i),
                                                    m1.rearrange("p (n t) -> p n t", t=2 * w)[:, :, 0:w], start=True, stop=True)
                        last = nc.tensor.matmul(ps(e)[:, 256 + i * 64:256 + (i + 1) * 64], m1,
                                                blk(row(a, R_Y), i).rearrange("p (n t) -> p n t", t=2 * w)[:, :, w:2 * w], start=True, stop=True)
                    last.then_inc(fill_of(e), 1)
                elif k == "nw":
                    h, a = e[1:]
                    pe.wait_ge(*released(("XY", h, a, NLEV - 1)))
                    if not first(e):
                        pe.wait_ge(*vacated(e))
                    for i in range(4):
                        last = nc.tensor.matmul(ps(e)[:, i * P:(i + 1) * P], blk(row(a, R_KBG), i), blk(row(a, R_Y), i), start=True, stop=True)
                    last.then_inc(fill_of(e), 1)
                elif k == "scanV":
                    h, b = e[1:]
                    a, i = b // 4, b % 4
                    key = ("V", h, b)
                    if i == 0:
                        pe.wait_ge(*released(("nw", h, a)))
                    if not first(key):
                        pe.wait_ge(*vacated(key))
                    last = nc.tensor.matmul(ps(key)[:, 0:P], blk(row(a, R_Y), i), blk(row(a, R_VB), i), start=True, stop=(b == 0))
                    if b:
                        pe.wait_ge(*released(("S", h, b - 1)))
                        last = nc.tensor.matmul(ps(key)[:, 0:P], blk(row(a, R_NW), i), dn_s[:, (b % 2) * P:(b % 2 + 1) * P], start=False, stop=True)
                    last.then_inc(fill_of(key), 1)
                elif k == "scanS":
                    h, b = e[1:]
                    a, i = b // 4, b % 4
                    vn = vnew[:, (b % 2) * P:(b % 2 + 1) * P]
                    pe.wait_ge(*released(("V", h, b)))
                    ko, ks = ("O", h, b), ("S", h, b)
                    if b < NB - 1:
                        if not first(ks):
                            pe.wait_ge(*vacated(ks))
                        nc.tensor.matmul(ps(ks)[:, 0:P], blk(row(a, R_KD), i), vn, start=True, stop=True).then_inc(fill_of(ks), 1)
                    if not first(ko):
                        pe.wait_ge(*vacated(ko))
                    if b:
                        nc.tensor.matmul(ps(ko)[:, 0:P], blk(row(a, R_QDECT), i), dn_s[:, (b % 2) * P:(b % 2 + 1) * P], start=True, stop=False)
                    nc.tensor.matmul(ps(ko)[:, 0:P], blk(row(a, R_ATT), i), vn, start=(b == 0), stop=True).then_inc(fill_of(ko), 1)
                elif k == "qabs":
                    b = e[1]
                    if b == 0:
                        for m in range(2):
                            for t in range(2):
                                pe.wait_ge(*released(("qsT", m, t)))
                    for odd in range(2):
                        key = ("qabs", b, odd)
                        p0 = 64 * odd
                        if not first(key):
                            pe.wait_ge(*vacated(key))
                        for m in range(2):
                            last = nc.tensor.matmul(ps(key)[:, m * P:(m + 1) * P], wukT[p0:p0 + 64, m * P:(m + 1) * P],
                                                    qsTv[p0:p0 + 64, m, b * P:(b + 1) * P], start=True, stop=True)
                        last.then_inc(fill_of(key), 1)
                elif k == "sc":
                    b, h, c = e[1:]
                    if (h, c) == (0, 0):
                        pe.wait_ge(*released(("qabs", b, 0)))
                        pe.wait_ge(*released(("qabs", b, 1)))
                    lo, hi = idx_chunks(b)[c]
                    if not first(e):
                        pe.wait_ge(*vacated(e))
                    nc.tensor.matmul(ps(e)[:, 0:hi - lo], qab[:, h * P:(h + 1) * P], cT[:, lo:hi], start=True, stop=True).then_inc(fill_of(e), 1)
                elif k == "msc":
                    b, i = e[1:]
                    if not first(e):
                        pe.wait_ge(*vacated(e))
                    p0 = 64 * i
                    for m in range(2):
                        last = nc.tensor.matmul(ps(e)[:, m * 256:(m + 1) * 256], qmTv[p0:p0 + 64, m, b * P:(b + 1) * P],
                                                kmT[p0:p0 + 64, m * 256:(m + 1) * 256], start=True, stop=True)
                    last.then_inc(fill_of(e), 1)
                elif k == "pT":
                    b, kt = e[1:]
                    if kt == 0:
                        pe.wait_ge(exps_ready, SAH * (b + 1))
                    if not first(e):
                        pe.wait_ge(*vacated(e))
                    for h in range(SAH):
                        last = tp(ps(e)[:, h * P:(h + 1) * P], xs[:, h, kt * P:(kt + 1) * P])
                    last.then_inc(fill_of(e), 1)
                elif k == "lat":
                    b, kt = e[1:]
                    key = ("lat", b)
                    if kt == 0:
                        if not first(key):
                            pe.wait_ge(*vacated(key))
                    pe.wait_ge(*released(("pT", b, kt)))
                    last = nc.tensor.matmul(ps(key)[:, :], sm[:, kt, 0:P], pTb[(order[e] - 1) % 3], start=(kt == 0), stop=(kt == b))
                    if kt == b:
                        last.then_inc(fill_of(key), 1)
                elif k == "mpT":
                    b, i = e[1:]
                    pe.wait_ge(*released(("msc", b, 0)))
                    pe.wait_ge(*released(("msc", b, 1)))
                    if not first(e):
                        pe.wait_ge(*vacated(e))
                    for h in range(4):
                        last = tp(ps(e)[:, h * P:(h + 1) * P], mp[:, h * 256 + i * P:h * 256 + (i + 1) * P])
                    last.then_inc(fill_of(e), 1)
                elif k == "o":
                    b = e[1]
                    pe.wait_ge(*released(("lat", b)))
                    if not first(e):
                        pe.wait_ge(*vacated(e))
                    for h in range(SAH):
                        nc.tensor.matmul(ps(e)[:, h * 64:(h + 1) * 64], latT[:, h * P:(h + 1) * P], wuv[:, h * 64:(h + 1) * 64], start=True, stop=True)
                    pe.wait_ge(*released(("mpT", b, 0)))
                    pe.wait_ge(*released(("mpT", b, 1)))
                    for h in range(4):
                        last = group(ps(e)[:, 256 + h * 64:256 + (h + 1) * 64],
                                     [(mpT[i][:, h * P:(h + 1) * P], vm[:, i * 256 + h * 64:i * 256 + (h + 1) * 64]) for i in range(2)])
                    last.then_inc(fill_of(e), 1)
                elif k == "mixT":
                    b, i = e[1:]
                    if i == 0:
                        pe.wait_ge(deltanet_gated, b + 1)
                    else:
                        pe.wait_ge(attention_gated, b + 1)
                    if not first(e):
                        pe.wait_ge(*vacated(e))
                    for c in range(4):
                        last = tp(ps(e)[:, c * P:(c + 1) * P], mix[:, (4 * i + c) * P:(4 * i + c + 1) * P])
                    last.then_inc(fill_of(e), 1)
                elif k == "y":
                    b, i = e[1:]
                    if (b, i) == (0, 0):
                        pe.wait_ge(w_sem, 16)
                    if i == 0:
                        pe.wait_ge(*released(("mixT", b, 0)))
                        pe.wait_ge(*released(("mixT", b, 1)))
                    if not first(e):
                        pe.wait_ge(*vacated(e))
                    group(ps(e)[:, :], [(mixT[c // 4][:, (c % 4) * P:(c % 4 + 1) * P], wout[:, c, i * 512:(i + 1) * 512]) for c in range(KT)]).then_inc(fill_of(e), 1)

        @block.vector
        def _(dve):
            v = nc.vector
            dve_chain = ctx.enter_context(nc.semaphore("dve_chain"))
            steps = [0]

            def link(ins):
                steps[0] += 1
                ins.then_inc(dve_chain, 1)
                dve.wait_ge(dve_chain, steps[0])

            def bc(ap, n):
                return ap.unsqueeze(2).broadcast_to([P, ap.shape[1], n])

            def rep(ap, n):
                return ap.unsqueeze(1).broadcast_to([P, n, ap.shape[1]])

            def quad(ap):
                return ap.rearrange("p (b t) -> p b t", b=4)

            v.memset(hbuf[:, 0:3], 0.0)
            v.memset(eps_rms, RMS_EPS)
            v.memset(one1, 1.0)
            v.memset(eps_ln, LN_EPS).then_inc(small_constants_set, 1)
            for e in plan:
                k = e[0]
                if k == "xT" and e[1] % 2:
                    dve.wait_ge(*filled(e))
                    v.tensor_copy(xT[:, e[1] // 2, 4:8, :], quad(ps(e)[:, :])).then_inc(release_of(e), 1)
                elif k == "small":
                    dve.wait_ge(*filled(e))
                    v.tensor_copy(sm[:, e[1], :], ps(e)[:, 0:144]).then_inc(release_of(e), 1)
                elif k == "wis":
                    dve.wait_ge(*released(("small", NB - 1)))
                    dve.wait_ge(*released(("small", NB - 2)))
                    link(v.tensor_scalar(wis, sm[:, :, 136:144], IXH ** -0.5, None, ALU.mult))
                elif k in ("qiT", "qsT", "qmT") and e[2] == 1:
                    dve.wait_ge(*filled(e))
                    dst = {"qiT": qiT, "qsT": qsTv, "qmT": qmTv}[k]
                    v.tensor_copy(dst[:, e[1], 512:1024], ps(e)[:, :]).then_inc(release_of(e), 1)
                elif k == "idx":
                    b, j, c = e[1:]
                    lo, hi = idx_chunks(b)[c]
                    r = rbuf[(order[e] - 1) % 3]
                    at = score_at(b)
                    w = wis[:, b, j:j + 1]
                    dve.wait_ge(*released(e))
                    if j == 0:
                        plain = hi - lo - (P if hi == (b + 1) * P else 0)
                        last = v.tensor_scalar(score[:, at + lo:at + lo + plain], r[:, 0:plain], w, None, ALU.mult)
                        if plain < hi - lo:
                            last = v.scalar_tensor_tensor(score[:, at + lo + plain:at + hi], r[:, plain:hi - lo], w,
                                                          cst[:, C_CAUS:C_CAUS + P], ALU.mult, ALU.add)
                    else:
                        dve.wait_ge(scores_summed, order[e] - 1)
                        last = v.scalar_tensor_tensor(score[:, at + lo:at + hi], r[:, 0:hi - lo], w,
                                                      score[:, at + lo:at + hi], ALU.mult, ALU.add)
                    last.then_inc(scores_summed, 1)
                elif k == "topk":
                    b, r = e[1:]
                    row_ = score[:, score_at(b):score_at(b + 1)]
                    if r == 0:
                        dve.wait_ge(scores_summed, order["idx", b, IXH - 1, len(idx_chunks(b)) - 1])
                    link(v.max(mx8[:, :], row_))
                    link(v.match_replace(row_, mx8[:, :], row_, TAKEN))
                elif k == "cwT":
                    dve.wait_ge(*filled(e))
                    v.tensor_copy(cw[:, :], ps(e)[:, 0:48]).then_inc(release_of(e), 1)
                elif k == "wukT":
                    dve.wait_ge(*filled(e))
                    v.tensor_copy(wukT[:, :], ps(e)[:, 0:256]).then_inc(release_of(e), 1)
                elif k == "gates":
                    hb = "p (h b) -> p h b"
                    dve.wait_ge(r_sem, 64)
                    link(v.tensor_tensor(s_y.rearrange(hb, h=4), sm[:, :, 132:136].rearrange("p b h -> p h b"), bc(dtb, NB), ALU.add))
                    link(v.tensor_scalar(s_neg, s_y, -1.0, None, ALU.mult))
                    v.tensor_tensor(s_neg, s_neg, s_y, ALU.min).then_inc(gate_steps_by_dve, 1)
                    dve.wait_ge(gate_steps_by_act, 1)
                    link(v.tensor_scalar(s_beta, s_beta, 1.0, None, ALU.add))
                    v.reciprocal(s_beta, s_beta)
                    link(v.scalar_tensor_tensor(s_y, s_y, 0.0, s_neg, ALU.max, ALU.add))
                    v.scalar_tensor_tensor(s_g.rearrange(hb, h=4), s_y.rearrange(hb, h=4), -1.0, bc(ealog, NB), ALU.mult, ALU.mult).then_inc(gate_steps_by_dve, 1)
                    for b in range(NB):
                        last = v.scalar_tensor_tensor(sm[:, b, 0:P], sm[:, b, 0:P], crs[:, b:b + 1], kvw, ALU.mult, ALU.mult)
                    last.then_inc(gate_steps_by_dve, 1)
                    dve.wait_ge(*filled(e))
                    v.tensor_copy(s_G, ps(e)[:, 0:32])
                    v.tensor_copy(s_Gt, ps(e)[:, 32:64]).then_inc(release_of(e), 1)
                    dve.wait_ge(*released(e))
                    v.tensor_scalar(s_nG, s_G, -1.0, None, ALU.mult)
                    v.tensor_tensor(s_dG, s_Gt, s_G, ALU.subtract).then_inc(gate_steps_by_dve, 1)
                elif k == "memT" and e[1] % 2:
                    dve.wait_ge(*filled(e))
                    v.tensor_copy(memT[:, 4:8, (e[1] // 2) * P:(e[1] // 2 + 1) * P], quad(ps(e)[:, :])).then_inc(release_of(e), 1)
                elif k == "cT" and e[1] == 1:
                    dve.wait_ge(*filled(e))
                    v.tensor_copy(cT[:, 512:1024], ps(e)[:, :]).then_inc(release_of(e), 1)
                elif k == "proj" and e[3:] == (1, 3):
                    h, part = e[1:3]
                    dve.wait_ge(*released(("proj", h, part, 0)))
                    dve.wait_ge(*released(("proj", h, part, 1)))
                    if h:
                        dve.wait_ge(*filled(("tok", h - 1, 1, part)))
                    y = qkv[:, part, :]
                    tap = [cw[:, j * 12 + part * 4 + h:j * 12 + part * 4 + h + 1] for j in range(4)]
                    link(v.tensor_scalar(y, hbuf[:, 3:3 + SEQ], tap[3], None, ALU.mult))
                    link(v.scalar_tensor_tensor(y, hbuf[:, 2:2 + SEQ], tap[2], y, ALU.mult, ALU.add))
                    link(v.scalar_tensor_tensor(y, hbuf[:, 1:1 + SEQ], tap[1], y, ALU.mult, ALU.add))
                    v.scalar_tensor_tensor(y, hbuf[:, 0:SEQ], tap[0], y, ALU.mult, ALU.add).then_inc(conv_done, 1)
                elif k == "ss" and e[2] == 0:
                    h = e[1]
                    dve.wait_ge(inverse_norms_ready, 2 * h + 2)
                    dve.wait_ge(gate_steps_by_act, 2)
                    hh = slice(h * NB, (h + 1) * NB)
                    v.tensor_tensor(sc_of["kb"], rs_k, s_beta[:, hh], ALU.mult)
                    v.tensor_scalar(sc_of["q"], rs_q, DND ** -0.5, None, ALU.mult)
                    link(v.tensor_tensor(sc_of["kd"], rs_k, s_eD[:, hh], ALU.mult))
                    v.tensor_tensor(sc_of["kbg"], sc_of["kb"], s_eG[:, hh], ALU.mult)
                    link(v.tensor_tensor(sc_of["qd"], sc_of["q"], s_eG[:, hh], ALU.mult))
                elif k == "tok":
                    h, a, part = e[1:]
                    dve.wait_ge(*filled(e))
                    src = quad(ps(e)[:, :])
                    qs_ = slice(4 * a, 4 * a + 4)
                    what = {1: ((R_KHAT, rs_k), (R_KB, sc_of["kb"]), (R_KBG, sc_of["kbg"]), (R_KD, sc_of["kd"])),
                            0: ((R_QHAT, sc_of["q"]), (R_QDEC, sc_of["qd"])),
                            2: ((R_VB, s_beta[:, h * NB:(h + 1) * NB]),)}[part]
                    for r, s in what:
                        last = v.tensor_tensor(quad(row(a, r)), src, bc(s[:, qs_], P), ALU.mult)
                    last.then_inc(release_of(e), 1)
                elif k == "GB":
                    h, a = e[1:]
                    dve.wait_ge(*filled(e))
                    v.tensor_tensor(quad(row(a, R_DARG)), quad(ps(e)[:, :]), rep(cst[:, C_NEG:C_NEG + P], 4), ALU.add).then_inc(release_of(e), 1)
                elif k in ("U", "At"):
                    h, a = e[1:]
                    dve.wait_ge(*filled(e))
                    dve.wait_ge(decays_ready, 2 * h + a + 1)
                    v.tensor_tensor(row(a, R_U if k == "U" else R_ATT), ps(e)[:, :], row(a, R_DEC), ALU.mult).then_inc(release_of(e), 1)
                elif k == "lv1":
                    h, a = e[1:]
                    dve.wait_ge(*filled(e))
                    v.tensor_tensor(quad(row(a, R_X)), rep(ident, 4), quad(ps(e)[:, :]), ALU.subtract).then_inc(release_of(e), 1)
                elif k == "XY":
                    h, a, s = e[1:]
                    w = 1 << s
                    dve.wait_ge(*filled(e))
                    halves = "p (n t) -> p n t"
                    if s < NLEV - 1:
                        xh = row(a, R_X).rearrange(halves, t=2 * w)[:, :, 0:w]
                        v.tensor_tensor(xh, xh, ps(e)[:, 0:256].rearrange(halves, t=w), ALU.subtract)
                    yh = row(a, R_Y).rearrange(halves, t=2 * w)[:, :, w:2 * w]
                    v.tensor_tensor(yh, yh, ps(e)[:, 256:512].rearrange(halves, t=w), ALU.subtract).then_inc(release_of(e), 1)
                elif k == "scanS" and e[2] < NB - 1:
                    h, b = e[1:]
                    key = ("S", h, b)
                    dve.wait_ge(*filled(key))
                    new = dn_s[:, ((b + 1) % 2) * P:((b + 1) % 2 + 1) * P]
                    if b == 0:
                        last = v.tensor_copy(new, ps(key)[:, 0:P])
                    else:
                        last = v.scalar_tensor_tensor(new, dn_s[:, (b % 2) * P:(b % 2 + 1) * P], s_gl[:, h * NB + b:h * NB + b + 1],
                                                      ps(key)[:, 0:P], ALU.mult, ALU.add)
                    last.then_inc(release_of(key), 1)
                elif k == "finals":
                    v.tensor_tensor(dm01[:, 0:P], cst[:, C_KT + 7 * P:C_KT + 8 * P], cst[:, C_CAUS:C_CAUS + P], ALU.add)
                    v.tensor_copy(dm01[:, P:2 * P], cst[:, C_KT + 6 * P:C_KT + 7 * P])
                    link(v.tensor_tensor(dm01[:, 2 * P:3 * P], cst[:, C_KT + 7 * P:C_KT + 8 * P], cst[:, C_CAUS:C_CAUS + P], ALU.add))
                elif k == "dm" and e[1] >= 2:
                    b = e[1]
                    d = score[:, score_at(b):score_at(b + 1)]
                    link(v.tensor_scalar(d, d, TAKEN, BIG, ALU.is_equal, ALU.mult))
                    kt0 = C_KT + (7 - b) * P
                    link(v.scalar_tensor_tensor(d, d, -BIG, cst[:, kt0:kt0 + (b + 1) * P], ALU.add, ALU.add))
                elif k == "sc":
                    b, h, c = e[1:]
                    lo, hi = idx_chunks(b)[c]
                    d = dm01[:, b * P:(2 * b + 1) * P] if b < 2 else score[:, score_at(b):score_at(b + 1)]
                    dve.wait_ge(*filled(e))
                    v.tensor_tensor_reduce(xs[:, h, lo:hi], d[:, lo:hi], ps(e)[:, 0:hi - lo], 1.0, -3.0e38, ALU.add, ALU.max,
                                                   mxp[:, 2 * h + c:2 * h + c + 1]).then_inc(release_of(e), 1)
                    if c == len(idx_chunks(b)) - 1:
                        dve.wait_ge(*released(e))
                        if c:
                            link(v.tensor_tensor(mxp[:, 2 * h:2 * h + 1], mxp[:, 2 * h:2 * h + 1], mxp[:, 2 * h + 1:2 * h + 2], ALU.max))
                        v.tensor_scalar(nmx[:, h:h + 1], mxp[:, 2 * h:2 * h + 1], -SLOPES[h], None, ALU.mult).then_inc(head_max_ready, 1)
                elif k == "msc":
                    b, i = e[1:]
                    dve.wait_ge(*filled(e))
                    link(v.tensor_reduce(mmx[:, 2 * i:2 * i + 2], ps(e)[:, :].rearrange("p (h n) -> p h n", h=2), AX, ALU.max))
                    v.tensor_scalar(mmx[:, 2 * i:2 * i + 2], mmx[:, 2 * i:2 * i + 2], -0.125, None, ALU.mult).then_inc(mem_max_ready, 1)
                elif k == "pT" and e[2] % 2:
                    dve.wait_ge(*filled(e))
                    v.tensor_copy(pTb[(order[e] - 1) % 3], ps(e)[:, :]).then_inc(release_of(e), 1)
                elif k == "mpT" and e[2] == 1:
                    dve.wait_ge(*filled(e))
                    v.tensor_copy(mpT[1], ps(e)[:, :]).then_inc(release_of(e), 1)
                elif k == "o":
                    b = e[1]
                    dve.wait_ge(exps_ready, SAH * (b + 1))
                    dve.wait_ge(*released(("msc", b, 0)))
                    dve.wait_ge(*released(("msc", b, 1)))
                    link(v.reciprocal(rinv, sums))
                    dve.wait_ge(*filled(e))
                    h8 = "p (h d) -> p h d"
                    v.tensor_tensor(otmp.rearrange(h8, h=8), ps(e)[:, :].rearrange(h8, h=8), bc(rinv, 64), ALU.mult).then_inc(release_of(e), 1)
                    dve.wait_ge(*released(e))
                    dve.wait_ge(*released(("z", b, 1)))
                    v.tensor_tensor(mix[:, 512:1024], otmp, zg[:, b, 512:1024], ALU.mult).then_inc(attention_gated, 1)
                elif k == "mixT" and e[2] == 1:
                    dve.wait_ge(*filled(e))
                    v.tensor_copy(mixT[1], ps(e)[:, :]).then_inc(release_of(e), 1)
                elif k == "y":
                    b, i = e[1:]
                    if i == 0:
                        dve.wait_ge(xr_sem, 16 * (b + 1))
                        if b:
                            dve.wait_ge(st_sem, 16 * b)
                    dve.wait_ge(*filled(e))
                    yh = yres[:, i * 512:(i + 1) * 512]
                    v.scalar_tensor_tensor(yh, xres[:, i * 512:(i + 1) * 512], ALPHA, ps(e)[:, :], ALU.mult, ALU.add).then_inc(release_of(e), 1)
                    dve.wait_ge(*released(e))
                    link(v.bn_stats(bst[:, 6 * i:6 * i + 6], yh))
                    if i == 1:
                        v.bn_aggr(mv, bst).then_inc(ln_stats_ready, 1)
                        dve.wait_ge(ln_rstd_ready, b + 1)
                        v.tensor_scalar(yres, yres, mv[:, 0:1], rstd, ALU.subtract, ALU.mult).then_inc(ln_scaled, 1)

        @block.scalar
        def _(act):
            sc = nc.scalar
            act_chain = ctx.enter_context(nc.semaphore("act_chain"))
            steps = [0]

            def link(ins):
                steps[0] += 1
                ins.then_inc(act_chain, 1)
                act.wait_ge(act_chain, steps[0])

            def copy(dst, src, scale=1.0):
                return sc.activation(dst, src, ACT.Copy, scale=scale)

            act.wait_ge(small_constants_set, 1)
            for e in plan:
                k = e[0]
                if k == "xT" and e[1] % 2 == 0:
                    act.wait_ge(*filled(e))
                    copy(xT[:, e[1] // 2, 0:4, :], ps(e)[:, :].rearrange("p (k t) -> p k t", k=4)).then_inc(release_of(e), 1)
                elif k == "kiT":
                    act.wait_ge(*filled(e))
                    copy(kiT[:, e[1] * 512:(e[1] + 1) * 512], ps(e)[:, :]).then_inc(release_of(e), 1)
                elif k in ("qiT", "qsT", "qmT") and e[2] == 0:
                    act.wait_ge(*filled(e))
                    dst = {"qiT": qiT, "qsT": qsTv, "qmT": qmTv}[k]
                    copy(dst[:, e[1], 0:512], ps(e)[:, :]).then_inc(release_of(e), 1)
                elif k == "idx":
                    b, j, c = e[1:]
                    lo, hi = idx_chunks(b)[c]
                    act.wait_ge(*filled(e))
                    if order[e] > 3:
                        act.wait_ge(scores_summed, order[e] - 3)
                    sc.activation(rbuf[(order[e] - 1) % 3][:, 0:hi - lo], ps(e)[:, 0:hi - lo], ACT.Relu, scale=IXD ** -0.5).then_inc(release_of(e), 1)
                elif k == "gates":
                    act.wait_ge(gate_steps_by_dve, 1)
                    for b in range(NB):
                        link(sc.activation(junk[:, :], sm[:, b, 0:P], ACT.Square, accum_out=css[:, b:b + 1]))
                    sc.activation(s_beta.rearrange("p (h b) -> p h b", h=4), sm[:, :, 128:132].rearrange("p b h -> p h b"), ACT.Exp, scale=-1.0)
                    act.wait_ge(r_sem, 64)
                    sc.activation(ealog, alog, ACT.Exp)
                    link(sc.activation(s_neg, s_neg, ACT.Exp))
                    sc.activation(s_neg, s_neg, ACT.Ln, bias=one1)
                    link(sc.activation(crs, css, ACT.Ln, bias=eps_rms, scale=1.0 / RANK))
                    sc.activation(crs, crs, ACT.Exp, scale=-0.5).then_inc(gate_steps_by_act, 1)
                    act.wait_ge(gate_steps_by_dve, 4)
                    sc.activation(s_eG, s_G, ACT.Exp)
                    sc.activation(s_eD, s_dG, ACT.Exp)
                    sc.activation(s_gl, s_Gt, ACT.Exp).then_inc(gate_steps_by_act, 1)
                elif k == "memT" and e[1] % 2 == 0:
                    act.wait_ge(*filled(e))
                    copy(memT[:, 0:4, (e[1] // 2) * P:(e[1] // 2 + 1) * P], ps(e)[:, :].rearrange("p (k t) -> p k t", k=4)).then_inc(release_of(e), 1)
                elif k == "kmT":
                    act.wait_ge(*filled(e))
                    copy(kmT[:, :], ps(e)[:, :]).then_inc(release_of(e), 1)
                elif k == "vm":
                    act.wait_ge(*filled(e))
                    copy(vm[:, :], ps(e)[:, :]).then_inc(release_of(e), 1)
                elif k == "cT" and e[1] == 0:
                    act.wait_ge(*filled(e))
                    copy(cT[:, 0:512], ps(e)[:, :]).then_inc(release_of(e), 1)
                elif k == "proj" and e[4] == 3:
                    h, part, t = e[1:4]
                    key = ("proj", h, part, t)
                    n = h * 3 + (1, 0, 2).index(part)
                    act.wait_ge(*filled(key))
                    if n:
                        act.wait_ge(conv_done, n)
                    copy(hbuf[:, 3 + t * 512:3 + (t + 1) * 512], ps(key)[:, :]).then_inc(release_of(key), 1)
                    if t == 1:
                        act.wait_ge(conv_done, n + 1)
                        sc.activation(qkv[:, part, :], qkv[:, part, :], ACT.Silu).then_inc(silu_done, 1)
                elif k == "ss":
                    h, part = e[1:]
                    n = order[e]
                    act.wait_ge(silu_done, 3 * h + 2)
                    at = 0 if part else 1024
                    sc.activation(arena[:, at:at + 1024], qkv[:, part, :], ACT.Square).then_inc(squares_ready, 1)
                    act.wait_ge(*filled(e))
                    rs = rs_k if part else rs_q
                    sc.activation(rs, ps(e)[:, 0:NB], ACT.Ln, bias=eps_rms).then_inc(release_of(e), 1)
                    act.wait_ge(*released(e))
                    sc.activation(rs, rs, ACT.Exp, scale=-0.5).then_inc(inverse_norms_ready, 1)
                elif k == "bT":
                    h, a, w = e[1:]
                    act.wait_ge(*filled(e))
                    copy(row(a, (R_KHATT, R_KBT, R_QHATT, R_QDECT)[w]), ps(e)[:, :]).then_inc(release_of(e), 1)
                elif k == "GB":
                    h, a = e[1:]
                    act.wait_ge(*released(e))
                    for i in range(4):
                        col = h * NB + 4 * a + i
                        d = blk(row(a, R_DEC), i)
                        last = sc.activation(d, d, ACT.Exp, bias=s_nG[:, col:col + 1])
                    last.then_inc(decays_ready, 1)
                elif k == "M":
                    h, a, s = e[1:]
                    act.wait_ge(*filled(e))
                    copy(row(a, R_M1), ps(e)[:, :]).then_inc(release_of(e), 1)
                elif k == "nw":
                    h, a = e[1:]
                    act.wait_ge(*filled(e))
                    copy(row(a, R_NW), ps(e)[:, :], -1.0).then_inc(release_of(e), 1)
                elif k == "scanV":
                    h, b = e[1:]
                    key = ("V", h, b)
                    act.wait_ge(*filled(key))
                    copy(vnew[:, (b % 2) * P:(b % 2 + 1) * P], ps(key)[:, 0:P]).then_inc(release_of(key), 1)
                elif k == "scanS":
                    h, b = e[1:]
                    key = ("O", h, b)
                    act.wait_ge(*filled(key))
                    copy(oall[:, b, h, :], ps(key)[:, 0:P])
                    if b or h:
                        act.wait_ge(*released(("O", h, b - 1) if b else ("O", h - 1, NB - 1)))
                    sc.activation(junk[:, :], ps(key)[:, 0:P], ACT.Square, accum_out=s_oss[:, b * 4 + h:b * 4 + h + 1]).then_inc(release_of(key), 1)
                elif k == "z" and e[2:] == (1, 3):
                    b = e[1]
                    act.wait_ge(*filled(("z", b, 0)))
                    act.wait_ge(*filled(("z", b, 1)))
                    sc.activation(zg[:, b, 0:512], ps(("z", b, 0))[:, :], ACT.Silu).then_inc(release_of(("z", b, 0)), 1)
                    sc.activation(zg[:, b, 512:1024], ps(("z", b, 1))[:, :], ACT.Silu).then_inc(release_of(("z", b, 1)), 1)
                elif k == "finals":
                    act.wait_ge(*released(("O", DNH - 1, NB - 1)))
                    link(sc.activation(s_orn, s_oss, ACT.Ln, bias=eps_rms, scale=1.0 / DND))
                    sc.activation(s_orn, s_orn, ACT.Exp, scale=-0.5).then_inc(output_norms_ready, 1)
                elif k == "qabs":
                    for odd in range(2):
                        key = (*e, odd)
                        act.wait_ge(*filled(key))
                        for m in range(2):
                            h = 2 * m + odd
                            last = copy(qab[:, h * P:(h + 1) * P], ps(key)[:, m * P:(m + 1) * P], SAD ** -0.5 / SLOPES[h])
                        last.then_inc(release_of(key), 1)
                elif k == "sc":
                    b, h, c = e[1:]
                    if c == len(idx_chunks(b)) - 1:
                        act.wait_ge(head_max_ready, SAH * b + h + 1)
                        p_ = xs[:, h, 0:(b + 1) * P]
                        sc.activation(p_, p_, ACT.Exp, scale=SLOPES[h], bias=nmx[:, h:h + 1], accum_out=sums[:, h:h + 1]).then_inc(exps_ready, 1)
                elif k == "msc":
                    b, i = e[1:]
                    act.wait_ge(mem_max_ready, 2 * b + i + 1)
                    for m in range(2):
                        g = 2 * m + i
                        last = sc.activation(mp[:, g * 256:(g + 1) * 256], ps(e)[:, m * 256:(m + 1) * 256], ACT.Exp, scale=0.125,
                                             bias=mmx[:, 2 * i + m:2 * i + m + 1], accum_out=sums[:, 4 + g:5 + g])
                    last.then_inc(release_of(e), 1)
                elif k == "pT" and e[2] % 2 == 0:
                    act.wait_ge(*filled(e))
                    copy(pTb[(order[e] - 1) % 3], ps(e)[:, :]).then_inc(release_of(e), 1)
                elif k == "lat" and e[2] == e[1]:
                    key = ("lat", e[1])
                    act.wait_ge(*filled(key))
                    copy(latT, ps(key)[:, :]).then_inc(release_of(key), 1)
                elif k == "mpT" and e[2] == 0:
                    act.wait_ge(*filled(e))
                    copy(mpT[0], ps(e)[:, :]).then_inc(release_of(e), 1)
                elif k == "mixT" and e[2] == 0:
                    act.wait_ge(*filled(e))
                    copy(mixT[0], ps(e)[:, :]).then_inc(release_of(e), 1)
                elif k == "y" and e[2] == 1:
                    b = e[1]
                    act.wait_ge(ln_stats_ready, b + 1)
                    link(sc.activation(rstd, mv[:, 1:2], ACT.Ln, bias=eps_ln))
                    sc.activation(rstd, rstd, ACT.Exp, scale=-0.5).then_inc(ln_rstd_ready, 1)

        @block.gpsimd
        def _(pool):
            g = nc.gpsimd
            pool_chain = ctx.enter_context(nc.semaphore("pool_chain"))
            steps = [0]

            def link(ins):
                steps[0] += 1
                ins.then_inc(pool_chain, 1)
                pool.wait_ge(pool_chain, steps[0])

            def rep(ap, n):
                return ap.unsqueeze(1).broadcast_to([P, n, ap.shape[1]])

            def quad(ap):
                return ap.rearrange("p (b t) -> p b t", b=4)

            pool.wait_ge(c_sem, 16)
            for e in plan:
                k = e[0]
                if k in ("lv1", "M"):
                    h, a = e[1:3]
                    s = e[3] if k == "M" else 0
                    if s == 0:
                        pool.wait_ge(*released(("U", h, a)))
                    elif s == 2:
                        pool.wait_ge(*filled(("lv1", h, a)))
                        pool.wait_ge(y_started, 2 * h + a + 1)
                    elif s > 2:
                        pool.wait_ge(*filled(("M", h, a, s - 2)))
                    uo = row(a, R_UO[s % 2])
                    g.tensor_tensor(quad(uo), quad(row(a, R_U)), rep(cst[:, C_LEV + s * P:C_LEV + (s + 1) * P], 4),
                                    ALU.mult).then_inc(level_masked, 1)
                    if s == 0:
                        pool.wait_ge(*released(("At", h, a)))
                        pool.wait_ge(level_masked, (h * NLEV) * 2 + a + 1)
                        g.tensor_tensor(quad(row(a, R_Y)), rep(ident, 4), quad(uo), ALU.subtract).then_inc(y_started, 1)
                elif k == "o":
                    b = e[1]
                    pool.wait_ge(output_norms_ready, 1)
                    pool.wait_ge(*released(("z", b, 0)))
                    if b:
                        pool.wait_ge(*filled(("mixT", b - 1, 0)))
                    m = mix[:, 0:512].rearrange("p (h d) -> p h d", h=4)
                    link(g.tensor_tensor(m, oall[:, b, :, :], s_orn[:, 4 * b:4 * b + 4].unsqueeze(2).broadcast_to([P, 4, P]), ALU.mult))
                    link(g.tensor_tensor(m, m, rep(nrmw, 4), ALU.mult))
                    g.tensor_tensor(mix[:, 0:512], mix[:, 0:512], zg[:, b, 0:512], ALU.mult).then_inc(deltanet_gated, 1)
                elif k == "y" and e[2] == 1:
                    b = e[1]
                    pool.wait_ge(ln_scaled, b + 1)
                    if b == 0:
                        pool.wait_ge(ln_sem, 32)
                    link(g.tensor_tensor(yres, yres, lng, ALU.mult))
                    g.tensor_tensor(yres, yres, lnb, ALU.add).then_inc(row_finished, 1)


_INS = ["x", "mem", "w_in", "conv_w", "dn_a_log", "dn_dt_bias", "dn_norm_w", "kv_norm_w", "w_uk", "w_uv", "w_mem_kv",
        "w_out", "ln_g", "ln_b"]


def kernel(**inputs):
    import numpy as _np
    import concourse.bacc as _bacc
    from concourse import mybir as _mybir
    from concourse.bass_utils import run_bass_kernel_spmd as _run

    nc = _bacc.Bacc("TRN2", target_bir_lowering=False, num_devices=1)
    arrays, args = {}, []
    for name in _INS:
        a = _np.ascontiguousarray(inputs[name])
        arrays[f"in_{name}"] = a
        args.append(nc.dram_tensor(f"in_{name}", a.shape, _mybir.dt.from_np(a.dtype), kind="ExternalInput").ap())
    consts = shape_constants()
    arrays["in_consts"] = consts
    args.append(nc.dram_tensor("in_consts", consts.shape, _mybir.dt.float32, kind="ExternalInput").ap())
    args.append(nc.dram_tensor("out_y", (1, SEQ, DM), _mybir.dt.float32, kind="ExternalOutput").ap())
    build(nc, *args)
    r = _run(nc, [arrays], core_ids=[0])
    return r.results[0]["out_y"]
```

```python
from contextlib import ExitStack

import numpy as np

import concourse.bass as bass
from concourse import mybir

P = 128
SEQ, DM = 1024, 1024
NB = SEQ // P
KT = DM // P
NMEM = 256
DNH, DND = 4, 128
SAH, SAD, RANK = 4, 64, 128
IXH, IXD = 8, 64
TOPK = 256
DNW = DNH * DND
OFF, acc_ = {}, 0
for name_, width_ in (("qa", DNW), ("ka", DNW), ("va", DNW), ("za", DNW), ("ba", DNH), ("aa", DNH), ("qs", 256),
                      ("ckv", RANK), ("zs", 256), ("qi", IXH * IXD), ("ki", IXD), ("wi", IXH), ("qm", 256), ("zm", 256)):
    OFF[name_] = acc_
    acc_ += width_
ALPHA = 2.0 ** 0.25
LN_EPS, RMS_EPS = 1e-5, 1e-6
SLOPES = [2.0 ** (-8.0 * (i + 1) / SAH) for i in range(SAH)]
BIG = 1.0e30
TINY = 2.0 ** -126
N_SEL = NB - 2
FLOAT_BITS = 32
COUNT_GROUPS = ((7, 2), (6, 3), (5, 4))
NLEV = 7
BLOCK_ORDER = (3, 4, 2, 5, 1, 6, 0, 7)
PLACE = {b: n for n, b in enumerate(BLOCK_ORDER)}
XS_W = SAH * (SEQ + P)
F32 = mybir.dt.float32
F32R = mybir.dt.float32r
BF16 = mybir.dt.bfloat16
U32 = mybir.dt.uint32
ALU = mybir.AluOpType
ACT = mybir.ActivationFunctionType
AX = mybir.AxisListType.X
C_ID, C_TRI, C_NEG, C_CAUS, C_ONE, C_LEV, C_KT = 0, 128, 256, 384, 512, 640, 640 + NLEV * 128
C_BIT = C_KT + SEQ
C_ALL = C_BIT + 32


def shape_constants():
    c = np.zeros((P, C_ALL), np.float32)
    p, f = np.arange(P)[:, None], np.arange(P)[None, :]
    c[:, C_ID:C_ID + P] = p == f
    c[:, C_TRI:C_TRI + P] = p <= f
    c[:, C_NEG:C_NEG + P] = np.where(p <= f, 0.0, -BIG)
    c[:, C_CAUS:C_CAUS + P] = np.where(f <= p, 0.0, -BIG)
    c[:, C_ONE:C_ONE + P] = 1.0
    for i in range(NLEV):
        s = 1 << i
        c[:, C_LEV + i * P:C_LEV + (i + 1) * P] = (p // (2 * s) == f // (2 * s)) & (p % (2 * s) < s) & (f % (2 * s) >= s)
    c[:, C_KT:C_BIT] = np.arange(SEQ)[None, :] - p - (SEQ - P)
    c[:, C_BIT:] = (1 << np.arange(32, dtype=np.uint32)).view(np.float32)
    return c


def idx_chunks(b):
    w = (b + 1) * P
    return [(0, w)] if w <= 512 else [(0, w // 2), (w // 2, w)]


def score_at(b):
    return sum((i + 1) * P for i in range(2, b))


SCORE_W = score_at(NB)


def make_plan():
    plan = []
    add = plan.append
    selection = [[*[("count", it, b) for b in group], *[("update", it)] * (group == COUNT_GROUPS[-1])]
                 for it in range(FLOAT_BITS) for group in COUNT_GROUPS]
    selection += [[("reach", 7), ("reach", 2)], [("reach", 6), ("reach", 3)], [("reach", 5), ("reach", 4), ("threshold",)]]
    selection += [[("dm", b)] for b in (3, 4, 2, 5, 6, 7)]

    def select(n=1):
        for _ in range(n):
            if selection:
                for e in selection.pop(0):
                    add(e)

    for i in range(NB):
        add(("xT", i))
    add(("kiT", 0))
    for m in range(2):
        for i in range(2):
            add(("xT", NB + 2 * m + i))
        add(("qiT", m, 0))
    for i in range(NB + 4, 2 * NB):
        add(("xT", i))
    add(("kiT", 1))
    for m, t in ((0, 1), (1, 1), (2, 0), (2, 1), (3, 0), (3, 1)):
        add(("qiT", m, t))
    for b in range(NB):
        add(("small", b))
    add(("wis",))
    add(("cwT",))
    add(("wukT",))

    def part_of(h, part, second=(), fourth=()):
        units = [[("proj", h, part, t, s)] for t in range(2) for s in range(4)]
        units[1] = [*second, *units[1]]
        units[3] = [*fourth, *units[3], ("conv", h, part, 0)]
        units[7] = [*units[7], ("conv", h, part, 1)]
        return units

    def head(h, after_k=(), after_q=(), after_v=()):
        return [*part_of(h, 1), *after_k,
                *part_of(h, 0, [("silu", h, 1)], [("ss", h, 1)]), *after_q,
                *part_of(h, 2, [("silu", h, 0)], [("ss", h, 0)]), *after_v[:1],
                [("silu", h, 2), ("norms", h)], *after_v[1:]]

    first_work = [*[[("memT", i)] for i in range(4)],
                  *head(0, [[("kmT",)], [("gates",)]], [[("vm",)], [("gate_sums",)]], [[("cT", 0)], [("cT", 1)]])]
    n_units = len(first_work)
    index_tiles = [("idx", b, j, c) for b in range(2, NB) for c in range(len(idx_chunks(b))) for j in range(IXH)]
    for i, e in enumerate(index_tiles):
        add(e)
        if (n_units - len(first_work)) * len(index_tiles) < n_units * (i + 1):
            for u in first_work.pop(0):
                add(u)
    for unit in first_work:
        for u in unit:
            add(u)
    attn_q = [[(k, m, t, s)] for k in ("qsT", "qmT") for m in range(2) for t in range(2) for s in range(4)]
    work = [[*head(1, (), (), attn_q[0:11])],
            [*attn_q[11:16], *head(2, (), (), attn_q[16:22])],
            [*attn_q[22:24], *head(3, (), (), attn_q[24:32])],
            [[("z", b, half, s)] for b in range(NB) for half in range(2) for s in range(4)]]
    slots_per_head = 26
    for h in range(DNH):
        todo = work[h]
        n_units, at = len(todo), [0]

        def fill():
            at[0] += 1
            while todo and n_units - len(todo) < n_units * at[0] / slots_per_head:
                for e in todo.pop(0):
                    add(e)
            select(1 if at[0] % 5 else 2)

        for a in range(2):
            add(("tok", h, a, 1))
            add(("tok", h, a, 0))
            add(("tok", h, a, 2))
            fill()
        add(("GB", h, 0))
        add(("GB", h, 1))
        for a in range(2):
            for w in range(4):
                add(("bT", h, a, w))
            fill()
        for a in range(2):
            add(("U", h, a))
            add(("At", h, a))
        fill()
        for a in range(2):
            add(("lv1", h, a))
        fill()
        for s in range(1, NLEV):
            for a in range(2):
                add(("M", h, a, s))
            fill()
            for a in range(2):
                add(("XY", h, a, s))
            fill()
        for a in range(2):
            add(("nw", h, a))
        for b in range(NB):
            add(("scanV", h, b))
            fill()
            add(("scanS", h, b))
        assert not todo
    add(("finals",))

    def scores(b, h):
        return [("sc", b, h, c) for c in range(len(idx_chunks(b)))]

    def attention(b):
        units = [[("pT", b, k)] for k in range(b + 1)] + [[("mpT", b, i)] for i in range(2)]
        units[0].append(("rinv", b))
        for k in range(b + 1):
            units[k + 2].append(("lat", b, k))
        return units

    def output(b):
        return [[("mixT", b, 0), ("mixT", b, 1)], [("y", b, 0)]]

    def normalise(b):
        return [("rstd", b), ("ln", b)]

    def merged(*queues):
        placed = sorted(((i + off) / (len(q) + off), qi, i) for qi, (off, q) in enumerate(queues) for i in range(len(q)))
        return [queues[qi][1][i] for _, qi, i in placed]

    first = BLOCK_ORDER[0]
    select(999)
    for e in [("deltanet_gate", first), ("qabs", first), *[t for h in range(SAH) for t in scores(first, h)], ("msc", first, 0), ("msc", first, 1)]:
        add(e)
    for n, b in enumerate(BLOCK_ORDER):
        queues = [(0, attention(b))]
        if n:
            queues.append((1, output(BLOCK_ORDER[n - 1]) + [[("deltanet_gate", b)]]))
        if n > 1:
            for e in normalise(BLOCK_ORDER[n - 2]):
                add(e)
        if n + 1 < NB:
            nb = BLOCK_ORDER[n + 1]
            queues.append((0.5, [[("qabs", nb)], scores(nb, 0), *[scores(nb, h) for h in range(1, SAH)]]))
        for unit in merged(*queues):
            for e in unit:
                add(e)
        if n + 1 < NB:
            add(("msc", nb, 0))
            add(("msc", nb, 1))
        if n:
            add(("y", BLOCK_ORDER[n - 1], 1))
        add(("o", b))
    for e in [*normalise(BLOCK_ORDER[-2]), *sum(output(BLOCK_ORDER[-1]), []), ("y", BLOCK_ORDER[-1], 1), *normalise(BLOCK_ORDER[-1])]:
        add(e)
    return plan


POOL_OF = {"xT": "P", "kiT": "P", "small": "P", "qiT": "P", "idx": "D", "cwT": "P", "wukT": "P", "gate_sums": "P",
           "memT": "P", "kmT": "P", "vm": "P", "cT": "P", "tok": "D", "GB": "D",
           "bT": "D", "U": "D", "At": "D", "lv1": "D", "M": "D", "XY": "D", "nw": "D", "sc": "L",
           "msc": "D", "mixT": "D", "y": "L", "pT": "D", "lat": "P", "mpT": "D", "o": "P"}


def tiles_of(e):
    k = e[0]
    if k == "proj":
        return [("P", ("proj", *e[1:4]))] if e[4] == 0 else []
    if k in ("qsT", "qmT"):
        return [("L", e[:3])] if e[3] == 0 else []
    if k == "ss":
        return [("L", ("ss", e[1]))] if e[2] == 1 else []
    if k == "z":
        return [("PL"[e[2]], ("z", e[1], e[2]))] if e[3] == 0 else []
    if k == "lat":
        return [("P", ("lat", e[1]))] if e[2] == 0 else []
    if k == "qabs":
        return [("D", (*e, 0)), ("D", (*e, 1))]
    if k == "scanV":
        return [("D", ("V", e[1], e[2]))]
    if k == "scanS":
        return [("D", ("S", e[1], e[2]))] * (e[2] < NB - 1) + [("D", ("O", e[1], e[2]))]
    return [(POOL_OF[k], e)] if k in POOL_OF else []


def weight_loads():
    loads = [("ki", [("w_in", OFF["ki"], 64, 0), ("w_in", OFF["ki"], 64, 64)]),
             ("qi0", [("w_in", OFF["qi"], 256, 0)]), ("qi1", [("w_in", OFF["qi"] + 256, 256, 0)]),
             ("small", [("w_in", OFF["ckv"], P, 0), ("w_in", OFF["ba"], 8, P), ("w_in", OFF["wi"], 8, P + 8)]),
             ("mk", [("w_mem_kv", 0, 256, 0)]), ("mv", [("w_mem_kv", 256, 256, 0)])]
    for h in range(DNH):
        loads.append((f"kq{h}", [("w_in", OFF["ka"] + h * P, P, 0), ("w_in", OFF["qa"] + h * P, P, P)]))
        loads.append((f"v{h}", [("w_in", OFF["va"] + h * P, P, 0)]))
        if h == 1:
            loads.append(("qs", [("w_in", OFF["qs"], 256, 0)]))
        if h == 2:
            loads.append(("qm", [("w_in", OFF["qm"], 256, 0)]))
    loads += [("z0", [("w_in", OFF["za"], 256, 0)]), ("z1", [("w_in", OFF["za"] + 256, 256, 0)]),
              ("z2", [("w_in", OFF["zs"], 256, 0)]), ("z3", [("w_in", OFF["zm"], 256, 0)])]
    return loads


def build(nc, x, mem, w_in, conv_w, dn_a_log, dn_dt_bias, dn_norm_w, kv_norm_w, w_uk, w_uv, w_mem_kv, w_out,
          ln_g, ln_b, consts, out, plan=None):
    plan = plan or make_plan()
    ctx = ExitStack()
    with ctx:
        def sb(name, cols):
            return ctx.enter_context(nc.sbuf_tensor(name, [P, cols], F32))

        def sem(name):
            return ctx.enter_context(nc.semaphore(name))

        cst = sb("cst", C_ALL)
        xT_ = sb("xT", NB * KT * P)
        ring = sb("ring", 4 * 2048)
        score = sb("score", SCORE_W)
        small = sb("small", NB * 144)
        cT = sb("cT", SEQ)
        qmT = sb("qmT", 2 * SEQ)
        qsT = sb("qsT", 2 * SEQ)
        hbuf = sb("hbuf", 3 + SEQ)
        qkvT = sb("qkvT", 3 * SEQ)
        kmT = sb("kmT", 2 * NMEM)
        vm = sb("vm", 2 * NMEM)
        wukT = sb("wukT", 2 * RANK)
        wuv = sb("wuv", SAH * SAD)
        at_ = nc.sbuf_base
        q2_ = nc.alloc_sbuf_tensor_at("q2", [P, IXH * SEQ], F32R, offset=at_)
        khi_ = nc.alloc_sbuf_tensor_at("khi", [P, SEQ], F32R, offset=at_ + 4 * IXH * SEQ)
        klo_ = nc.alloc_sbuf_tensor_at("klo", [P, SEQ], F32R, offset=at_ + 4 * (IXH + 1) * SEQ)
        oall_ = sb("oall", 4 * SEQ)
        arena = sb("arena", 24 * 512)
        cw = sb("cw", 48)
        rows = sb("rows", 128 + 128 + 8)
        sc32 = sb("sc32", 14 * 32)
        hsc = sb("hsc", 16 + 16 + 6 * 8)
        dn_s = sb("dn_s", 2 * 128)
        vnew = sb("vnew", 2 * 128)
        wis_ = sb("wis", 64)
        misc = sb("misc", 64)
        sel = sb("sel", 10 * N_SEL)
        junk = sb("junk", 128)

        ident = cst[:, C_ID:C_ID + P]
        tri = cst[:, C_TRI:C_TRI + P]
        ones = cst[:, C_ONE:C_ONE + P]
        xT = xT_[:, :].rearrange("p (b k t) -> p b k t", b=NB, k=KT)
        zg = xT_[:, :].rearrange("p (b c) -> p b c", b=NB)
        slots = ring[:, :].rearrange("p (s k n) -> p s k n", s=4, k=KT)
        wout = ring[:, :].rearrange("p (k n) -> p k n", k=KT)
        q2 = q2_[:, :].rearrange("p (j t) -> p j t", j=IXH)
        khi, klo = khi_[:, :], klo_[:, :]
        oall = oall_[:, :].rearrange("p (b h d) -> p b h d", b=NB, h=DNH)
        sm = small[:, :].rearrange("p (b c) -> p b c", b=NB)
        qmTv = qmT[:, :].rearrange("p (m t) -> p m t", m=2)
        qsTv = qsT[:, :].rearrange("p (m t) -> p m t", m=2)
        qkv = qkvT[:, :].rearrange("p (a t) -> p a t", a=3)
        wis = wis_[:, :].rearrange("p (b j) -> p b j", b=NB)
        kvw, nrmw = rows[:, 0:128], rows[:, 128:256]
        alog, dtb = rows[:, 256:260], rows[:, 260:264]
        rbuf = [arena[:, 6144 + i * 512:6656 + i * 512] for i in range(3)]
        memnat = arena[:, 7680:9728].rearrange("p (m c) -> p m c", m=2)
        memT = arena[:, 9728:11776].rearrange("p (k t) -> p k t", k=KT)
        wuknat = arena[:, 11776:12032]
        cwnat = arena[:, 12032:12160]
        xnat = [score[:, i * 1024:(i + 1) * 1024] for i in range(4)]

        def row(a, i):
            return arena[:, (12 * a + i) * 512:(12 * a + i + 1) * 512]

        def blk(ap, i):
            return ap[:, i * P:(i + 1) * P]

        R_KHAT, R_KB, R_QHAT, R_QDEC, R_KBG, R_KD, R_VB, R_KHATT, R_KBT, R_QHATT, R_QDECT, R_DEC = range(12)
        R_UO, R_M1, R_NW, R_X, R_U, R_ATT, R_Y, R_DARG = (0, 1), 2, 0, 7, 8, 9, 11, 11

        def av(at, n):
            return arena[:, at:at + n]

        def xs_of(b):
            at = 0 if PLACE[b] % 2 else XS_W - SAH * (b + 1) * P
            return av(at, SAH * (b + 1) * P).rearrange("p (h n) -> p h n", h=SAH)

        pTb = [av(XS_W + i * 512, 512) for i in range(3)]
        latT = av(6144, 512)
        qab = av(6656, 512)
        mp = av(7168, 1024)
        mpT = [av(8192 + i * 512, 512) for i in range(2)]
        mix = av(9216, 1024)
        mixT = [av(10240 + i * 512, 512) for i in range(2)]
        yres = av(11264, 1024)
        otmp = hbuf[:, 384:896]
        lng, lnb = qkvT[:, 0:1024], qkvT[:, 1024:2048]
        xres = qkvT[:, 2048:3072]
        picked_above, picked_ties, tie_rank = (qkvT[:, i * 1024:(i + 1) * 1024] for i in range(3))
        dm01 = hbuf[:, 0:384]
        (s_beta, s_y, s_neg, s_g, s_G, s_Gt, s_nG, s_dG, s_eG, s_eD, s_gl, s_oss, s_orn, s_tmp) = (
            sc32[:, i * 32:(i + 1) * 32] for i in range(14))
        css, crs = misc[:, 0:8], misc[:, 8:16]
        n_low, n_half, t_sign, n_off, bit_kept, bits, bits_tried, candidate, t_high, t_low = (
            sel[:, i * N_SEL:(i + 1) * N_SEL] for i in range(10))
        signs = [cst[:, C_KT + i * 512:C_KT + (i + 1) * 512].bitcast(BF16) for i in range(2)]
        eps_rms, eps_ln, one1 = misc[:, 16:17], misc[:, 17:18], misc[:, 18:19]
        mxp, nmx = misc[:, 20:28], misc[:, 28:32]
        sums, rinv = misc[:, 32:40], misc[:, 40:48]
        mmx = misc[:, 48:52]
        bst, mv, rstd, ealog = hsc[:, 0:12], hsc[:, 12:14], hsc[:, 14:15], misc[:, 52:56]
        rs_k, rs_q = hsc[:, 16:24], hsc[:, 24:32]
        sc_of = {n: hsc[:, 32 + 8 * i:40 + 8 * i] for i, n in enumerate(("kb", "q", "qd"))}

        pools = {"P": (0, 1), "L": (2, 3), "D": (4, 5, 6, 7)}
        banks = [ctx.enter_context(nc.psum_tensor(f"bank{i}", [P, 512], F32)) for i in range(8)]
        filled_sem = [sem(f"filled{i}") for i in range(8)]
        released_sem = [sem(f"released{i}") for i in range(8)]
        bank_of, use_of, count = {}, {}, {k: 0 for k in pools}
        for e in plan:
            for pool, key in tiles_of(e):
                n = count[pool]
                bank_of[key] = pools[pool][n % len(pools[pool])]
                use_of[key] = n // len(pools[pool]) + 1
                count[pool] += 1

        def ps(key):
            return banks[bank_of[key]]

        def vacated(key):
            return released_sem[bank_of[key]], use_of[key] - 1

        def first(key):
            return use_of[key] == 1

        def filled(key):
            return filled_sem[bank_of[key]], use_of[key]

        def released(key):
            return released_sem[bank_of[key]], use_of[key]

        def fill_of(key):
            return filled_sem[bank_of[key]]

        def release_of(key):
            return released_sem[bank_of[key]]

        small_constants_set = sem("small_constants_set")
        gate_steps_by_dve = sem("gate_steps_by_dve")
        key_hi_ready = sem("key_hi_ready")
        query_hi_ready = sem("query_hi_ready")
        scores_summed = sem("scores_summed")
        candidates_ready = sem("candidates_ready")
        keys_counted = sem("keys_counted")
        keys_selected = sem("keys_selected")
        conv_done = sem("conv_done")
        head_max_ready = sem("head_max_ready")
        mem_max_ready = sem("mem_max_ready")
        attention_gated = sem("attention_gated")
        ln_stats_ready = sem("ln_stats_ready")
        ln_scaled = sem("ln_scaled")
        silu_done = sem("silu_done")
        squares_ready = sem("squares_ready")
        k_squares_summed = sem("k_squares_summed")
        inverse_norms_ready = sem("inverse_norms_ready")
        decays_ready = sem("decays_ready")
        exps_ready = sem("exps_ready")
        gate_steps_by_act = sem("gate_steps_by_act")
        output_norms_ready = sem("output_norms_ready")
        ln_rstd_ready = sem("ln_rstd_ready")
        level_masked = sem("level_masked")
        keys_decayed = sem("keys_decayed")
        y_started = sem("y_started")
        deltanet_gated = sem("deltanet_gated")
        row_finished = sem("row_finished")
        order = {}
        seen = {}
        for e in plan:
            seen[e[0]] = seen.get(e[0], 0) + 1
            order[e] = seen[e[0]]

        loads = weight_loads()
        load_at = {n: i for i, (n, _) in enumerate(loads)}
        loaded_sem = [sem(f"loaded{i}") for i in range(4)]
        last_use = {"ki": ("kiT", 1), "small": ("small", NB - 1), "qi0": ("qiT", 1, 1), "qi1": ("qiT", 3, 1),
                    "qs": ("qsT", 1, 1), "qm": ("qmT", 1, 1), "mk": ("kmT",), "mv": ("vm",)}
        for h in range(DNH):
            last_use[f"kq{h}"] = ("proj", h, 0, 1)
            last_use[f"v{h}"] = ("proj", h, 2, 1)
        load_need = {}
        total = [0] * 4
        for i, (n, pieces) in enumerate(loads):
            total[i % 4] += 16 * len(pieces)
            load_need[n] = total[i % 4]
        x_sem = [sem(f"x_loaded{i}") for i in range(4)]
        c_sem = sem("consts_loaded")
        m_sem = sem("mem_loaded")
        bit_sem = sem("bits_loaded")
        kt_sem = sem("distances_loaded")
        r_sem = sem("rows_loaded")
        w_sem = sem("wout_loaded")
        xr_sem = sem("xres_loaded")
        ln_sem = sem("lnrows_loaded")
        st_sem = sem("stored")

        def slot(name):
            return slots[:, load_at[name] % 4]

        def weights(pe, name):
            pe.wait_ge(loaded_sem[load_at[name] % 4], load_need[name])

        block = ctx.enter_context(nc.Block())

        @block.sync
        def _(sp):
            xv = x.rearrange("a (b p) c -> (a b) p c", p=P)
            ov = out.rearrange("a (b p) c -> (a b) p c", p=P)
            src = {"w_in": w_in.rearrange("a (k p) n -> p (a k) n", p=P),
                   "w_mem_kv": w_mem_kv.rearrange("a (k p) n -> p (a k) n", p=P)}
            sp.dma_start(cst[:, 0:C_KT], consts[:, 0:C_KT]).then_inc(c_sem, 16)
            for b in range(4):
                sp.dma_start(xnat[b], xv[b]).then_inc(x_sem[b], 16)

            def load(i):
                if i >= 4:
                    sp.wait_ge(*filled(last_use[loads[i - 4][0]]))
                for t, col, w, at in loads[i][1]:
                    sp.dma_start(slots[:, i % 4, :, at:at + w], src[t][:, :, col:col + w]).then_inc(loaded_sem[i % 4], 16)

            load(0)
            for b in range(4, NB):
                sp.wait_ge(*filled(("xT", 2 * (b - 4) + 1)))
                sp.dma_start(xnat[b - 4], xv[b]).then_inc(x_sem[b - 4], 16)
                if b == 4:
                    load(1)
            load(2)
            load(3)
            sp.dma_start(wuknat.rearrange("p (h d) -> p h d", h=SAH), w_uk.rearrange("a h r d -> r (a h) d")).then_inc(m_sem, 16)
            sp.dma_start(cwnat[0:48, :], conv_w.rearrange("a j (c p) -> (a j c) p", p=P)).then_inc(m_sem, 16)
            sp.dma_start(memnat, mem.rearrange("a (m p) c -> p (a m) c", p=P)).then_inc(m_sem, 16)
            sp.dma_start(wuv[:, :].rearrange("p (h d) -> p h d", h=SAH), w_uv.rearrange("a h r d -> r (a h) d")).then_inc(m_sem, 16)
            for dst, s in ((kvw, kv_norm_w), (nrmw, dn_norm_w), (alog, dn_a_log), (dtb, dn_dt_bias)):
                sp.dma_start(dst, s.broadcast_to([P, dst.shape[1]])).then_inc(r_sem, 16)
            sp.dma_start(cst[:, C_BIT:C_ALL], consts[:, C_BIT:C_ALL]).then_inc(bit_sem, 16)
            for i in range(4, len(loads)):
                load(i)
            sp.wait_ge(keys_counted, N_SEL * FLOAT_BITS)
            sp.dma_start(cst[:, C_KT:C_BIT], consts[:, C_KT:C_BIT]).then_inc(kt_sem, 16)
            if ("finals",) not in order:
                return
            sp.wait_ge(*filled(("z", NB - 1, 0)))
            sp.wait_ge(*filled(("z", NB - 1, 1)))
            sp.dma_start(wout, w_out.rearrange("a (k p) n -> p (a k) n", p=P)).then_inc(w_sem, 16)
            for part in range(3):
                sp.wait_ge(*filled(("tok", DNH - 1, 1, part)))
            sp.wait_ge(keys_selected, N_SEL)
            sp.dma_start(lng, ln_g.broadcast_to([P, DM])).then_inc(ln_sem, 16)
            sp.dma_start(lnb, ln_b.broadcast_to([P, DM])).then_inc(ln_sem, 16)
            for n, b in enumerate(BLOCK_ORDER):
                if n:
                    sp.wait_ge(*released(("y", BLOCK_ORDER[n - 1], 0)))
                    sp.wait_ge(*released(("y", BLOCK_ORDER[n - 1], 1)))
                sp.dma_start(xres, xv[b]).then_inc(xr_sem, 16)
                if n:
                    sp.wait_ge(row_finished, n)
                    sp.dma_start(ov[BLOCK_ORDER[n - 1]], yres).then_inc(st_sem, 16)
            sp.wait_ge(row_finished, NB)
            sp.dma_start(ov[BLOCK_ORDER[-1]], yres).then_inc(st_sem, 16)
            sp.wait_ge(st_sem, 16 * NB)

        @block.tensor
        def _(pe):
            def group(dst, pairs):
                for i, (w, r) in enumerate(pairs):
                    last = nc.tensor.matmul(dst, w, r, start=(i == 0), stop=(i == len(pairs) - 1))
                return last

            def tp(dst, src, n=P):
                return nc.tensor.transpose(dst, src, ident[0:n, 0:n])

            pe.wait_ge(c_sem, 16)
            for e in plan:
                k = e[0]
                if k == "xT":
                    b, half = e[1] // 2, e[1] % 2
                    if half == 0:
                        pe.wait_ge(x_sem[b % 4], 16 * (b // 4 + 1))
                    if not first(e):
                        pe.wait_ge(*vacated(e))
                    for i in range(4):
                        c = 4 * half + i
                        last = tp(ps(e)[:, i * P:(i + 1) * P], xnat[b % 4][:, c * P:(c + 1) * P])
                    last.then_inc(fill_of(e), 1)
                elif k == "kiT":
                    t = e[1]
                    if t == 0:
                        weights(pe, "ki")
                    pe.wait_ge(*released(("xT", (t + 1) * NB - 2)))
                    pe.wait_ge(*released(("xT", (t + 1) * NB - 1)))
                    if not first(e):
                        pe.wait_ge(*vacated(e))
                    group(ps(e)[:, :], [(slot("ki")[:, c, 0:P], xT[:, 4 * t:4 * t + 4, c, :]) for c in range(KT)]).then_inc(fill_of(e), 1)
                elif k == "small":
                    b = e[1]
                    if b == 0:
                        weights(pe, "small")
                    if not first(e):
                        pe.wait_ge(*vacated(e))
                    group(ps(e)[:, 0:144], [(xT[:, b, c, :], slot("small")[:, c, 0:144]) for c in range(KT)]).then_inc(fill_of(e), 1)
                elif k in ("qsT", "qmT"):
                    m, t, s = e[1:]
                    key = (k, m, t)
                    if s == 0:
                        if t == 0:
                            weights(pe, k[:2])
                        if not first(key):
                            pe.wait_ge(*vacated(key))
                    for c in (2 * s, 2 * s + 1):
                        last = nc.tensor.matmul(ps(key)[:, :], slot(k[:2])[:, c, m * P:(m + 1) * P], xT[:, 4 * t:4 * t + 4, c, :],
                                                start=(c == 0), stop=(c == KT - 1))
                    if s == 3:
                        last.then_inc(fill_of(key), 1)
                elif k == "qiT":
                    m, t = e[1], e[2]
                    name = f"qi{m // 2}"
                    if (m % 2, t) == (0, 0):
                        weights(pe, name)
                    if not first(e):
                        pe.wait_ge(*vacated(e))
                    mc = (m % 2) * P
                    group(ps(e)[:, :], [(slot(name)[:, c, mc:mc + P], xT[:, 4 * t:4 * t + 4, c, :]) for c in range(KT)]).then_inc(fill_of(e), 1)
                elif k == "idx":
                    b, j, c = e[1:]
                    if (j, c) == (0, 0):
                        if b == 2:
                            pe.wait_ge(*released(("kiT", 0)))
                            pe.wait_ge(*released(("kiT", 1)))
                            for m in range(4):
                                for t in range(2):
                                    pe.wait_ge(*released(("qiT", m, t)))
                    lo, hi = idx_chunks(b)[c]
                    if not first(e):
                        pe.wait_ge(*vacated(e))
                    qb = q2[:, j, b * P:(b + 1) * P]
                    group(ps(e)[:, 0:hi - lo], [(qb, khi[:, lo:hi]), (qb, klo[:, lo:hi])]).then_inc(fill_of(e), 1)
                elif k == "cwT":
                    pe.wait_ge(m_sem, 64)
                    if not first(e):
                        pe.wait_ge(*vacated(e))
                    tp(ps(e)[:, 0:48], cwnat[0:48, :], 48).then_inc(fill_of(e), 1)
                elif k == "wukT":
                    if not first(e):
                        pe.wait_ge(*vacated(e))
                    tp(ps(e)[:, 0:P], wuknat[:, 0:P])
                    tp(ps(e)[:, P:2 * P], wuknat[:, P:2 * P]).then_inc(fill_of(e), 1)
                elif k == "gate_sums":
                    if not first(e):
                        pe.wait_ge(*vacated(e))
                    pe.wait_ge(gate_steps_by_dve, 2)
                    nc.tensor.matmul(ps(e)[:, 0:32], tri, s_g, start=True, stop=True)
                    nc.tensor.matmul(ps(e)[:, 32:64], ones, s_g, start=True, stop=True).then_inc(fill_of(e), 1)
                elif k == "memT":
                    m, half = e[1] // 2, e[1] % 2
                    if not first(e):
                        pe.wait_ge(*vacated(e))
                    for i in range(4):
                        c = 4 * half + i
                        last = tp(ps(e)[:, i * P:(i + 1) * P], memnat[:, m, c * P:(c + 1) * P])
                    last.then_inc(fill_of(e), 1)
                elif k == "kmT":
                    weights(pe, "mk")
                    for i in range(4):
                        pe.wait_ge(*released(("memT", i)))
                    if not first(e):
                        pe.wait_ge(*vacated(e))
                    for m in range(2):
                        last = group(ps(e)[:, m * 256:(m + 1) * 256],
                                     [(slot("mk")[:, c, m * P:(m + 1) * P], memT[:, c, :]) for c in range(KT)])
                    last.then_inc(fill_of(e), 1)
                elif k == "vm":
                    weights(pe, "mv")
                    if not first(e):
                        pe.wait_ge(*vacated(e))
                    for m in range(2):
                        last = group(ps(e)[:, m * 256:(m + 1) * 256],
                                     [(memT[:, c, m * P:(m + 1) * P], slot("mv")[:, c, :]) for c in range(KT)])
                    last.then_inc(fill_of(e), 1)
                elif k == "cT":
                    pe.wait_ge(gate_steps_by_dve, 3)
                    if not first(e):
                        pe.wait_ge(*vacated(e))
                    for i in range(4):
                        last = tp(ps(e)[:, i * P:(i + 1) * P], sm[:, 4 * e[1] + i, 0:P])
                    last.then_inc(fill_of(e), 1)
                elif k == "proj":
                    h, part, t, s = e[1:]
                    key = ("proj", h, part, t)
                    name = f"v{h}" if part == 2 else f"kq{h}"
                    at = P if part == 0 else 0
                    if s == 0:
                        if t == 0:
                            weights(pe, name)
                        if not first(key):
                            pe.wait_ge(*vacated(key))
                    for c in (2 * s, 2 * s + 1):
                        last = nc.tensor.matmul(ps(key)[:, :], slot(name)[:, c, at:at + P], xT[:, 4 * t:4 * t + 4, c, :],
                                                start=(c == 0), stop=(c == KT - 1))
                    if s == 3:
                        last.then_inc(fill_of(key), 1)
                elif k == "z":
                    b, half, s = e[1:]
                    key = ("z", b, half)
                    if s == 0:
                        if b == 0:
                            weights(pe, f"z{2 * half}")
                            weights(pe, f"z{2 * half + 1}")
                        if not first(key):
                            pe.wait_ge(*vacated(key))
                    q = s // 2
                    for c in range(4 * (s % 2), 4 * (s % 2) + 4):
                        last = nc.tensor.matmul(ps(key)[:, q * 256:(q + 1) * 256], xT[:, b, c, :], slot(f"z{2 * half + q}")[:, c, :],
                                                start=(c == 0), stop=(c == KT - 1))
                    if s == 3:
                        last.then_inc(fill_of(key), 1)
                elif k == "ss":
                    h, part = e[1:]
                    key = ("ss", h)
                    pe.wait_ge(squares_ready, order[e])
                    if part == 1 and not first(key):
                        pe.wait_ge(*vacated(key))
                    at = 0 if part else NB
                    for b in range(NB):
                        last = nc.tensor.matmul(ps(key)[:, at + b:at + b + 1], hbuf[:, 3 + b * P:3 + (b + 1) * P], ones[:, 0:1],
                                                start=True, stop=True)
                    if part:
                        last.then_inc(k_squares_summed, 1)
                    else:
                        last.then_inc(fill_of(key), 1)
                elif k == "tok":
                    h, a, part = e[1:]
                    if (a, part) == (0, 1):
                        pe.wait_ge(silu_done, 3 * h + 3)
                    if not first(e):
                        pe.wait_ge(*vacated(e))
                    for i in range(4):
                        last = tp(ps(e)[:, i * P:(i + 1) * P], qkv[:, part, (4 * a + i) * P:(4 * a + i + 1) * P])
                    last.then_inc(fill_of(e), 1)
                elif k == "bT":
                    h, a, w = e[1:]
                    pe.wait_ge(*released(("tok", h, a, 1 if w < 2 else 0)))
                    if not first(e):
                        pe.wait_ge(*vacated(e))
                    src = row(a, (R_KHAT, R_KB, R_QHAT, R_QDEC)[w])
                    for i in range(4):
                        last = tp(ps(e)[:, i * P:(i + 1) * P], blk(src, i))
                    last.then_inc(fill_of(e), 1)
                elif k == "GB":
                    h, a = e[1:]
                    if not first(e):
                        pe.wait_ge(*vacated(e))
                    for i in range(4):
                        col = h * NB + 4 * a + i
                        last = nc.tensor.matmul(ps(e)[:, i * P:(i + 1) * P], s_g[:, col:col + 1].broadcast_to([P, P]), tri, start=True, stop=True)
                    last.then_inc(fill_of(e), 1)
                elif k in ("U", "At"):
                    h, a = e[1:]
                    pe.wait_ge(*released(("bT", h, a, 0)))
                    pe.wait_ge(*released(("bT", h, a, 1 if k == "U" else 2)))
                    if not first(e):
                        pe.wait_ge(*vacated(e))
                    other = row(a, R_KBT if k == "U" else R_QHATT)
                    for i in range(4):
                        last = nc.tensor.matmul(ps(e)[:, i * P:(i + 1) * P], blk(row(a, R_KHATT), i), blk(other, i), start=True, stop=True)
                    last.then_inc(fill_of(e), 1)
                elif k == "lv1":
                    h, a = e[1:]
                    pe.wait_ge(level_masked, ((h * NLEV) + 0) * 2 + a + 1)
                    if not first(e):
                        pe.wait_ge(*vacated(e))
                    for i in range(4):
                        last = tp(ps(e)[:, i * P:(i + 1) * P], blk(row(a, R_UO[0]), i))
                    last.then_inc(fill_of(e), 1)
                elif k == "M":
                    h, a, s = e[1:]
                    pe.wait_ge(level_masked, (h * NLEV + s) * 2 + a + 1)
                    if s == 1:
                        pe.wait_ge(*released(("lv1", h, a)))
                    else:
                        pe.wait_ge(*released(("XY", h, a, s - 1)))
                    if not first(e):
                        pe.wait_ge(*vacated(e))
                    for i in range(4):
                        last = nc.tensor.matmul(ps(e)[:, i * P:(i + 1) * P], blk(row(a, R_UO[s % 2]), i), blk(row(a, R_X), i), start=True, stop=True)
                    last.then_inc(fill_of(e), 1)
                elif k == "XY":
                    h, a, s = e[1:]
                    pe.wait_ge(*released(("M", h, a, s)))
                    pe.wait_ge(y_started, 2 * h + a + 1)
                    if not first(e):
                        pe.wait_ge(*vacated(e))
                    w = 1 << s
                    for i in range(4):
                        m1 = blk(row(a, R_M1), i)
                        if s < NLEV - 1:
                            last = nc.tensor.matmul(ps(e)[:, i * 64:(i + 1) * 64], blk(row(a, R_Y), i),
                                                    m1.rearrange("p (n t) -> p n t", t=2 * w)[:, :, 0:w], start=True, stop=True)
                        last = nc.tensor.matmul(ps(e)[:, 256 + i * 64:256 + (i + 1) * 64], m1,
                                                blk(row(a, R_Y), i).rearrange("p (n t) -> p n t", t=2 * w)[:, :, w:2 * w], start=True, stop=True)
                    last.then_inc(fill_of(e), 1)
                elif k == "nw":
                    h, a = e[1:]
                    pe.wait_ge(*released(("XY", h, a, NLEV - 1)))
                    pe.wait_ge(keys_decayed, 2 * h + a + 1)
                    if not first(e):
                        pe.wait_ge(*vacated(e))
                    for i in range(4):
                        last = nc.tensor.matmul(ps(e)[:, i * P:(i + 1) * P], blk(row(a, R_KBG), i), blk(row(a, R_Y), i), start=True, stop=True)
                    last.then_inc(fill_of(e), 1)
                elif k == "scanV":
                    h, b = e[1:]
                    a, i = b // 4, b % 4
                    key = ("V", h, b)
                    if i == 0:
                        pe.wait_ge(*released(("nw", h, a)))
                    if not first(key):
                        pe.wait_ge(*vacated(key))
                    last = nc.tensor.matmul(ps(key)[:, 0:P], blk(row(a, R_Y), i), blk(row(a, R_VB), i), start=True, stop=(b == 0))
                    if b:
                        pe.wait_ge(*released(("S", h, b - 1)))
                        last = nc.tensor.matmul(ps(key)[:, 0:P], blk(row(a, R_NW), i), dn_s[:, (b % 2) * P:(b % 2 + 1) * P], start=False, stop=True)
                    last.then_inc(fill_of(key), 1)
                elif k == "scanS":
                    h, b = e[1:]
                    a, i = b // 4, b % 4
                    vn = vnew[:, (b % 2) * P:(b % 2 + 1) * P]
                    pe.wait_ge(*released(("V", h, b)))
                    ko, ks = ("O", h, b), ("S", h, b)
                    if b < NB - 1:
                        if not first(ks):
                            pe.wait_ge(*vacated(ks))
                        nc.tensor.matmul(ps(ks)[:, 0:P], blk(row(a, R_KD), i), vn, start=True, stop=True).then_inc(fill_of(ks), 1)
                    if not first(ko):
                        pe.wait_ge(*vacated(ko))
                    if b:
                        nc.tensor.matmul(ps(ko)[:, 0:P], blk(row(a, R_QDECT), i), dn_s[:, (b % 2) * P:(b % 2 + 1) * P], start=True, stop=False)
                    nc.tensor.matmul(ps(ko)[:, 0:P], blk(row(a, R_ATT), i), vn, start=(b == 0), stop=True).then_inc(fill_of(ko), 1)
                elif k == "qabs":
                    b = e[1]
                    if PLACE[b] == 0:
                        for m in range(2):
                            for t in range(2):
                                pe.wait_ge(*released(("qsT", m, t)))
                    for odd in range(2):
                        key = ("qabs", b, odd)
                        p0 = 64 * odd
                        if not first(key):
                            pe.wait_ge(*vacated(key))
                        for m in range(2):
                            last = nc.tensor.matmul(ps(key)[:, m * P:(m + 1) * P], wukT[p0:p0 + 64, m * P:(m + 1) * P],
                                                    qsTv[p0:p0 + 64, m, b * P:(b + 1) * P], start=True, stop=True)
                        last.then_inc(fill_of(key), 1)
                elif k == "sc":
                    b, h, c = e[1:]
                    if (h, c) == (0, 0):
                        pe.wait_ge(*released(("qabs", b, 0)))
                        pe.wait_ge(*released(("qabs", b, 1)))
                    lo, hi = idx_chunks(b)[c]
                    if not first(e):
                        pe.wait_ge(*vacated(e))
                    nc.tensor.matmul(ps(e)[:, 0:hi - lo], qab[:, h * P:(h + 1) * P], cT[:, lo:hi], start=True, stop=True).then_inc(fill_of(e), 1)
                elif k == "msc":
                    b, i = e[1:]
                    if not first(e):
                        pe.wait_ge(*vacated(e))
                    p0 = 64 * i
                    for m in range(2):
                        last = nc.tensor.matmul(ps(e)[:, m * 256:(m + 1) * 256], qmTv[p0:p0 + 64, m, b * P:(b + 1) * P],
                                                kmT[p0:p0 + 64, m * 256:(m + 1) * 256], start=True, stop=True)
                    last.then_inc(fill_of(e), 1)
                elif k == "pT":
                    b, kt = e[1:]
                    if kt == 0:
                        pe.wait_ge(exps_ready, SAH * (PLACE[b] + 1))
                    if not first(e):
                        pe.wait_ge(*vacated(e))
                    for h in range(SAH):
                        last = tp(ps(e)[:, h * P:(h + 1) * P], xs_of(b)[:, h, kt * P:(kt + 1) * P])
                    last.then_inc(fill_of(e), 1)
                elif k == "lat":
                    b, kt = e[1:]
                    key = ("lat", b)
                    if kt == 0:
                        if not first(key):
                            pe.wait_ge(*vacated(key))
                    pe.wait_ge(*released(("pT", b, kt)))
                    last = nc.tensor.matmul(ps(key)[:, :], sm[:, kt, 0:P], pTb[(order[e] - 1) % 3], start=(kt == 0), stop=(kt == b))
                    if kt == b:
                        last.then_inc(fill_of(key), 1)
                elif k == "mpT":
                    b, i = e[1:]
                    pe.wait_ge(*released(("msc", b, 0)))
                    pe.wait_ge(*released(("msc", b, 1)))
                    if not first(e):
                        pe.wait_ge(*vacated(e))
                    for h in range(4):
                        last = tp(ps(e)[:, h * P:(h + 1) * P], mp[:, h * 256 + i * P:h * 256 + (i + 1) * P])
                    last.then_inc(fill_of(e), 1)
                elif k == "o":
                    b = e[1]
                    pe.wait_ge(*released(("lat", b)))
                    if not first(e):
                        pe.wait_ge(*vacated(e))
                    for h in range(SAH):
                        nc.tensor.matmul(ps(e)[:, h * 64:(h + 1) * 64], latT[:, h * P:(h + 1) * P], wuv[:, h * 64:(h + 1) * 64], start=True, stop=True)
                    pe.wait_ge(*released(("mpT", b, 0)))
                    pe.wait_ge(*released(("mpT", b, 1)))
                    for h in range(4):
                        last = group(ps(e)[:, 256 + h * 64:256 + (h + 1) * 64],
                                     [(mpT[i][:, h * P:(h + 1) * P], vm[:, i * 256 + h * 64:i * 256 + (h + 1) * 64]) for i in range(2)])
                    last.then_inc(fill_of(e), 1)
                elif k == "mixT":
                    b, i = e[1:]
                    if i == 0:
                        pe.wait_ge(deltanet_gated, PLACE[b] + 1)
                    else:
                        pe.wait_ge(attention_gated, PLACE[b] + 1)
                    if not first(e):
                        pe.wait_ge(*vacated(e))
                    for c in range(4):
                        last = tp(ps(e)[:, c * P:(c + 1) * P], mix[:, (4 * i + c) * P:(4 * i + c + 1) * P])
                    last.then_inc(fill_of(e), 1)
                elif k == "y":
                    b, i = e[1:]
                    if (PLACE[b], i) == (0, 0):
                        pe.wait_ge(w_sem, 16)
                    if i == 0:
                        pe.wait_ge(*released(("mixT", b, 0)))
                        pe.wait_ge(*released(("mixT", b, 1)))
                    if not first(e):
                        pe.wait_ge(*vacated(e))
                    group(ps(e)[:, :], [(mixT[c // 4][:, (c % 4) * P:(c % 4 + 1) * P], wout[:, c, i * 512:(i + 1) * 512]) for c in range(KT)]).then_inc(fill_of(e), 1)

        @block.vector
        def _(dve):
            v = nc.vector
            dve_chain = ctx.enter_context(nc.semaphore("dve_chain"))
            steps = [0]

            def link(ins):
                steps[0] += 1
                ins.then_inc(dve_chain, 1)
                dve.wait_ge(dve_chain, steps[0])

            def bc(ap, n):
                return ap.unsqueeze(2).broadcast_to([P, ap.shape[1], n])

            def rep(ap, n):
                return ap.unsqueeze(1).broadcast_to([P, n, ap.shape[1]])

            def quad(ap):
                return ap.rearrange("p (b t) -> p b t", b=4)

            v.memset(hbuf[:, 0:3], 0.0)
            v.memset(eps_rms, RMS_EPS)
            v.memset(one1, 1.0)
            v.memset(candidate, 0.0)
            for b in range(2, NB):
                v.memset(n_half[:, b - 2:b - 1], (b + 1) * P - 2 * TOPK + 0.5)
            v.memset(eps_ln, LN_EPS).then_inc(small_constants_set, 1)
            for e in plan:
                k = e[0]
                if k == "xT" and e[1] % 2:
                    dve.wait_ge(*filled(e))
                    v.tensor_copy(xT[:, e[1] // 2, 4:8, :], quad(ps(e)[:, :])).then_inc(release_of(e), 1)
                elif k == "small":
                    dve.wait_ge(*filled(e))
                    v.tensor_copy(sm[:, e[1], :], ps(e)[:, 0:144]).then_inc(release_of(e), 1)
                elif k == "wis":
                    dve.wait_ge(*released(("small", NB - 1)))
                    dve.wait_ge(*released(("small", NB - 2)))
                    link(v.tensor_scalar(wis, sm[:, :, 136:144], IXH ** -0.5, None, ALU.mult))
                elif k == "kiT":
                    cols = slice(e[1] * 512, (e[1] + 1) * 512)
                    dve.wait_ge(key_hi_ready, order[e])
                    v.tensor_tensor(klo[:, cols], ps(e)[:, :], khi[:, cols].bitcast(F32), ALU.subtract).then_inc(release_of(e), 1)
                elif k == "qiT":
                    m, t = e[1:]
                    dve.wait_ge(query_hi_ready, order[e])
                    for odd in range(2):
                        hi = q2[0:64, 2 * m + odd, t * 512:(t + 1) * 512].bitcast(F32)
                        last = v.tensor_tensor(q2[64:128, 2 * m + odd, t * 512:(t + 1) * 512], ps(e)[64 * odd:64 * odd + 64, :], hi, ALU.subtract)
                    last.then_inc(release_of(e), 1)
                elif k in ("qsT", "qmT") and e[2:] == (1, 3):
                    key = e[:3]
                    dst = qsTv if k == "qsT" else qmTv
                    dve.wait_ge(*filled(key))
                    v.tensor_copy(dst[:, e[1], 512:1024], ps(key)[:, :]).then_inc(release_of(key), 1)
                elif k == "idx":
                    b, j, c = e[1:]
                    lo, hi = idx_chunks(b)[c]
                    r = rbuf[(order[e] - 1) % 3]
                    at = score_at(b)
                    w = wis[:, b, j:j + 1]
                    dve.wait_ge(*released(e))
                    if j == 0:
                        plain = hi - lo - (P if hi == (b + 1) * P else 0)
                        last = v.tensor_scalar(score[:, at + lo:at + lo + plain], r[:, 0:plain], w, None, ALU.mult)
                        if plain < hi - lo:
                            last = v.scalar_tensor_tensor(score[:, at + lo + plain:at + hi], r[:, plain:hi - lo], w,
                                                          cst[:, C_CAUS:C_CAUS + P], ALU.mult, ALU.add)
                    else:
                        dve.wait_ge(scores_summed, order[e] - 1)
                        last = v.scalar_tensor_tensor(score[:, at + lo:at + hi], r[:, 0:hi - lo], w,
                                                      score[:, at + lo:at + hi], ALU.mult, ALU.add)
                    last.then_inc(scores_summed, 1)
                elif k == "update":
                    it = e[1]
                    dve.wait_ge(keys_counted, N_SEL * (it + 1))
                    link(v.tensor_tensor(n_off, n_low, n_half, ALU.subtract))
                    if it == 0:
                        dve.wait_ge(bit_sem, 16)
                        link(v.tensor_scalar(t_sign, n_off, 0.0, 2.0, ALU.is_lt, ALU.mult))
                        link(v.tensor_scalar(t_sign, t_sign, -1.0, None, ALU.add))
                        v.memset(bits, 0.0)
                        v.tensor_scalar(candidate, t_sign, 2.0, None, ALU.mult).then_inc(candidates_ready, 1)
                    else:
                        bit = FLOAT_BITS - 1 - it
                        link(v.tensor_tensor(n_off, n_off, t_sign, ALU.mult))
                        link(v.tensor_scalar(bit_kept.bitcast(U32), n_off, 0.0, float(1 << bit), ALU.is_lt, ALU.mult))
                        if bit:
                            link(v.scalar_tensor_tensor(bits_tried.bitcast(U32), bit_kept.bitcast(U32), cst[:, C_BIT + bit - 1:C_BIT + bit].bitcast(U32),
                                                        bits.bitcast(U32), ALU.bitwise_or, ALU.bitwise_or))
                            v.tensor_tensor(candidate, bits_tried, t_sign, ALU.mult).then_inc(candidates_ready, 1)
                        link(v.tensor_tensor(bits.bitcast(U32), bits.bitcast(U32), bit_kept.bitcast(U32), ALU.bitwise_or))
                        if bit == 0:
                            low, carry, up = bit_kept.bitcast(U32), n_off.bitcast(U32), bits_tried.bitcast(U32)
                            link(v.tensor_scalar(carry, bits.bitcast(U32), 16, None, ALU.logical_shift_right))
                            link(v.tensor_scalar(up, carry, 16, None, ALU.logical_shift_left))
                            link(v.tensor_tensor(low, bits.bitcast(U32), up, ALU.bitwise_xor))
                            link(v.tensor_scalar(low, low, 1.0, None, ALU.add))
                            link(v.tensor_scalar(carry, low, 16, None, ALU.logical_shift_right))
                            link(v.tensor_scalar(carry, carry, 16, None, ALU.logical_shift_left))
                            link(v.tensor_tensor(low, low, carry, ALU.bitwise_xor))
                            link(v.tensor_tensor(up, up, carry, ALU.add))
                            link(v.tensor_tensor(up, up, low, ALU.bitwise_or))
                            link(v.tensor_tensor(bits, bits, t_sign, ALU.mult))
                            link(v.tensor_tensor(bits_tried, bits_tried, t_sign, ALU.mult))
                            v.tensor_tensor(t_high, bits, bits_tried, ALU.max)
                            link(v.tensor_tensor(t_low, bits, bits_tried, ALU.min))
                elif k == "reach":
                    b = e[1]
                    one = slice(b - 2, b - 1)
                    w = (b + 1) * P
                    link(v.tensor_scalar(picked_above[:, 0:w], score[:, score_at(b):score_at(b + 1)], t_high[:, one], 0.0, ALU.is_ge, ALU.add,
                                         accum_out=n_low[:, one]))
                elif k == "threshold":
                    link(v.tensor_scalar(n_off, n_low, TOPK - 0.5, None, ALU.is_ge))
                    link(v.tensor_scalar(bit_kept, n_off, 0.5, None, ALU.is_lt))
                    link(v.tensor_tensor(t_high, t_high, n_off, ALU.mult))
                    link(v.tensor_tensor(t_low, t_low, bit_kept, ALU.mult))
                    link(v.tensor_tensor(candidate, t_high, t_low, ALU.add))
                    link(v.tensor_scalar(n_off, candidate, TINY, None, ALU.is_ge))
                    link(v.scalar_tensor_tensor(n_off, candidate, -TINY, n_off, ALU.is_le, ALU.add))
                    link(v.tensor_tensor(candidate, candidate, n_off, ALU.mult))
                elif k == "cwT":
                    dve.wait_ge(*filled(e))
                    v.tensor_copy(cw[:, :], ps(e)[:, 0:48]).then_inc(release_of(e), 1)
                elif k == "wukT":
                    dve.wait_ge(*filled(e))
                    v.tensor_copy(wukT[:, :], ps(e)[:, 0:256]).then_inc(release_of(e), 1)
                elif k == "gates":
                    hb = "p (h b) -> p h b"
                    dve.wait_ge(r_sem, 64)
                    link(v.tensor_tensor(s_y.rearrange(hb, h=4), sm[:, :, 132:136].rearrange("p b h -> p h b"), bc(dtb, NB), ALU.add))
                    link(v.tensor_scalar(s_neg, s_y, -1.0, None, ALU.mult))
                    v.tensor_tensor(s_neg, s_neg, s_y, ALU.min).then_inc(gate_steps_by_dve, 1)
                    dve.wait_ge(gate_steps_by_act, 1)
                    link(v.tensor_scalar(s_beta, s_beta, 1.0, None, ALU.add))
                    v.reciprocal(s_beta, s_beta)
                    link(v.scalar_tensor_tensor(s_y, s_y, 0.0, s_neg, ALU.max, ALU.add))
                    v.scalar_tensor_tensor(s_g.rearrange(hb, h=4), s_y.rearrange(hb, h=4), -1.0, bc(ealog, NB), ALU.mult, ALU.mult).then_inc(gate_steps_by_dve, 1)
                    for b in range(NB):
                        last = v.scalar_tensor_tensor(sm[:, b, 0:P], sm[:, b, 0:P], crs[:, b:b + 1], kvw, ALU.mult, ALU.mult)
                    last.then_inc(gate_steps_by_dve, 1)
                elif k == "gate_sums":
                    dve.wait_ge(*filled(e))
                    v.tensor_copy(s_G, ps(e)[:, 0:32])
                    v.tensor_copy(s_Gt, ps(e)[:, 32:64]).then_inc(release_of(e), 1)
                    dve.wait_ge(*released(e))
                    v.tensor_scalar(s_nG, s_G, -1.0, None, ALU.mult)
                    v.tensor_tensor(s_dG, s_Gt, s_G, ALU.subtract).then_inc(gate_steps_by_dve, 1)
                elif k == "memT" and e[1] % 2:
                    dve.wait_ge(*filled(e))
                    v.tensor_copy(memT[:, 4:8, (e[1] // 2) * P:(e[1] // 2 + 1) * P], quad(ps(e)[:, :])).then_inc(release_of(e), 1)
                elif k == "cT" and e[1] == 1:
                    dve.wait_ge(*filled(e))
                    v.tensor_copy(cT[:, 512:1024], ps(e)[:, :]).then_inc(release_of(e), 1)
                elif k == "conv":
                    h, part, t = e[1:]
                    dve.wait_ge(*released(("proj", h, part, t)))
                    if h and t == 0:
                        dve.wait_ge(*filled(("tok", h - 1, 1, part)))
                    y = qkv[:, part, t * 512:(t + 1) * 512]
                    tap = [cw[:, j * 12 + part * 4 + h:j * 12 + part * 4 + h + 1] for j in range(4)]
                    shifted = [hbuf[:, j + t * 512:j + (t + 1) * 512] for j in range(4)]
                    link(v.tensor_scalar(y, shifted[3], tap[3], None, ALU.mult))
                    link(v.scalar_tensor_tensor(y, shifted[2], tap[2], y, ALU.mult, ALU.add))
                    link(v.scalar_tensor_tensor(y, shifted[1], tap[1], y, ALU.mult, ALU.add))
                    v.scalar_tensor_tensor(y, shifted[0], tap[0], y, ALU.mult, ALU.add).then_inc(conv_done, 1)
                elif k == "norms":
                    h = e[1]
                    dve.wait_ge(inverse_norms_ready, h + 1)
                    dve.wait_ge(gate_steps_by_act, 2)
                    hh = slice(h * NB, (h + 1) * NB)
                    v.tensor_tensor(sc_of["kb"], rs_k, s_beta[:, hh], ALU.mult)
                    link(v.tensor_scalar(sc_of["q"], rs_q, DND ** -0.5, None, ALU.mult))
                    link(v.tensor_tensor(sc_of["qd"], sc_of["q"], s_eG[:, hh], ALU.mult))
                elif k == "tok":
                    h, a, part = e[1:]
                    if (h, a, part) == (0, 0, 1):
                        dve.wait_ge(scores_summed, seen["idx"])
                    dve.wait_ge(*filled(e))
                    src = quad(ps(e)[:, :])
                    qs_ = slice(4 * a, 4 * a + 4)
                    what = {1: ((R_KHAT, rs_k), (R_KB, sc_of["kb"])),
                            0: ((R_QHAT, sc_of["q"]), (R_QDEC, sc_of["qd"])),
                            2: ((R_VB, s_beta[:, h * NB:(h + 1) * NB]),)}[part]
                    for r, s in what:
                        last = v.tensor_tensor(quad(row(a, r)), src, bc(s[:, qs_], P), ALU.mult)
                    last.then_inc(release_of(e), 1)
                elif k == "GB":
                    h, a = e[1:]
                    dve.wait_ge(*filled(e))
                    v.tensor_tensor(quad(row(a, R_DARG)), quad(ps(e)[:, :]), rep(cst[:, C_NEG:C_NEG + P], 4), ALU.add).then_inc(release_of(e), 1)
                elif k in ("U", "At"):
                    h, a = e[1:]
                    dve.wait_ge(*filled(e))
                    dve.wait_ge(decays_ready, 2 * h + a + 1)
                    v.tensor_tensor(row(a, R_U if k == "U" else R_ATT), ps(e)[:, :], row(a, R_DEC), ALU.mult).then_inc(release_of(e), 1)
                elif k == "lv1":
                    h, a = e[1:]
                    dve.wait_ge(*filled(e))
                    v.tensor_tensor(quad(row(a, R_X)), rep(ident, 4), quad(ps(e)[:, :]), ALU.subtract).then_inc(release_of(e), 1)
                elif k == "XY":
                    h, a, s = e[1:]
                    w = 1 << s
                    dve.wait_ge(*filled(e))
                    halves = "p (n t) -> p n t"
                    if s < NLEV - 1:
                        xh = row(a, R_X).rearrange(halves, t=2 * w)[:, :, 0:w]
                        v.tensor_tensor(xh, xh, ps(e)[:, 0:256].rearrange(halves, t=w), ALU.subtract)
                    yh = row(a, R_Y).rearrange(halves, t=2 * w)[:, :, w:2 * w]
                    v.tensor_tensor(yh, yh, ps(e)[:, 256:512].rearrange(halves, t=w), ALU.subtract).then_inc(release_of(e), 1)
                elif k == "scanV":
                    h, b = e[1:]
                    key = ("V", h, b)
                    dve.wait_ge(*filled(key))
                    v.tensor_copy(vnew[:, (b % 2) * P:(b % 2 + 1) * P], ps(key)[:, 0:P]).then_inc(release_of(key), 1)
                elif k == "scanS" and e[2] < NB - 1:
                    h, b = e[1:]
                    key = ("S", h, b)
                    dve.wait_ge(*filled(key))
                    new = dn_s[:, ((b + 1) % 2) * P:((b + 1) % 2 + 1) * P]
                    if b == 0:
                        last = v.tensor_copy(new, ps(key)[:, 0:P])
                    else:
                        last = v.scalar_tensor_tensor(new, dn_s[:, (b % 2) * P:(b % 2 + 1) * P], s_gl[:, h * NB + b:h * NB + b + 1],
                                                      ps(key)[:, 0:P], ALU.mult, ALU.add)
                    last.then_inc(release_of(key), 1)
                elif k == "finals":
                    dve.wait_ge(kt_sem, 16)
                    v.tensor_tensor(dm01[:, 0:P], cst[:, C_KT + 7 * P:C_KT + 8 * P], cst[:, C_CAUS:C_CAUS + P], ALU.add)
                    v.tensor_copy(dm01[:, P:2 * P], cst[:, C_KT + 6 * P:C_KT + 7 * P])
                    link(v.tensor_tensor(dm01[:, 2 * P:3 * P], cst[:, C_KT + 7 * P:C_KT + 8 * P], cst[:, C_CAUS:C_CAUS + P], ALU.add))
                elif k == "dm":
                    b = e[1]
                    w = (b + 1) * P
                    one = slice(b - 2, b - 1)
                    d = score[:, score_at(b):score_at(b + 1)]
                    above, ties, rank = picked_above[:, 0:w], picked_ties[:, 0:w], tie_rank[:, 0:w]
                    link(v.tensor_scalar(above, d, candidate[:, one], 0.0, ALU.is_gt, ALU.add, accum_out=n_low[:, one]))
                    link(v.tensor_scalar(ties, d, candidate[:, one], None, ALU.is_equal))
                    v.tensor_scalar(n_off[:, one], n_low[:, one], -1.0, TOPK + 0.5, ALU.mult, ALU.add)
                    link(v.tensor_tensor_scan(rank, ties, ties, 0.0, ALU.add, ALU.max))
                    link(v.scalar_tensor_tensor(ties, rank, n_off[:, one], ties, ALU.is_le, ALU.mult))
                    link(v.scalar_tensor_tensor(ties, above, -1.0, ties, ALU.add, ALU.add))
                    dve.wait_ge(kt_sem, 16)
                    kt0 = C_KT + (7 - b) * P
                    v.scalar_tensor_tensor(d, ties, BIG, cst[:, kt0:kt0 + w], ALU.mult, ALU.add).then_inc(keys_selected, 1)
                elif k == "sc":
                    b, h, c = e[1:]
                    lo, hi = idx_chunks(b)[c]
                    d = dm01[:, b * P:(2 * b + 1) * P] if b < 2 else score[:, score_at(b):score_at(b + 1)]
                    if (b, h, c) == (BLOCK_ORDER[0], 0, 0):
                        dve.wait_ge(keys_selected, N_SEL)
                    dve.wait_ge(*filled(e))
                    v.tensor_tensor_reduce(xs_of(b)[:, h, lo:hi], d[:, lo:hi], ps(e)[:, 0:hi - lo], 1.0, -3.0e38, ALU.add, ALU.max,
                                                   mxp[:, 2 * h + c:2 * h + c + 1]).then_inc(release_of(e), 1)
                    if c == len(idx_chunks(b)) - 1:
                        dve.wait_ge(*released(e))
                        if c:
                            link(v.tensor_tensor(mxp[:, 2 * h:2 * h + 1], mxp[:, 2 * h:2 * h + 1], mxp[:, 2 * h + 1:2 * h + 2], ALU.max))
                        v.tensor_scalar(nmx[:, h:h + 1], mxp[:, 2 * h:2 * h + 1], -SLOPES[h], None, ALU.mult).then_inc(head_max_ready, 1)
                elif k == "msc":
                    b, i = e[1:]
                    dve.wait_ge(*filled(e))
                    link(v.tensor_reduce(mmx[:, 2 * i:2 * i + 2], ps(e)[:, :].rearrange("p (h n) -> p h n", h=2), AX, ALU.max))
                    v.tensor_scalar(mmx[:, 2 * i:2 * i + 2], mmx[:, 2 * i:2 * i + 2], -0.125, None, ALU.mult).then_inc(mem_max_ready, 1)
                elif k == "pT" and e[2] % 2:
                    dve.wait_ge(*filled(e))
                    v.tensor_copy(pTb[(order[e] - 1) % 3], ps(e)[:, :]).then_inc(release_of(e), 1)
                elif k == "mpT" and e[2] == 1:
                    dve.wait_ge(*filled(e))
                    v.tensor_copy(mpT[1], ps(e)[:, :]).then_inc(release_of(e), 1)
                elif k == "rinv":
                    b = e[1]
                    dve.wait_ge(exps_ready, SAH * (PLACE[b] + 1))
                    dve.wait_ge(*released(("msc", b, 0)))
                    dve.wait_ge(*released(("msc", b, 1)))
                    link(v.reciprocal(rinv, sums))
                elif k == "o":
                    b = e[1]
                    dve.wait_ge(*filled(e))
                    h8 = "p (h d) -> p h d"
                    v.tensor_tensor(otmp.rearrange(h8, h=8), ps(e)[:, :].rearrange(h8, h=8), bc(rinv, 64), ALU.mult).then_inc(release_of(e), 1)
                    dve.wait_ge(*released(e))
                    dve.wait_ge(*released(("z", b, 1)))
                    v.tensor_tensor(mix[:, 512:1024], otmp, zg[:, b, 512:1024], ALU.mult).then_inc(attention_gated, 1)
                elif k == "mixT" and e[2] == 1:
                    dve.wait_ge(*filled(e))
                    v.tensor_copy(mixT[1], ps(e)[:, :]).then_inc(release_of(e), 1)
                elif k == "y":
                    b, i = e[1:]
                    if i == 0:
                        dve.wait_ge(xr_sem, 16 * (PLACE[b] + 1))
                        if PLACE[b]:
                            dve.wait_ge(st_sem, 16 * PLACE[b])
                    dve.wait_ge(*filled(e))
                    yh = yres[:, i * 512:(i + 1) * 512]
                    v.scalar_tensor_tensor(yh, xres[:, i * 512:(i + 1) * 512], ALPHA, ps(e)[:, :], ALU.mult, ALU.add).then_inc(release_of(e), 1)
                    dve.wait_ge(*released(e))
                    link(v.bn_stats(bst[:, 6 * i:6 * i + 6], yh))
                    if i == 1:
                        v.bn_aggr(mv, bst).then_inc(ln_stats_ready, 1)
                elif k == "ln":
                    b = e[1]
                    dve.wait_ge(ln_rstd_ready, PLACE[b] + 1)
                    v.tensor_scalar(yres, yres, mv[:, 0:1], rstd, ALU.subtract, ALU.mult).then_inc(ln_scaled, 1)

        @block.scalar
        def _(act):
            sc = nc.scalar
            act_chain = ctx.enter_context(nc.semaphore("act_chain"))
            steps = [0]

            def link(ins):
                steps[0] += 1
                ins.then_inc(act_chain, 1)
                act.wait_ge(act_chain, steps[0])

            def copy(dst, src, scale=1.0):
                return sc.activation(dst, src, ACT.Copy, scale=scale)

            act.wait_ge(small_constants_set, 1)
            for e in plan:
                k = e[0]
                if k == "xT" and e[1] % 2 == 0:
                    act.wait_ge(*filled(e))
                    copy(xT[:, e[1] // 2, 0:4, :], ps(e)[:, :].rearrange("p (k t) -> p k t", k=4)).then_inc(release_of(e), 1)
                elif k == "kiT":
                    act.wait_ge(*filled(e))
                    copy(khi[:, e[1] * 512:(e[1] + 1) * 512], ps(e)[:, :]).then_inc(key_hi_ready, 1)
                elif k == "qiT":
                    m, t = e[1:]
                    act.wait_ge(*filled(e))
                    for odd in range(2):
                        last = copy(q2[0:64, 2 * m + odd, t * 512:(t + 1) * 512], ps(e)[64 * odd:64 * odd + 64, :])
                    last.then_inc(query_hi_ready, 1)
                elif k in ("qsT", "qmT") and e[2:] == (0, 3):
                    key = e[:3]
                    dst = qsTv if k == "qsT" else qmTv
                    act.wait_ge(*filled(key))
                    copy(dst[:, e[1], 0:512], ps(key)[:, :]).then_inc(release_of(key), 1)
                elif k == "idx":
                    b, j, c = e[1:]
                    lo, hi = idx_chunks(b)[c]
                    act.wait_ge(*filled(e))
                    if order[e] > 3:
                        act.wait_ge(scores_summed, order[e] - 3)
                    sc.activation(rbuf[(order[e] - 1) % 3][:, 0:hi - lo], ps(e)[:, 0:hi - lo], ACT.Relu, scale=IXD ** -0.5).then_inc(release_of(e), 1)
                elif k == "count":
                    it, b = e[1:]
                    w = (b + 1) * P
                    if it == 0:
                        act.wait_ge(scores_summed, order["idx", b, IXH - 1, len(idx_chunks(b)) - 1])
                    else:
                        act.wait_ge(candidates_ready, it)
                    if order[e] > 2:
                        act.wait_ge(keys_counted, order[e] - 2)
                    sc.activation(signs[order[e] % 2][:, 0:w], score[:, score_at(b):score_at(b + 1)], ACT.Sign, scale=-1.0,
                                  bias=candidate[:, b - 2:b - 1], accum_out=n_low[:, b - 2:b - 1]).then_inc(keys_counted, 1)
                elif k == "gates":
                    act.wait_ge(gate_steps_by_dve, 1)
                    for b in range(NB):
                        link(sc.activation(junk[:, :], sm[:, b, 0:P], ACT.Square, accum_out=css[:, b:b + 1]))
                    sc.activation(s_beta.rearrange("p (h b) -> p h b", h=4), sm[:, :, 128:132].rearrange("p b h -> p h b"), ACT.Exp, scale=-1.0)
                    act.wait_ge(r_sem, 64)
                    sc.activation(ealog, alog, ACT.Exp)
                    link(sc.activation(s_neg, s_neg, ACT.Exp))
                    sc.activation(s_neg, s_neg, ACT.Ln, bias=one1)
                    link(sc.activation(crs, css, ACT.Ln, bias=eps_rms, scale=1.0 / RANK))
                    sc.activation(crs, crs, ACT.Exp, scale=-0.5).then_inc(gate_steps_by_act, 1)
                elif k == "gate_sums":
                    act.wait_ge(gate_steps_by_dve, 4)
                    sc.activation(s_eG, s_G, ACT.Exp)
                    sc.activation(s_eD, s_dG, ACT.Exp)
                    sc.activation(s_gl, s_Gt, ACT.Exp).then_inc(gate_steps_by_act, 1)
                elif k == "memT" and e[1] % 2 == 0:
                    act.wait_ge(*filled(e))
                    copy(memT[:, 0:4, (e[1] // 2) * P:(e[1] // 2 + 1) * P], ps(e)[:, :].rearrange("p (k t) -> p k t", k=4)).then_inc(release_of(e), 1)
                elif k == "kmT":
                    act.wait_ge(*filled(e))
                    copy(kmT[:, :], ps(e)[:, :]).then_inc(release_of(e), 1)
                elif k == "vm":
                    act.wait_ge(*filled(e))
                    copy(vm[:, :], ps(e)[:, :]).then_inc(release_of(e), 1)
                elif k == "cT" and e[1] == 0:
                    act.wait_ge(*filled(e))
                    copy(cT[:, 0:512], ps(e)[:, :]).then_inc(release_of(e), 1)
                elif k == "proj" and e[4] == 3:
                    h, part, t = e[1:4]
                    key = ("proj", h, part, t)
                    n = h * 3 + (1, 0, 2).index(part)
                    act.wait_ge(*filled(key))
                    if n and t == 0:
                        act.wait_ge(conv_done, 2 * n)
                        if part == 0:
                            act.wait_ge(k_squares_summed, h + 1)
                        if part == 2:
                            act.wait_ge(*filled(("ss", h)))
                    copy(hbuf[:, 3 + t * 512:3 + (t + 1) * 512], ps(key)[:, :]).then_inc(release_of(key), 1)
                elif k == "silu":
                    h, part = e[1:]
                    n = h * 3 + (1, 0, 2).index(part)
                    act.wait_ge(conv_done, 2 * n + 2)
                    sc.activation(qkv[:, part, :], qkv[:, part, :], ACT.Silu).then_inc(silu_done, 1)
                    if part < 2:
                        act.wait_ge(silu_done, n + 1)
                        sc.activation(hbuf[:, 3:3 + SEQ], qkv[:, part, :], ACT.Square).then_inc(squares_ready, 1)
                elif k == "norms":
                    h = e[1]
                    key = ("ss", h)
                    act.wait_ge(*filled(key))
                    if h:
                        act.wait_ge(*released(("tok", h - 1, 1, 1)))
                    rs = hsc[:, 16:32]
                    sc.activation(rs, ps(key)[:, 0:2 * NB], ACT.Ln, bias=eps_rms).then_inc(release_of(key), 1)
                    act.wait_ge(*released(key))
                    sc.activation(rs, rs, ACT.Exp, scale=-0.5).then_inc(inverse_norms_ready, 1)
                elif k == "bT":
                    h, a, w = e[1:]
                    act.wait_ge(*filled(e))
                    copy(row(a, (R_KHATT, R_KBT, R_QHATT, R_QDECT)[w]), ps(e)[:, :]).then_inc(release_of(e), 1)
                elif k == "GB":
                    h, a = e[1:]
                    act.wait_ge(*released(e))
                    for i in range(4):
                        col = h * NB + 4 * a + i
                        d = blk(row(a, R_DEC), i)
                        last = sc.activation(d, d, ACT.Exp, bias=s_nG[:, col:col + 1])
                    last.then_inc(decays_ready, 1)
                elif k == "M":
                    h, a, s = e[1:]
                    act.wait_ge(*filled(e))
                    copy(row(a, R_M1), ps(e)[:, :]).then_inc(release_of(e), 1)
                elif k == "nw":
                    h, a = e[1:]
                    act.wait_ge(*filled(e))
                    copy(row(a, R_NW), ps(e)[:, :], -1.0).then_inc(release_of(e), 1)
                elif k == "scanS":
                    h, b = e[1:]
                    key = ("O", h, b)
                    act.wait_ge(*filled(key))
                    copy(oall[:, b, h, :], ps(key)[:, 0:P])
                    if b or h:
                        act.wait_ge(*released(("O", h, b - 1) if b else ("O", h - 1, NB - 1)))
                    sc.activation(junk[:, :], ps(key)[:, 0:P], ACT.Square, accum_out=s_oss[:, b * 4 + h:b * 4 + h + 1]).then_inc(release_of(key), 1)
                elif k == "z" and e[2:] == (1, 3):
                    b = e[1]
                    act.wait_ge(*filled(("z", b, 0)))
                    act.wait_ge(*filled(("z", b, 1)))
                    sc.activation(zg[:, b, 0:512], ps(("z", b, 0))[:, :], ACT.Silu).then_inc(release_of(("z", b, 0)), 1)
                    sc.activation(zg[:, b, 512:1024], ps(("z", b, 1))[:, :], ACT.Silu).then_inc(release_of(("z", b, 1)), 1)
                elif k == "finals":
                    act.wait_ge(*released(("O", DNH - 1, NB - 1)))
                    link(sc.activation(s_orn, s_oss, ACT.Ln, bias=eps_rms, scale=1.0 / DND))
                    sc.activation(s_orn, s_orn, ACT.Exp, scale=-0.5).then_inc(output_norms_ready, 1)
                elif k == "qabs":
                    for odd in range(2):
                        key = (*e, odd)
                        act.wait_ge(*filled(key))
                        for m in range(2):
                            h = 2 * m + odd
                            last = copy(qab[:, h * P:(h + 1) * P], ps(key)[:, m * P:(m + 1) * P], SAD ** -0.5 / SLOPES[h])
                        last.then_inc(release_of(key), 1)
                elif k == "sc":
                    b, h, c = e[1:]
                    if c == len(idx_chunks(b)) - 1:
                        act.wait_ge(head_max_ready, SAH * PLACE[b] + h + 1)
                        p_ = xs_of(b)[:, h, :]
                        sc.activation(p_, p_, ACT.Exp, scale=SLOPES[h], bias=nmx[:, h:h + 1], accum_out=sums[:, h:h + 1]).then_inc(exps_ready, 1)
                elif k == "msc":
                    b, i = e[1:]
                    act.wait_ge(mem_max_ready, 2 * PLACE[b] + i + 1)
                    for m in range(2):
                        g = 2 * m + i
                        last = sc.activation(mp[:, g * 256:(g + 1) * 256], ps(e)[:, m * 256:(m + 1) * 256], ACT.Exp, scale=0.125,
                                             bias=mmx[:, 2 * i + m:2 * i + m + 1], accum_out=sums[:, 4 + g:5 + g])
                    last.then_inc(release_of(e), 1)
                elif k == "pT" and e[2] % 2 == 0:
                    act.wait_ge(*filled(e))
                    copy(pTb[(order[e] - 1) % 3], ps(e)[:, :]).then_inc(release_of(e), 1)
                elif k == "lat" and e[2] == e[1]:
                    key = ("lat", e[1])
                    act.wait_ge(*filled(key))
                    copy(latT, ps(key)[:, :]).then_inc(release_of(key), 1)
                elif k == "mpT" and e[2] == 0:
                    act.wait_ge(*filled(e))
                    copy(mpT[0], ps(e)[:, :]).then_inc(release_of(e), 1)
                elif k == "mixT" and e[2] == 0:
                    act.wait_ge(*filled(e))
                    copy(mixT[0], ps(e)[:, :]).then_inc(release_of(e), 1)
                elif k == "rstd":
                    b = e[1]
                    act.wait_ge(ln_stats_ready, PLACE[b] + 1)
                    link(sc.activation(rstd, mv[:, 1:2], ACT.Ln, bias=eps_ln))
                    sc.activation(rstd, rstd, ACT.Exp, scale=-0.5).then_inc(ln_rstd_ready, 1)

        @block.gpsimd
        def _(pool):
            g = nc.gpsimd
            pool_chain = ctx.enter_context(nc.semaphore("pool_chain"))
            steps = [0]

            def link(ins):
                steps[0] += 1
                ins.then_inc(pool_chain, 1)
                pool.wait_ge(pool_chain, steps[0])

            def rep(ap, n):
                return ap.unsqueeze(1).broadcast_to([P, n, ap.shape[1]])

            def quad(ap):
                return ap.rearrange("p (b t) -> p b t", b=4)

            def bc(ap, n):
                return ap.unsqueeze(2).broadcast_to([P, ap.shape[1], n])

            pool.wait_ge(c_sem, 16)
            for e in plan:
                k = e[0]
                if k == "tok" and e[3] == 1:
                    h, a = e[1:3]
                    cols = slice(h * NB + 4 * a, h * NB + 4 * a + 4)
                    pool.wait_ge(*released(e))
                    pool.wait_ge(gate_steps_by_act, 2)
                    g.tensor_tensor(quad(row(a, R_KBG)), quad(row(a, R_KB)), bc(s_eG[:, cols], P), ALU.mult)
                    g.tensor_tensor(quad(row(a, R_KD)), quad(row(a, R_KHAT)), bc(s_eD[:, cols], P), ALU.mult).then_inc(keys_decayed, 1)
                elif k in ("lv1", "M"):
                    h, a = e[1:3]
                    s = e[3] if k == "M" else 0
                    if s == 0:
                        pool.wait_ge(*released(("U", h, a)))
                        pool.wait_ge(keys_decayed, 2 * h + a + 1)
                    elif s == 2:
                        pool.wait_ge(*filled(("lv1", h, a)))
                        pool.wait_ge(y_started, 2 * h + a + 1)
                    elif s > 2:
                        pool.wait_ge(*filled(("M", h, a, s - 2)))
                    uo = row(a, R_UO[s % 2])
                    g.tensor_tensor(quad(uo), quad(row(a, R_U)), rep(cst[:, C_LEV + s * P:C_LEV + (s + 1) * P], 4),
                                    ALU.mult).then_inc(level_masked, 1)
                    if s == 0:
                        pool.wait_ge(*released(("At", h, a)))
                        pool.wait_ge(level_masked, (h * NLEV) * 2 + a + 1)
                        g.tensor_tensor(quad(row(a, R_Y)), rep(ident, 4), quad(uo), ALU.subtract).then_inc(y_started, 1)
                elif k == "deltanet_gate":
                    b = e[1]
                    pool.wait_ge(output_norms_ready, 1)
                    pool.wait_ge(*released(("z", b, 0)))
                    if PLACE[b]:
                        pool.wait_ge(*filled(("mixT", BLOCK_ORDER[PLACE[b] - 1], 0)))
                    m = mix[:, 0:512].rearrange("p (h d) -> p h d", h=4)
                    link(g.tensor_tensor(m, oall[:, b, :, :], s_orn[:, 4 * b:4 * b + 4].unsqueeze(2).broadcast_to([P, 4, P]), ALU.mult))
                    link(g.tensor_tensor(m, m, rep(nrmw, 4), ALU.mult))
                    g.tensor_tensor(mix[:, 0:512], mix[:, 0:512], zg[:, b, 0:512], ALU.mult).then_inc(deltanet_gated, 1)
                elif k == "ln":
                    b = e[1]
                    pool.wait_ge(ln_scaled, PLACE[b] + 1)
                    if PLACE[b] == 0:
                        pool.wait_ge(ln_sem, 32)
                    link(g.tensor_tensor(yres, yres, lng, ALU.mult))
                    g.tensor_tensor(yres, yres, lnb, ALU.add).then_inc(row_finished, 1)


_INS = ["x", "mem", "w_in", "conv_w", "dn_a_log", "dn_dt_bias", "dn_norm_w", "kv_norm_w", "w_uk", "w_uv", "w_mem_kv",
        "w_out", "ln_g", "ln_b"]


def kernel(**inputs):
    import numpy as _np
    import concourse.bacc as _bacc
    from concourse import mybir as _mybir
    from concourse.bass_utils import run_bass_kernel_spmd as _run

    nc = _bacc.Bacc("TRN2", target_bir_lowering=False, num_devices=1)
    arrays, args = {}, []
    for name in _INS:
        a = _np.ascontiguousarray(inputs[name])
        arrays[f"in_{name}"] = a
        args.append(nc.dram_tensor(f"in_{name}", a.shape, _mybir.dt.from_np(a.dtype), kind="ExternalInput").ap())
    consts = shape_constants()
    arrays["in_consts"] = consts
    args.append(nc.dram_tensor("in_consts", consts.shape, _mybir.dt.float32, kind="ExternalInput").ap())
    args.append(nc.dram_tensor("out_y", (1, SEQ, DM), _mybir.dt.float32, kind="ExternalOutput").ap())
    build(nc, *args)
    r = _run(nc, [arrays], core_ids=[0])
    return r.results[0]["out_y"]
```

```python
from contextlib import ExitStack

import numpy as np

import concourse.bass as bass
from concourse import mybir

P = 128
SEQ, DM = 1024, 1024
NB = SEQ // P
KT = DM // P
NMEM = 256
DNH, DND = 4, 128
SAH, SAD, RANK = 4, 64, 128
IXH, IXD = 8, 64
TOPK = 256
DNW = DNH * DND
OFF, acc_ = {}, 0
for name_, width_ in (("qa", DNW), ("ka", DNW), ("va", DNW), ("za", DNW), ("ba", DNH), ("aa", DNH), ("qs", 256),
                      ("ckv", RANK), ("zs", 256), ("qi", IXH * IXD), ("ki", IXD), ("wi", IXH), ("qm", 256), ("zm", 256)):
    OFF[name_] = acc_
    acc_ += width_
ALPHA = 2.0 ** 0.25
LN_EPS, RMS_EPS = 1e-5, 1e-6
SLOPES = [2.0 ** (-8.0 * (i + 1) / SAH) for i in range(SAH)]
BIG = 1.0e30
TINY = 2.0 ** -126
N_SEL = NB - 2
FLOAT_BITS = 32
COUNT_GROUPS = ((7, 2), (6, 3), (5, 4))
NLEV = 7
N_SIDE = 12
STAGED_MEM = ("wukT", "kmT", "vm")
N_SLOTS = 3
BLOCK_ORDER = (3, 4, 2, 5, 1, 6, 0, 7)
PLACE = {b: n for n, b in enumerate(BLOCK_ORDER)}
XS_W = SAH * (SEQ + P)
MIXT_AT = 10240
F32 = mybir.dt.float32
F32R = mybir.dt.float32r
BF16 = mybir.dt.bfloat16
U32 = mybir.dt.uint32
ALU = mybir.AluOpType
ACT = mybir.ActivationFunctionType
AX = mybir.AxisListType.X
C_ID, C_TRI, C_NEG, C_CAUS, C_ONE, C_LEV, C_KT = 0, 128, 256, 384, 512, 640, 640 + NLEV * 128
C_BIT = C_KT + SEQ
C_ALL = C_BIT + 32


def shape_constants():
    c = np.zeros((P, C_ALL), np.float32)
    p, f = np.arange(P)[:, None], np.arange(P)[None, :]
    c[:, C_ID:C_ID + P] = p == f
    c[:, C_TRI:C_TRI + P] = p <= f
    c[:, C_NEG:C_NEG + P] = np.where(p <= f, 0.0, -BIG)
    c[:, C_CAUS:C_CAUS + P] = np.where(f <= p, 0.0, -BIG)
    c[:, C_ONE:C_ONE + P] = 1.0
    for i in range(NLEV):
        s = 1 << i
        c[:, C_LEV + i * P:C_LEV + (i + 1) * P] = (p // (2 * s) == f // (2 * s)) & (p % (2 * s) < s) & (f % (2 * s) >= s)
    c[:, C_KT:C_BIT] = np.arange(SEQ)[None, :] - p - (SEQ - P)
    c[:, C_BIT:] = (1 << np.arange(32, dtype=np.uint32)).view(np.float32)
    return c


def idx_chunks(b):
    w = (b + 1) * P
    return [(0, w)] if w <= 512 else [(0, w // 2), (w // 2, w)]


def score_at(b):
    return sum((i + 1) * P for i in range(2, b))


SCORE_W = score_at(NB)


FILL = {"tok": 1.0, "bT": 1.25, "U": 1.0, "lv1": 1.0, "M": 1.25, "XY": 1.25, "scan": 1.0}
SELECT_RATE = 1.04


def make_plan():
    plan = []
    add = plan.append
    selection = [[*[("count", it, b) for b in group], *[("update", it)] * (group == COUNT_GROUPS[-1])]
                 for it in range(FLOAT_BITS) for group in COUNT_GROUPS]
    selection += [[("reach", 7), ("reach", 2)], [("reach", 6), ("reach", 3)], [("reach", 5), ("reach", 4), ("threshold",)]]
    selection += [[("dm", b, i), ("dm", b, i + 1)] for b in (3, 4, 2, 5, 6, 7) for i in (0, 2, 4)]

    def select(n=1):
        for _ in range(n):
            if selection:
                for e in selection.pop(0):
                    add(e)

    for i in range(NB):
        add(("xT", i))
    add(("split", "ki"))
    add(("split", "qi0"))
    add(("kiT", 0))
    for m in range(2):
        for i in range(2):
            add(("xT", NB + 2 * m + i))
        if m == 0:
            add(("split", "qi1"))
        add(("qiT", m, 0))
    for i in range(NB + 4, 2 * NB):
        add(("xT", i))
    add(("kiT", 1))
    add(("qiT", 0, 1))
    add(("split", "qi2"))
    add(("qiT", 1, 1))
    add(("split", "qi3"))
    add(("split", "small"))
    add(("qiT", 2, 0))
    add(("qiT", 2, 1))
    add(("split", "k0"))
    add(("qiT", 3, 0))
    add(("qiT", 3, 1))
    for b in range(NB):
        add(("small", b))
    add(("wis",))
    add(("cwT",))
    add(("wukT",))

    def part_of(h, part, second=(), fourth=()):
        units = [[("proj", h, part, t, s)] for t in range(2) for s in range(4)]
        units[1] = [*second, *units[1]]
        units[3] = [*fourth, *units[3], ("conv", h, part, 0)]
        units[7] = [*units[7], ("conv", h, part, 1)]
        return units

    def head(h, after_k=(), after_q=(), after_v=()):
        return [*part_of(h, 1), *after_k,
                *part_of(h, 0, [("silu", h, 1)], [("ss", h, 1)]), *after_q,
                *part_of(h, 2, [("silu", h, 0)], [("ss", h, 0)]), *after_v[:1],
                [("silu", h, 2), ("norms", h)], *after_v[1:]]

    side = [[("side", g, t, s)] for g in range(N_SIDE) for t in range(2) for s in range(4)]
    first_work = [*[[("memT", i)] for i in range(4)],
                  *head(0, [[("kmT",)], [("gates",)]], [[("vm",)], [("gate_sums",)]], side[0:8])]
    n_units = len(first_work)
    index_tiles = [("idx", b, j, c) for b in range(2, NB) for c in range(len(idx_chunks(b))) for j in range(IXH)]
    for i, e in enumerate(index_tiles):
        add(e)
        if (n_units - len(first_work)) * len(index_tiles) < n_units * (i + 1):
            for u in first_work.pop(0):
                add(u)
    for unit in first_work:
        for u in unit:
            add(u)
    work = [head(1, (), (), side[8:24]), head(2, (), (), side[24:40]), head(3, (), (), side[40:56]), side[56:]]
    owed, activations = [0.0], [0]
    fill_in_all = 2 * FILL["tok"] + 2 * FILL["bT"] + FILL["U"] + FILL["lv1"] + (NLEV - 1) * (FILL["M"] + FILL["XY"]) + NB * FILL["scan"]
    for h in range(DNH):
        todo = work[h]
        n_units, at = len(todo), [0]

        def fill(kind):
            at[0] += FILL[kind]
            while todo and n_units - len(todo) < n_units * at[0] / (fill_in_all - 2 * FILL["scan"] * (h == DNH - 1)):
                for e in todo.pop(0):
                    add(e)
                    activations[0] += e[0] in ("silu", "norms")
            owed[0] += SELECT_RATE
            if activations[0] == 0:
                n = min(2, int(owed[0]))
                select(n)
                owed[0] -= n
            activations[0] = 0

        for a in range(2):
            add(("tok", h, a, 1))
            add(("tok", h, a, 0))
            add(("tok", h, a, 2))
            fill("tok")
        add(("GB", h, 0))
        add(("GB", h, 1))
        for a in range(2):
            for w in range(4):
                add(("bT", h, a, w))
            fill("bT")
        for a in range(2):
            add(("U", h, a))
            add(("At", h, a))
        fill("U")
        for a in range(2):
            add(("lv1", h, a))
        fill("lv1")
        for s in range(1, NLEV):
            for a in range(2):
                add(("M", h, a, s))
            fill("M")
            for a in range(2):
                add(("XY", h, a, s))
            fill("XY")
        for a in range(2):
            add(("nw", h, a))
        for b in range(NB):
            add(("scanV", h, b))
            fill("scan")
            add(("scanS", h, b))
        assert not todo
    add(("finals",))

    def scores(b, h):
        return [("sc", b, h, c) for c in range(len(idx_chunks(b)))]

    def attention(b):
        units = [[("pT", b, k)] for k in range(b + 1)] + [[("mpT", b, i)] for i in range(2)]
        units[0].append(("rinv", b))
        for k in range(b + 1):
            units[k + 2].append(("lat", b, k))
        return units

    def output(b):
        return [[("mixT", b, 0), ("mixT", b, 1)], [("mix_split", b)], [], [("y", b, 0)]]

    def normalise(b):
        return [("rstd", b), ("ln", b)]

    def merged(*queues):
        placed = sorted(((i + off) / (len(q) + off), qi, i) for qi, (off, q) in enumerate(queues) for i in range(len(q)))
        return [queues[qi][1][i] for _, qi, i in placed]

    first = BLOCK_ORDER[0]
    select(999)
    for e in [("cT", 0), ("cT", 1), ("deltanet_scale", first), ("qabs", first), *[t for h in range(SAH) for t in scores(first, h)], ("msc", first, 0), ("msc", first, 1)]:
        add(e)
    for n, b in enumerate(BLOCK_ORDER):
        queues = [(0, attention(b))]
        if n:
            before = output(BLOCK_ORDER[n - 1])
            before[2].append(("deltanet_scale", b))
            queues.append((1, before))
        if n > 1:
            for e in normalise(BLOCK_ORDER[n - 2]):
                add(e)
        if n + 1 < NB:
            nb = BLOCK_ORDER[n + 1]
            queues.append((0.5, [[("qabs", nb)], scores(nb, 0), *[scores(nb, h) for h in range(1, SAH)]]))
        if n < 2:
            queues.append((2, [[("split", f"out{i}")] for i in range(4 * n, 4 * n + 4)]))
        for unit in merged(*queues):
            for e in unit:
                add(e)
        if n + 1 < NB:
            add(("msc", nb, 0))
            add(("msc", nb, 1))
        if n:
            add(("y", BLOCK_ORDER[n - 1], 1))
        add(("o", b))
    for e in [*normalise(BLOCK_ORDER[-2]), *sum(output(BLOCK_ORDER[-1]), []), ("y", BLOCK_ORDER[-1], 1), *normalise(BLOCK_ORDER[-1])]:
        add(e)
    return with_splits(plan)


def group_of(e):
    k = e[0]
    if k == "qiT":
        return f"qi{e[1]}"
    if k == "proj":
        return f"{'qkv'[e[2]]}{e[1]}"
    if k == "side":
        return f"side{e[1]}"
    return {"kiT": "ki", "kmT": "mk", "vm": "mv"}.get(k)


def group_order(plan):
    return list(dict.fromkeys(g for g in map(group_of, plan) if g))


def with_splits(plan):
    groups = group_order(plan)
    steps, seen, done = [], set(), {e[1] for e in plan if e[0] == "split"}
    for e in plan:
        g = group_of(e)
        if g and g not in seen:
            seen.add(g)
            for ahead in groups[len(seen):len(seen) + 1]:
                if ahead not in done and ahead not in ("mk", "mv"):
                    steps.append(("split", ahead))
                    done.add(ahead)
        steps.append(e)
    return steps


POOL_OF = {"xT": "P", "kiT": "P", "small": "P", "qiT": "P", "idx": "D", "cwT": "P", "wukT": "P", "gate_sums": "P",
           "memT": "P", "kmT": "P", "vm": "P", "cT": "P", "tok": "D", "GB": "D",
           "bT": "D", "U": "D", "At": "D", "lv1": "D", "M": "D", "XY": "D", "nw": "D", "sc": "L",
           "msc": "D", "mixT": "D", "y": "L", "pT": "D", "lat": "P", "mpT": "D", "o": "P"}


def tiles_of(e):
    k = e[0]
    if k == "proj":
        return [("P", ("proj", *e[1:4]))] if e[4] == 0 else []
    if k == "side":
        return [("L", e[:3])] if e[3] == 0 else []
    if k == "ss":
        return [("L", ("ss", e[1]))] if e[2] == 1 else []
    if k == "lat":
        return [("P", ("lat", e[1]))] if e[2] == 0 else []
    if k == "qabs":
        return [("D", (*e, 0)), ("D", (*e, 1))]
    if k == "scanV":
        return [("D", ("V", e[1], e[2]))]
    if k == "scanS":
        return [("D", ("S", e[1], e[2]))] * (e[2] < NB - 1) + [("D", ("O", e[1], e[2]))]
    return [(POOL_OF[k], e)] if k in POOL_OF else []


def weight_pieces(group):
    side = [OFF["qs"], OFF["qs"] + P, OFF["qm"], OFF["qm"] + P, *[OFF["za"] + i * P for i in range(4)],
            OFF["zs"], OFF["zs"] + P, OFF["zm"], OFF["zm"] + P]
    if group == "ki":
        return [("w_in", OFF["ki"], 64, 0), ("w_in", OFF["ki"], 64, 64)]
    if group == "small":
        return [("w_in", OFF["ckv"], P, 0), ("w_in", OFF["ba"], 8, P), ("w_in", OFF["wi"], 8, P + 8)]
    if group in ("mk", "mv"):
        return [("w_mem_kv", 256 * (group == "mv"), 256, 0)]
    if group[:2] == "qi":
        return [("w_in", OFF["qi"] + P * int(group[2:]), P, 0)]
    if group[:4] == "side":
        return [("w_in", side[int(group[4:])], P, 0)]
    return [("w_in", OFF[group[0] + "a"] + P * int(group[1:]), P, 0)]


def build(nc, x, mem, w_in, conv_w, dn_a_log, dn_dt_bias, dn_norm_w, kv_norm_w, w_uk, w_uv, w_mem_kv, w_out,
          ln_g, ln_b, consts, side_q, side_z, side_mem, out, plan=None):
    plan = plan or make_plan()
    ctx = ExitStack()
    with ctx:
        def sb(name, cols):
            return ctx.enter_context(nc.sbuf_tensor(name, [P, cols], F32))

        def sem(name):
            return ctx.enter_context(nc.semaphore(name))

        cst = sb("cst", C_ALL)
        base = nc.sbuf_base
        sb("ring_and_x", N_SLOTS * 2048 + 2 * NB * KT * P)

        def over(name, start, cols, dtype=F32):
            return nc.alloc_sbuf_tensor_at(name, [P, cols], dtype, offset=base + 4 * start)

        ring = over("ring", 0, N_SLOTS * 2048)
        ring_r = over("ring_split", 0, N_SLOTS * 2048, F32R)
        x_hi_ = over("x_hi", N_SLOTS * 2048, NB * KT * P, F32R)
        x_lo_ = over("x_lo", N_SLOTS * 2048 + NB * KT * P, NB * KT * P, F32R)
        wout_ = over("w_out_sb", 0, KT * DM)
        wout_lo_ = over("w_out_lo", 0, KT * DM, F32R)
        wout_hi_ = over("w_out_hi", KT * DM, KT * DM, F32R)
        zgT_ = over("zgT", 2 * KT * DM, 2 * KT * P)
        qsT = over("qsT", 2 * KT * (DM + P), 4 * P)
        qmT = over("qmT", 2 * KT * (DM + P) + 4 * P, 4 * P)
        cT = over("cT", 2 * KT * (DM + P) + 8 * P, SEQ)
        kmT = over("kmT", 2 * KT * (DM + P) + 8 * P + SEQ, 2 * NMEM)
        vm = over("vm", 2 * KT * (DM + P) + 8 * P + SEQ + 2 * NMEM, 2 * NMEM)
        mix_hi = over("mix_hi", 2 * KT * (DM + P) + 8 * P + SEQ + 4 * NMEM, DM, F32R)
        score = sb("score", SCORE_W)
        small = sb("small", NB * 144)
        small_w = nc.alloc_sbuf_tensor_at("small_w", [P, 2 * KT * 144], F32R, offset=nc.sbuf_base)
        qkvT = sb("qkvT", 3 * SEQ)
        hbuf = sb("hbuf", 3 + SEQ)
        stage = sb("stage", 512)
        at_ = nc.sbuf_base
        q2_ = nc.alloc_sbuf_tensor_at("q2", [P, IXH * SEQ], F32R, offset=at_)
        khi_ = nc.alloc_sbuf_tensor_at("khi", [P, SEQ], F32R, offset=at_ + 4 * IXH * SEQ)
        klo_ = nc.alloc_sbuf_tensor_at("klo", [P, SEQ], F32R, offset=at_ + 4 * (IXH + 1) * SEQ)
        oall_ = sb("oall", 4 * SEQ)
        mix_lo = nc.alloc_sbuf_tensor_at("mix_lo", [P, DM], F32R, offset=nc.sbuf_base + 4 * MIXT_AT)
        arena = sb("arena", 24 * 512)
        cw = sb("cw", 48)
        rows = sb("rows", 128 + 1 + 8)
        sc32 = sb("sc32", 14 * 32)
        hsc = sb("hsc", 16 + 16 + 6 * 8)
        dn_s = sb("dn_s", 2 * 128)
        vnew = sb("vnew", 2 * 128)
        wis_ = sb("wis", 64)
        misc = sb("misc", 64)
        sel = sb("sel", 10 * N_SEL)
        junk = sb("junk", 128)

        ident = cst[:, C_ID:C_ID + P]
        tri = cst[:, C_TRI:C_TRI + P]
        ones = cst[:, C_ONE:C_ONE + P]
        x_hi = x_hi_[:, :].rearrange("p (b k t) -> p b k t", b=NB, k=KT)
        x_lo = x_lo_[:, :].rearrange("p (b k t) -> p b k t", b=NB, k=KT)
        wout = wout_[:, :].rearrange("p (k n) -> p k n", k=KT)
        wout_lo = wout_lo_[:, :].rearrange("p (k n) -> p k n", k=KT)
        wout_hi = wout_hi_[:, :].rearrange("p (k n) -> p k n", k=KT)
        zgT = zgT_[:, :].rearrange("p (i c t) -> p i c t", i=2, c=KT)
        wukT, wuv = stage[:, 0:256], stage[:, 256:512]
        q2 = q2_[:, :].rearrange("p (j t) -> p j t", j=IXH)
        khi, klo = khi_[:, :], klo_[:, :]
        oall = oall_[:, :].rearrange("p (b h d) -> p b h d", b=NB, h=DNH)
        sm = small[:, :].rearrange("p (b c) -> p b c", b=NB)
        qmTv = qmT[:, :].rearrange("p (i m t) -> p i m t", i=2, m=2)
        qsTv = qsT[:, :].rearrange("p (i m t) -> p i m t", i=2, m=2)
        qkv = qkvT[:, :].rearrange("p (a t) -> p a t", a=3)
        wis = wis_[:, :].rearrange("p (b j) -> p b j", b=NB)
        kvw, nrmw = rows[:, 0:128], rows[:, 128:129]
        alog, dtb = rows[:, 129:133], rows[:, 133:137]
        rbuf = [arena[:, 6144 + i * 512:6656 + i * 512] for i in range(3)]
        memnat = arena[:, 7680:9728].rearrange("p (m c) -> p m c", m=2)
        memT = arena[:, 9728:11776].rearrange("p (k t) -> p k t", k=KT)
        wuknat = arena[:, 11776:12032]
        cwnat = arena[:, 12032:12160]
        xnat = [score[:, i * 1024:(i + 1) * 1024] for i in range(4)]

        def row(a, i):
            return arena[:, (12 * a + i) * 512:(12 * a + i + 1) * 512]

        def blk(ap, i):
            return ap[:, i * P:(i + 1) * P]

        R_KHAT, R_KB, R_QHAT, R_QDEC, R_KBG, R_KD, R_VB, R_KHATT, R_KBT, R_QHATT, R_QDECT, R_DEC = range(12)
        R_UO, R_M1, R_NW, R_X, R_U, R_ATT, R_Y, R_DARG = (0, 1), 2, 0, 7, 8, 9, 11, 11

        def av(at, n):
            return arena[:, at:at + n]

        def xs_of(b):
            at = 0 if PLACE[b] % 2 else XS_W - SAH * (b + 1) * P
            return av(at, SAH * (b + 1) * P).rearrange("p (h n) -> p h n", h=SAH)

        pTb = [av(XS_W + i * 512, 512) for i in range(3)]
        latT = av(6144, 512)
        qab = av(6656, 512)
        mp = av(7168, 1024)
        mpT = [av(8192 + i * 512, 512) for i in range(2)]
        mix = av(9216, 1024)
        mixT = [av(MIXT_AT + i * 512, 512) for i in range(2)]
        yres = av(11264, 1024)
        lng, lnb = qkvT[:, 0:1024], qkvT[:, 1024:2048]
        xres = qkvT[:, 2048:3072]
        picked_above, picked_ties, tie_rank = (qkvT[:, i * 1024:(i + 1) * 1024] for i in range(3))
        dm01 = hbuf[:, 0:384]
        (s_beta, s_y, s_neg, s_g, s_G, s_Gt, s_nG, s_dG, s_eG, s_eD, s_gl, s_oss, s_orn, s_tmp) = (
            sc32[:, i * 32:(i + 1) * 32] for i in range(14))
        css, crs = misc[:, 0:8], misc[:, 8:16]
        n_low, n_half, t_sign, n_off, bit_kept, bits, bits_tried, candidate, t_high, t_low = (
            sel[:, i * N_SEL:(i + 1) * N_SEL] for i in range(10))
        signs = [cst[:, C_KT + i * 512:C_KT + (i + 1) * 512].bitcast(BF16) for i in range(2)]
        eps_rms, eps_ln, one1 = misc[:, 16:17], misc[:, 17:18], misc[:, 18:19]
        mxp, nmx = misc[:, 20:28], misc[:, 28:32]
        sums, rinv = misc[:, 32:40], misc[:, 40:48]
        mmx = misc[:, 48:52]
        bst, mv, rstd, ealog = hsc[:, 0:12], hsc[:, 12:14], hsc[:, 14:15], misc[:, 52:56]
        rs_k, rs_q = hsc[:, 16:24], hsc[:, 24:32]
        sc_of = {n: hsc[:, 32 + 8 * i:40 + 8 * i] for i, n in enumerate(("kb", "q", "qd"))}

        pools = {"P": (0, 1), "L": (2, 3), "D": (4, 5, 6, 7)}
        banks = [ctx.enter_context(nc.psum_tensor(f"bank{i}", [P, 512], F32)) for i in range(8)]
        filled_sem = [sem(f"filled{i}") for i in range(8)]
        released_sem = [sem(f"released{i}") for i in range(8)]
        bank_of, use_of, count = {}, {}, {k: 0 for k in pools}
        for e in plan:
            for pool, key in tiles_of(e):
                n = count[pool]
                bank_of[key] = pools[pool][n % len(pools[pool])]
                use_of[key] = n // len(pools[pool]) + 1
                count[pool] += 1

        def ps(key):
            return banks[bank_of[key]]

        def vacated(key):
            return released_sem[bank_of[key]], use_of[key] - 1

        def first(key):
            return use_of[key] == 1

        def filled(key):
            return filled_sem[bank_of[key]], use_of[key]

        def released(key):
            return released_sem[bank_of[key]], use_of[key]

        def fill_of(key):
            return filled_sem[bank_of[key]]

        def release_of(key):
            return released_sem[bank_of[key]]

        small_constants_set = sem("small_constants_set")
        gate_steps_by_dve = sem("gate_steps_by_dve")
        key_hi_ready = sem("key_hi_ready")
        query_hi_ready = sem("query_hi_ready")
        scores_summed = sem("scores_summed")
        candidates_ready = sem("candidates_ready")
        keys_counted = sem("keys_counted")
        keys_selected = sem("keys_selected")
        conv_done = sem("conv_done")
        head_max_ready = sem("head_max_ready")
        mem_max_ready = sem("mem_max_ready")
        ln_stats_ready = sem("ln_stats_ready")
        ln_scaled = sem("ln_scaled")
        silu_done = sem("silu_done")
        squares_ready = sem("squares_ready")
        k_squares_summed = sem("k_squares_summed")
        inverse_norms_ready = sem("inverse_norms_ready")
        decays_ready = sem("decays_ready")
        exps_ready = sem("exps_ready")
        gate_steps_by_act = sem("gate_steps_by_act")
        output_norms_ready = sem("output_norms_ready")
        ln_rstd_ready = sem("ln_rstd_ready")
        ln_rstd_refined = sem("ln_rstd_refined")
        level_masked = sem("level_masked")
        x_hi_ready = sem("x_hi_ready")
        weights_hi_ready = sem("weights_hi_ready")
        weights_split = sem("weights_split")
        mix_hi_ready = sem("mix_hi_ready")
        mix_split = sem("mix_split")
        keys_decayed = sem("keys_decayed")
        y_started = sem("y_started")
        deltanet_scaled = sem("deltanet_scaled")
        row_finished = sem("row_finished")
        order = {}
        seen = {}
        for e in plan:
            seen[e[0]] = seen.get(e[0], 0) + 1
            order[e] = seen[e[0]]

        groups = group_order(plan)
        place_of = {g: i for i, g in enumerate(groups)}
        loaded_sem = [sem(f"loaded{i}") for i in range(N_SLOTS)]
        first_use, last_use = {}, {}
        for e in plan:
            if group_of(e):
                first_use.setdefault(group_of(e), e)
                last_use[group_of(e)] = e[:-1] if e[0] in ("proj", "side") else e
        opens = {first_use[g]: g for g in groups}
        load_need = {}
        total = [0] * N_SLOTS
        for i, g in enumerate(groups):
            total[i % N_SLOTS] += 16 * len(weight_pieces(g))
            load_need[g] = total[i % N_SLOTS]
        small_w_sem = sem("small_weights_loaded")
        side_stored = sem("side_results_stored")
        queries_back = [sem(f"queries_loaded{i}") for i in range(2)]
        side_mem_back = sem("memory_keys_loaded")
        gates_back = [sem(f"gates_loaded{i}") for i in range(2)]
        staged = [e for e in plan if e[0] in ("wukT", "kmT", "vm") or e[0] == "side" and e[3] == 3]
        staged_at = {e: i for i, e in enumerate(staged)}
        x_sem = [sem(f"x_loaded{i}") for i in range(4)]
        c_sem = sem("consts_loaded")
        m_sem = sem("mem_loaded")
        bit_sem = sem("bits_loaded")
        kt_sem = sem("distances_loaded")
        r_sem = sem("rows_loaded")
        w_sem = [sem(f"wout_loaded{i}") for i in range(2)]
        xr_sem = sem("xres_loaded")
        ln_sem = sem("lnrows_loaded")
        st_sem = sem("stored")

        def raw(name):
            at, n = 2048 * (place_of[name] % N_SLOTS), 256 if name in ("mk", "mv") else P
            return ring[:, at:at + KT * n].rearrange("p (k n) -> p k n", k=KT)

        def w_lo(name):
            if name == "small":
                return small_w[:, 0:KT * 144].rearrange("p (k n) -> p k n", k=KT)
            at = 2048 * (place_of[name] % N_SLOTS)
            return ring_r[:, at:at + 1024].rearrange("p (k n) -> p k n", k=KT)

        def w_hi(name):
            if name == "small":
                return small_w[:, KT * 144:2 * KT * 144].rearrange("p (k n) -> p k n", k=KT)
            at = 2048 * (place_of[name] % N_SLOTS) + 1024
            return ring_r[:, at:at + 1024].rearrange("p (k n) -> p k n", k=KT)

        def out_piece(view, name):
            j = int(name[3:])
            return view[:, 2 * (j % 4):2 * (j % 4) + 2, 512 * (j // 4):512 * (j // 4) + 512]

        small_raw = qkvT[:, 0:KT * 144].rearrange("p (k n) -> p k n", k=KT)

        block = ctx.enter_context(nc.Block())

        @block.sync
        def _(sp):
            xv = x.rearrange("a (b p) c -> (a b) p c", p=P)
            ov = out.rearrange("a (b p) c -> (a b) p c", p=P)
            src = {"w_in": w_in.rearrange("a (k p) n -> p (a k) n", p=P),
                   "w_mem_kv": w_mem_kv.rearrange("a (k p) n -> p (a k) n", p=P)}
            sp.dma_start(cst[:, 0:C_KT], consts[:, 0:C_KT]).then_inc(c_sem, 16)
            for b in range(4):
                sp.dma_start(xnat[b], xv[b]).then_inc(x_sem[b], 16)

            def load(i):
                g = groups[i]
                if i >= N_SLOTS:
                    sp.wait_ge(*filled(last_use[groups[i - N_SLOTS]]))
                for t, col, w, at in weight_pieces(g):
                    sp.dma_start(raw(g)[:, :, at:at + w], src[t][:, :, col:col + w]).then_inc(loaded_sem[i % N_SLOTS], 16)

            load(0)
            for b in range(4, NB):
                sp.wait_ge(*filled(("xT", 2 * (b - 4) + 1)))
                sp.dma_start(xnat[b - 4], xv[b]).then_inc(x_sem[b - 4], 16)
                if b == 4:
                    load(1)
            load(2)
            for t, col, w, at in weight_pieces("small"):
                sp.dma_start(small_raw[:, :, at:at + w], src[t][:, :, col:col + w]).then_inc(small_w_sem, 16)
            sp.dma_start(wuknat.rearrange("p (h d) -> p h d", h=SAH), w_uk.rearrange("a h r d -> r (a h) d")).then_inc(m_sem, 16)
            sp.dma_start(cwnat[0:48, :], conv_w.rearrange("a j (c p) -> (a j c) p", p=P)).then_inc(m_sem, 16)
            sp.dma_start(memnat, mem.rearrange("a (m p) c -> p (a m) c", p=P)).then_inc(m_sem, 16)
            sp.dma_start(nrmw, dn_norm_w.rearrange("a p -> p a")).then_inc(r_sem, 16)
            for dst, s in ((kvw, kv_norm_w), (alog, dn_a_log), (dtb, dn_dt_bias)):
                sp.dma_start(dst, s.broadcast_to([P, dst.shape[1]])).then_inc(r_sem, 16)
            sp.dma_start(cst[:, C_BIT:C_ALL], consts[:, C_BIT:C_ALL]).then_inc(bit_sem, 16)
            for e in plan:
                i = place_of.get(opens.get(e), 0)
                if i and i + 2 < len(groups):
                    load(i + 2)
                if e in staged_at:
                    key = e[:3] if e[0] == "side" else e
                    sp.wait_ge(*released(key))
                    if e[0] == "side":
                        to = side_q[e[1]] if e[1] < 4 else side_z[e[1] - 4]
                        sp.dma_start(to[:, e[2] * 512:(e[2] + 1) * 512], stage[:, :]).then_inc(side_stored, 16)
                    else:
                        i = STAGED_MEM.index(e[0])
                        n = (256, 512, 512)[i]
                        sp.dma_start(side_mem[i, :, 0:n], stage[:, 0:n]).then_inc(side_stored, 16)
                if e == ("reach", 7):
                    sp.wait_ge(keys_counted, N_SEL * FLOAT_BITS)
                    sp.dma_start(cst[:, C_KT:C_BIT], consts[:, C_KT:C_BIT]).then_inc(kt_sem, 16)
            sp.wait_ge(*filled(last_use[groups[-1]]))
            sp.wait_ge(side_stored, 16 * len(staged))
            def load_queries(n):
                cols = slice(BLOCK_ORDER[n] * P, (BLOCK_ORDER[n] + 1) * P)
                sp.dma_start(qsTv[:, n % 2], side_q[0:2, :, cols].rearrange("m p t -> p m t")).then_inc(queries_back[n % 2], 16)
                sp.dma_start(qmTv[:, n % 2], side_q[2:4, :, cols].rearrange("m p t -> p m t")).then_inc(queries_back[n % 2], 16)

            def load_gates(n):
                cols = slice(BLOCK_ORDER[n] * P, (BLOCK_ORDER[n] + 1) * P)
                sp.dma_start(zgT[:, n % 2], side_z[:, :, cols].rearrange("c p t -> p c t")).then_inc(gates_back[n % 2], 16)

            sp.dma_start(wukT, side_mem[0][:, 0:256]).then_inc(side_mem_back, 16)
            load_queries(0)
            sp.dma_start(wuv.rearrange("p (h d) -> p h d", h=SAH), w_uv.rearrange("a h r d -> r (a h) d")).then_inc(side_mem_back, 16)
            sp.dma_start(kmT[:, :], side_mem[1]).then_inc(side_mem_back, 16)
            sp.dma_start(vm[:, :], side_mem[2]).then_inc(side_mem_back, 16)
            load_queries(1)
            for i in range(2):
                half = slice(i * 512, (i + 1) * 512)
                sp.dma_start(wout[:, :, half], w_out.rearrange("a (k p) n -> p (a k) n", p=P)[:, :, half]).then_inc(w_sem[i], 16)
                load_gates(i)
            for part in range(3):
                sp.wait_ge(*filled(("tok", DNH - 1, 1, part)))
            sp.wait_ge(keys_selected, N_SEL)
            sp.dma_start(lng, ln_g.broadcast_to([P, DM])).then_inc(ln_sem, 16)
            sp.dma_start(lnb, ln_b.broadcast_to([P, DM])).then_inc(ln_sem, 16)
            for n, b in enumerate(BLOCK_ORDER):
                if n + 2 < NB:
                    sp.wait_ge(*filled(("msc", b, 1)))
                    load_queries(n + 2)
                if n:
                    sp.wait_ge(*released(("y", BLOCK_ORDER[n - 1], 0)))
                    sp.wait_ge(*released(("y", BLOCK_ORDER[n - 1], 1)))
                    if n + 1 < NB:
                        load_gates(n + 1)
                sp.dma_start(xres, xv[b]).then_inc(xr_sem, 16)
                if n:
                    sp.wait_ge(row_finished, n)
                    sp.dma_start(ov[BLOCK_ORDER[n - 1]], yres).then_inc(st_sem, 16)
            sp.wait_ge(row_finished, NB)
            sp.dma_start(ov[BLOCK_ORDER[-1]], yres).then_inc(st_sem, 16)
            sp.wait_ge(st_sem, 16 * NB)

        @block.tensor
        def _(pe):
            def group(dst, pairs):
                for i, (w, r) in enumerate(pairs):
                    last = nc.tensor.matmul(dst, w, r, start=(i == 0), stop=(i == len(pairs) - 1))
                return last

            def project(dst, name, t, chunks):
                for c in chunks:
                    hi, lo = w_hi(name)[:, c, :], w_lo(name)[:, c, :]
                    xh, xl = x_hi[:, 4 * t:4 * t + 4, c, :], x_lo[:, 4 * t:4 * t + 4, c, :]
                    nc.tensor.matmul(dst, hi, xh, start=(c == 0), stop=False)
                    nc.tensor.matmul(dst, hi, xl, start=False, stop=False)
                    last = nc.tensor.matmul(dst, lo, xh, start=False, stop=(c == KT - 1))
                return last

            def tp(dst, src, n=P):
                return nc.tensor.transpose(dst, src, ident[0:n, 0:n])

            pe.wait_ge(c_sem, 16)
            for e in plan:
                k = e[0]
                if k == "xT":
                    b, half = e[1] // 2, e[1] % 2
                    if half == 0:
                        pe.wait_ge(x_sem[b % 4], 16 * (b // 4 + 1))
                    if not first(e):
                        pe.wait_ge(*vacated(e))
                    for i in range(4):
                        c = 4 * half + i
                        last = tp(ps(e)[:, i * P:(i + 1) * P], xnat[b % 4][:, c * P:(c + 1) * P])
                    last.then_inc(fill_of(e), 1)
                elif k in ("kiT", "qiT"):
                    t = e[-1]
                    if t == 0:
                        pe.wait_ge(weights_split, order["split", group_of(e)])
                    pe.wait_ge(*released(("xT", (t + 1) * NB - 2)))
                    pe.wait_ge(*released(("xT", (t + 1) * NB - 1)))
                    if not first(e):
                        pe.wait_ge(*vacated(e))
                    project(ps(e)[:, :], group_of(e), t, range(KT)).then_inc(fill_of(e), 1)
                elif k == "small":
                    b = e[1]
                    if b == 0:
                        pe.wait_ge(weights_split, order["split", "small"])
                    if not first(e):
                        pe.wait_ge(*vacated(e))
                    hi, lo = w_hi("small"), w_lo("small")
                    group(ps(e)[:, 0:144], [pair for c in range(KT) for pair in ((x_hi[:, b, c, :], hi[:, c, :]), (x_hi[:, b, c, :], lo[:, c, :]),
                                                                                (x_lo[:, b, c, :], hi[:, c, :]))]).then_inc(fill_of(e), 1)
                elif k == "side":
                    g, t, s = e[1:]
                    key = e[:3]
                    if s == 0:
                        if t == 0:
                            pe.wait_ge(weights_split, order["split", group_of(e)])
                        if not first(key):
                            pe.wait_ge(*vacated(key))
                    last = project(ps(key)[:, :], group_of(e), t, (2 * s, 2 * s + 1))
                    if s == 3:
                        last.then_inc(fill_of(key), 1)
                elif k == "idx":
                    b, j, c = e[1:]
                    if (j, c) == (0, 0):
                        if b == 2:
                            pe.wait_ge(*released(("kiT", 0)))
                            pe.wait_ge(*released(("kiT", 1)))
                            for m in range(4):
                                for t in range(2):
                                    pe.wait_ge(*released(("qiT", m, t)))
                    lo, hi = idx_chunks(b)[c]
                    if not first(e):
                        pe.wait_ge(*vacated(e))
                    qb = q2[:, j, b * P:(b + 1) * P]
                    group(ps(e)[:, 0:hi - lo], [(qb, khi[:, lo:hi]), (qb, klo[:, lo:hi])]).then_inc(fill_of(e), 1)
                elif k == "cwT":
                    pe.wait_ge(m_sem, 48)
                    if not first(e):
                        pe.wait_ge(*vacated(e))
                    tp(ps(e)[:, 0:48], cwnat[0:48, :], 48).then_inc(fill_of(e), 1)
                elif k == "wukT":
                    if not first(e):
                        pe.wait_ge(*vacated(e))
                    tp(ps(e)[:, 0:P], wuknat[:, 0:P])
                    tp(ps(e)[:, P:2 * P], wuknat[:, P:2 * P]).then_inc(fill_of(e), 1)
                elif k == "gate_sums":
                    if not first(e):
                        pe.wait_ge(*vacated(e))
                    pe.wait_ge(gate_steps_by_dve, 2)
                    nc.tensor.matmul(ps(e)[:, 0:32], tri, s_g, start=True, stop=True)
                    nc.tensor.matmul(ps(e)[:, 32:64], ones, s_g, start=True, stop=True).then_inc(fill_of(e), 1)
                elif k == "memT":
                    m, half = e[1] // 2, e[1] % 2
                    if not first(e):
                        pe.wait_ge(*vacated(e))
                    for i in range(4):
                        c = 4 * half + i
                        last = tp(ps(e)[:, i * P:(i + 1) * P], memnat[:, m, c * P:(c + 1) * P])
                    last.then_inc(fill_of(e), 1)
                elif k == "kmT":
                    pe.wait_ge(loaded_sem[place_of["mk"] % N_SLOTS], load_need["mk"])
                    for i in range(4):
                        pe.wait_ge(*released(("memT", i)))
                    if not first(e):
                        pe.wait_ge(*vacated(e))
                    for m in range(2):
                        last = group(ps(e)[:, m * 256:(m + 1) * 256],
                                     [(raw("mk")[:, c, m * P:(m + 1) * P], memT[:, c, :]) for c in range(KT)])
                    last.then_inc(fill_of(e), 1)
                elif k == "vm":
                    pe.wait_ge(loaded_sem[place_of["mv"] % N_SLOTS], load_need["mv"])
                    if not first(e):
                        pe.wait_ge(*vacated(e))
                    for m in range(2):
                        last = group(ps(e)[:, m * 256:(m + 1) * 256],
                                     [(memT[:, c, m * P:(m + 1) * P], raw("mv")[:, c, :]) for c in range(KT)])
                    last.then_inc(fill_of(e), 1)
                elif k == "cT":
                    pe.wait_ge(gate_steps_by_dve, 3)
                    if not first(e):
                        pe.wait_ge(*vacated(e))
                    for i in range(4):
                        last = tp(ps(e)[:, i * P:(i + 1) * P], sm[:, 4 * e[1] + i, 0:P])
                    last.then_inc(fill_of(e), 1)
                elif k == "proj":
                    h, part, t, s = e[1:]
                    key = ("proj", h, part, t)
                    if s == 0:
                        if t == 0:
                            pe.wait_ge(weights_split, order["split", group_of(e)])
                        if not first(key):
                            pe.wait_ge(*vacated(key))
                    last = project(ps(key)[:, :], group_of(e), t, (2 * s, 2 * s + 1))
                    if s == 3:
                        last.then_inc(fill_of(key), 1)
                elif k == "ss":
                    h, part = e[1:]
                    key = ("ss", h)
                    pe.wait_ge(squares_ready, order[e])
                    if part == 1 and not first(key):
                        pe.wait_ge(*vacated(key))
                    at = 0 if part else NB
                    for b in range(NB):
                        last = nc.tensor.matmul(ps(key)[:, at + b:at + b + 1], hbuf[:, 3 + b * P:3 + (b + 1) * P], ones[:, 0:1],
                                                start=True, stop=True)
                    if part:
                        last.then_inc(k_squares_summed, 1)
                    else:
                        last.then_inc(fill_of(key), 1)
                elif k == "tok":
                    h, a, part = e[1:]
                    if (a, part) == (0, 1):
                        pe.wait_ge(silu_done, 3 * h + 3)
                    if not first(e):
                        pe.wait_ge(*vacated(e))
                    for i in range(4):
                        last = tp(ps(e)[:, i * P:(i + 1) * P], qkv[:, part, (4 * a + i) * P:(4 * a + i + 1) * P])
                    last.then_inc(fill_of(e), 1)
                elif k == "bT":
                    h, a, w = e[1:]
                    pe.wait_ge(*released(("tok", h, a, 1 if w < 2 else 0)))
                    if not first(e):
                        pe.wait_ge(*vacated(e))
                    src = row(a, (R_KHAT, R_KB, R_QHAT, R_QDEC)[w])
                    for i in range(4):
                        last = tp(ps(e)[:, i * P:(i + 1) * P], blk(src, i))
                    last.then_inc(fill_of(e), 1)
                elif k == "GB":
                    h, a = e[1:]
                    if not first(e):
                        pe.wait_ge(*vacated(e))
                    for i in range(4):
                        col = h * NB + 4 * a + i
                        last = nc.tensor.matmul(ps(e)[:, i * P:(i + 1) * P], s_g[:, col:col + 1].broadcast_to([P, P]), tri, start=True, stop=True)
                    last.then_inc(fill_of(e), 1)
                elif k in ("U", "At"):
                    h, a = e[1:]
                    pe.wait_ge(*released(("bT", h, a, 0)))
                    pe.wait_ge(*released(("bT", h, a, 1 if k == "U" else 2)))
                    if not first(e):
                        pe.wait_ge(*vacated(e))
                    other = row(a, R_KBT if k == "U" else R_QHATT)
                    for i in range(4):
                        last = nc.tensor.matmul(ps(e)[:, i * P:(i + 1) * P], blk(row(a, R_KHATT), i), blk(other, i), start=True, stop=True)
                    last.then_inc(fill_of(e), 1)
                elif k == "lv1":
                    h, a = e[1:]
                    pe.wait_ge(level_masked, ((h * NLEV) + 0) * 2 + a + 1)
                    if not first(e):
                        pe.wait_ge(*vacated(e))
                    for i in range(4):
                        last = tp(ps(e)[:, i * P:(i + 1) * P], blk(row(a, R_UO[0]), i))
                    last.then_inc(fill_of(e), 1)
                elif k == "M":
                    h, a, s = e[1:]
                    pe.wait_ge(level_masked, (h * NLEV + s) * 2 + a + 1)
                    if s == 1:
                        pe.wait_ge(*released(("lv1", h, a)))
                    else:
                        pe.wait_ge(*released(("XY", h, a, s - 1)))
                    if not first(e):
                        pe.wait_ge(*vacated(e))
                    for i in range(4):
                        last = nc.tensor.matmul(ps(e)[:, i * P:(i + 1) * P], blk(row(a, R_UO[s % 2]), i), blk(row(a, R_X), i), start=True, stop=True)
                    last.then_inc(fill_of(e), 1)
                elif k == "XY":
                    h, a, s = e[1:]
                    pe.wait_ge(*released(("M", h, a, s)))
                    pe.wait_ge(y_started, 2 * h + a + 1)
                    if not first(e):
                        pe.wait_ge(*vacated(e))
                    w = 1 << s
                    for i in range(4):
                        m1 = blk(row(a, R_M1), i)
                        if s < NLEV - 1:
                            last = nc.tensor.matmul(ps(e)[:, i * 64:(i + 1) * 64], blk(row(a, R_Y), i),
                                                    m1.rearrange("p (n t) -> p n t", t=2 * w)[:, :, 0:w], start=True, stop=True)
                        last = nc.tensor.matmul(ps(e)[:, 256 + i * 64:256 + (i + 1) * 64], m1,
                                                blk(row(a, R_Y), i).rearrange("p (n t) -> p n t", t=2 * w)[:, :, w:2 * w], start=True, stop=True)
                    last.then_inc(fill_of(e), 1)
                elif k == "nw":
                    h, a = e[1:]
                    pe.wait_ge(*released(("XY", h, a, NLEV - 1)))
                    pe.wait_ge(keys_decayed, 2 * h + a + 1)
                    if not first(e):
                        pe.wait_ge(*vacated(e))
                    for i in range(4):
                        last = nc.tensor.matmul(ps(e)[:, i * P:(i + 1) * P], blk(row(a, R_KBG), i), blk(row(a, R_Y), i), start=True, stop=True)
                    last.then_inc(fill_of(e), 1)
                elif k == "scanV":
                    h, b = e[1:]
                    a, i = b // 4, b % 4
                    key = ("V", h, b)
                    if i == 0:
                        pe.wait_ge(*released(("nw", h, a)))
                    if not first(key):
                        pe.wait_ge(*vacated(key))
                    last = nc.tensor.matmul(ps(key)[:, 0:P], blk(row(a, R_Y), i), blk(row(a, R_VB), i), start=True, stop=(b == 0))
                    if b:
                        pe.wait_ge(*released(("S", h, b - 1)))
                        last = nc.tensor.matmul(ps(key)[:, 0:P], blk(row(a, R_NW), i), dn_s[:, (b % 2) * P:(b % 2 + 1) * P], start=False, stop=True)
                    last.then_inc(fill_of(key), 1)
                elif k == "scanS":
                    h, b = e[1:]
                    a, i = b // 4, b % 4
                    vn = vnew[:, (b % 2) * P:(b % 2 + 1) * P]
                    pe.wait_ge(*released(("V", h, b)))
                    ko, ks = ("O", h, b), ("S", h, b)
                    if b < NB - 1:
                        if not first(ks):
                            pe.wait_ge(*vacated(ks))
                        nc.tensor.matmul(ps(ks)[:, 0:P], blk(row(a, R_KD), i), vn, start=True, stop=True).then_inc(fill_of(ks), 1)
                    if not first(ko):
                        pe.wait_ge(*vacated(ko))
                    if b:
                        nc.tensor.matmul(ps(ko)[:, 0:P], blk(row(a, R_QDECT), i), dn_s[:, (b % 2) * P:(b % 2 + 1) * P], start=True, stop=False)
                    nc.tensor.matmul(ps(ko)[:, 0:P], blk(row(a, R_ATT), i), vn, start=(b == 0), stop=True).then_inc(fill_of(ko), 1)
                elif k == "qabs":
                    b = e[1]
                    if PLACE[b] == 0:
                        pe.wait_ge(side_mem_back, 64)
                    pe.wait_ge(queries_back[PLACE[b] % 2], 32 * (PLACE[b] // 2 + 1))
                    for odd in range(2):
                        key = ("qabs", b, odd)
                        p0 = 64 * odd
                        if not first(key):
                            pe.wait_ge(*vacated(key))
                        for m in range(2):
                            last = nc.tensor.matmul(ps(key)[:, m * P:(m + 1) * P], wukT[p0:p0 + 64, m * P:(m + 1) * P],
                                                    qsTv[p0:p0 + 64, PLACE[b] % 2, m, :], start=True, stop=True)
                        last.then_inc(fill_of(key), 1)
                elif k == "sc":
                    b, h, c = e[1:]
                    if (h, c) == (0, 0):
                        pe.wait_ge(*released(("qabs", b, 0)))
                        pe.wait_ge(*released(("qabs", b, 1)))
                    lo, hi = idx_chunks(b)[c]
                    if not first(e):
                        pe.wait_ge(*vacated(e))
                    nc.tensor.matmul(ps(e)[:, 0:hi - lo], qab[:, h * P:(h + 1) * P], cT[:, lo:hi], start=True, stop=True).then_inc(fill_of(e), 1)
                elif k == "msc":
                    b, i = e[1:]
                    if not first(e):
                        pe.wait_ge(*vacated(e))
                    p0 = 64 * i
                    for m in range(2):
                        last = nc.tensor.matmul(ps(e)[:, m * 256:(m + 1) * 256], qmTv[p0:p0 + 64, PLACE[b] % 2, m, :],
                                                kmT[p0:p0 + 64, m * 256:(m + 1) * 256], start=True, stop=True)
                    last.then_inc(fill_of(e), 1)
                elif k == "pT":
                    b, kt = e[1:]
                    if kt == 0:
                        pe.wait_ge(exps_ready, SAH * (PLACE[b] + 1))
                    if not first(e):
                        pe.wait_ge(*vacated(e))
                    for h in range(SAH):
                        last = tp(ps(e)[:, h * P:(h + 1) * P], xs_of(b)[:, h, kt * P:(kt + 1) * P])
                    last.then_inc(fill_of(e), 1)
                elif k == "lat":
                    b, kt = e[1:]
                    key = ("lat", b)
                    if kt == 0:
                        if not first(key):
                            pe.wait_ge(*vacated(key))
                    pe.wait_ge(*released(("pT", b, kt)))
                    last = nc.tensor.matmul(ps(key)[:, :], sm[:, kt, 0:P], pTb[(order[e] - 1) % 3], start=(kt == 0), stop=(kt == b))
                    if kt == b:
                        last.then_inc(fill_of(key), 1)
                elif k == "mpT":
                    b, i = e[1:]
                    pe.wait_ge(*released(("msc", b, 0)))
                    pe.wait_ge(*released(("msc", b, 1)))
                    if not first(e):
                        pe.wait_ge(*vacated(e))
                    for h in range(4):
                        last = tp(ps(e)[:, h * P:(h + 1) * P], mp[:, h * 256 + i * P:h * 256 + (i + 1) * P])
                    last.then_inc(fill_of(e), 1)
                elif k == "o":
                    b = e[1]
                    pe.wait_ge(*released(("lat", b)))
                    if not first(e):
                        pe.wait_ge(*vacated(e))
                    for h in range(SAH):
                        nc.tensor.matmul(ps(e)[:, h * 64:(h + 1) * 64], latT[:, h * P:(h + 1) * P], wuv[:, h * 64:(h + 1) * 64], start=True, stop=True)
                    pe.wait_ge(*released(("mpT", b, 0)))
                    pe.wait_ge(*released(("mpT", b, 1)))
                    for h in range(4):
                        last = group(ps(e)[:, 256 + h * 64:256 + (h + 1) * 64],
                                     [(mpT[i][:, h * P:(h + 1) * P], vm[:, i * 256 + h * 64:i * 256 + (h + 1) * 64]) for i in range(2)])
                    last.then_inc(fill_of(e), 1)
                elif k == "mixT":
                    b, i = e[1:]
                    if i == 0:
                        pe.wait_ge(deltanet_scaled, PLACE[b] + 1)
                    else:
                        pe.wait_ge(*released(("o", b)))
                    if not first(e):
                        pe.wait_ge(*vacated(e))
                    for c in range(4):
                        last = tp(ps(e)[:, c * P:(c + 1) * P], mix[:, (4 * i + c) * P:(4 * i + c + 1) * P])
                    last.then_inc(fill_of(e), 1)
                elif k == "y":
                    b, i = e[1:]
                    if PLACE[b] == 0:
                        pe.wait_ge(weights_split, order["split", f"out{4 * i + 3}"])
                    if i == 0:
                        pe.wait_ge(mix_split, PLACE[b] + 1)
                    if not first(e):
                        pe.wait_ge(*vacated(e))
                    half = slice(i * 512, (i + 1) * 512)
                    pairs = []
                    for c in range(KT):
                        mh, ml = mix_hi[:, c * P:(c + 1) * P], mix_lo[:, c * P:(c + 1) * P]
                        pairs += [(mh, wout_hi[:, c, half]), (mh, wout_lo[:, c, half]), (ml, wout_hi[:, c, half])]
                    group(ps(e)[:, :], pairs).then_inc(fill_of(e), 1)

        @block.vector
        def _(dve):
            v = nc.vector
            dve_chain = ctx.enter_context(nc.semaphore("dve_chain"))
            steps = [0]

            def link(ins):
                steps[0] += 1
                ins.then_inc(dve_chain, 1)
                dve.wait_ge(dve_chain, steps[0])

            def bc(ap, n):
                return ap.unsqueeze(2).broadcast_to([P, ap.shape[1], n])

            def rep(ap, n):
                return ap.unsqueeze(1).broadcast_to([P, n, ap.shape[1]])

            def quad(ap):
                return ap.rearrange("p (b t) -> p b t", b=4)

            v.memset(hbuf[:, 0:3], 0.0)
            v.memset(eps_rms, RMS_EPS)
            v.memset(one1, 1.0)
            v.memset(candidate, 0.0)
            for b in range(2, NB):
                v.memset(n_half[:, b - 2:b - 1], (b + 1) * P - 2 * TOPK + 0.5)
            v.memset(eps_ln, LN_EPS).then_inc(small_constants_set, 1)
            for e in plan:
                k = e[0]
                if k == "xT":
                    b, cs = e[1] // 2, slice(4 * (e[1] % 2), 4 * (e[1] % 2) + 4)
                    dve.wait_ge(x_hi_ready, order[e])
                    v.tensor_tensor(x_lo[:, b, cs, :], quad(ps(e)[:, :]), x_hi[:, b, cs, :].bitcast(F32), ALU.subtract).then_inc(release_of(e), 1)
                elif k == "split":
                    name = e[1]
                    dve.wait_ge(weights_hi_ready, order[e])
                    if name[:3] == "out":
                        hi, lo, whole = out_piece(wout_hi, name), out_piece(wout_lo, name), out_piece(wout, name)
                    else:
                        hi, lo, whole = w_hi(name), w_lo(name), small_raw if name == "small" else raw(name)
                    v.tensor_tensor(lo, whole, hi.bitcast(F32), ALU.subtract).then_inc(weights_split, 1)
                elif k == "small":
                    dve.wait_ge(*filled(e))
                    v.tensor_copy(sm[:, e[1], :], ps(e)[:, 0:144]).then_inc(release_of(e), 1)
                elif k == "wis":
                    dve.wait_ge(*released(("small", NB - 1)))
                    dve.wait_ge(*released(("small", NB - 2)))
                    link(v.tensor_scalar(wis, sm[:, :, 136:144], IXH ** -0.5, None, ALU.mult))
                elif k == "kiT":
                    cols = slice(e[1] * 512, (e[1] + 1) * 512)
                    dve.wait_ge(key_hi_ready, order[e])
                    v.tensor_tensor(klo[:, cols], ps(e)[:, :], khi[:, cols].bitcast(F32), ALU.subtract).then_inc(release_of(e), 1)
                elif k == "qiT":
                    m, t = e[1:]
                    dve.wait_ge(query_hi_ready, order[e])
                    for odd in range(2):
                        hi = q2[0:64, 2 * m + odd, t * 512:(t + 1) * 512].bitcast(F32)
                        last = v.tensor_tensor(q2[64:128, 2 * m + odd, t * 512:(t + 1) * 512], ps(e)[64 * odd:64 * odd + 64, :], hi, ALU.subtract)
                    last.then_inc(release_of(e), 1)
                elif k == "side" and e[1] < 4 and e[3] == 3:
                    key = e[:3]
                    dve.wait_ge(*filled(key))
                    dve.wait_ge(side_stored, 16 * staged_at[e])
                    v.tensor_copy(stage[:, :], ps(key)[:, :]).then_inc(release_of(key), 1)
                elif k == "idx":
                    b, j, c = e[1:]
                    lo, hi = idx_chunks(b)[c]
                    r = rbuf[(order[e] - 1) % 3]
                    at = score_at(b)
                    w = wis[:, b, j:j + 1]
                    dve.wait_ge(*released(e))
                    if j == 0:
                        plain = hi - lo - (P if hi == (b + 1) * P else 0)
                        last = v.tensor_scalar(score[:, at + lo:at + lo + plain], r[:, 0:plain], w, None, ALU.mult)
                        if plain < hi - lo:
                            last = v.scalar_tensor_tensor(score[:, at + lo + plain:at + hi], r[:, plain:hi - lo], w,
                                                          cst[:, C_CAUS:C_CAUS + P], ALU.mult, ALU.add)
                    else:
                        dve.wait_ge(scores_summed, order[e] - 1)
                        last = v.scalar_tensor_tensor(score[:, at + lo:at + hi], r[:, 0:hi - lo], w,
                                                      score[:, at + lo:at + hi], ALU.mult, ALU.add)
                    last.then_inc(scores_summed, 1)
                elif k == "update":
                    it = e[1]
                    dve.wait_ge(keys_counted, N_SEL * (it + 1))
                    link(v.tensor_tensor(n_off, n_low, n_half, ALU.subtract))
                    if it == 0:
                        dve.wait_ge(bit_sem, 16)
                        link(v.tensor_scalar(t_sign, n_off, 0.0, 2.0, ALU.is_lt, ALU.mult))
                        link(v.tensor_scalar(t_sign, t_sign, -1.0, None, ALU.add))
                        v.memset(bits, 0.0)
                        v.tensor_scalar(candidate, t_sign, 2.0, None, ALU.mult).then_inc(candidates_ready, 1)
                    else:
                        bit = FLOAT_BITS - 1 - it
                        link(v.tensor_tensor(n_off, n_off, t_sign, ALU.mult))
                        link(v.tensor_scalar(bit_kept.bitcast(U32), n_off, 0.0, float(1 << bit), ALU.is_lt, ALU.mult))
                        if bit:
                            link(v.scalar_tensor_tensor(bits_tried.bitcast(U32), bit_kept.bitcast(U32), cst[:, C_BIT + bit - 1:C_BIT + bit].bitcast(U32),
                                                        bits.bitcast(U32), ALU.bitwise_or, ALU.bitwise_or))
                            v.tensor_tensor(candidate, bits_tried, t_sign, ALU.mult).then_inc(candidates_ready, 1)
                        link(v.tensor_tensor(bits.bitcast(U32), bits.bitcast(U32), bit_kept.bitcast(U32), ALU.bitwise_or))
                        if bit == 0:
                            low, carry, up = bit_kept.bitcast(U32), n_off.bitcast(U32), bits_tried.bitcast(U32)
                            link(v.tensor_scalar(carry, bits.bitcast(U32), 16, None, ALU.logical_shift_right))
                            link(v.tensor_scalar(up, carry, 16, None, ALU.logical_shift_left))
                            link(v.tensor_tensor(low, bits.bitcast(U32), up, ALU.bitwise_xor))
                            link(v.tensor_scalar(low, low, 1.0, None, ALU.add))
                            link(v.tensor_scalar(carry, low, 16, None, ALU.logical_shift_right))
                            link(v.tensor_scalar(carry, carry, 16, None, ALU.logical_shift_left))
                            link(v.tensor_tensor(low, low, carry, ALU.bitwise_xor))
                            link(v.tensor_tensor(up, up, carry, ALU.add))
                            link(v.tensor_tensor(up, up, low, ALU.bitwise_or))
                            link(v.tensor_tensor(bits, bits, t_sign, ALU.mult))
                            link(v.tensor_tensor(bits_tried, bits_tried, t_sign, ALU.mult))
                            v.tensor_tensor(t_high, bits, bits_tried, ALU.max)
                            link(v.tensor_tensor(t_low, bits, bits_tried, ALU.min))
                elif k == "reach":
                    b = e[1]
                    one = slice(b - 2, b - 1)
                    w = (b + 1) * P
                    link(v.tensor_scalar(picked_above[:, 0:w], score[:, score_at(b):score_at(b + 1)], t_high[:, one], 0.0, ALU.is_ge, ALU.add,
                                         accum_out=n_low[:, one]))
                elif k == "threshold":
                    link(v.tensor_scalar(n_off, n_low, TOPK - 0.5, None, ALU.is_ge))
                    link(v.tensor_scalar(bit_kept, n_off, 0.5, None, ALU.is_lt))
                    link(v.tensor_tensor(t_high, t_high, n_off, ALU.mult))
                    link(v.tensor_tensor(t_low, t_low, bit_kept, ALU.mult))
                    link(v.tensor_tensor(candidate, t_high, t_low, ALU.add))
                    link(v.tensor_scalar(n_off, candidate, TINY, None, ALU.is_ge))
                    link(v.scalar_tensor_tensor(n_off, candidate, -TINY, n_off, ALU.is_le, ALU.add))
                    link(v.tensor_tensor(candidate, candidate, n_off, ALU.mult))
                elif k == "cwT":
                    dve.wait_ge(*filled(e))
                    v.tensor_copy(cw[:, :], ps(e)[:, 0:48]).then_inc(release_of(e), 1)
                elif k == "gates":
                    hb = "p (h b) -> p h b"
                    dve.wait_ge(r_sem, 64)
                    link(v.tensor_tensor(s_y.rearrange(hb, h=4), sm[:, :, 132:136].rearrange("p b h -> p h b"), bc(dtb, NB), ALU.add))
                    link(v.tensor_scalar(s_neg, s_y, -1.0, None, ALU.mult))
                    v.tensor_tensor(s_neg, s_neg, s_y, ALU.min).then_inc(gate_steps_by_dve, 1)
                    dve.wait_ge(gate_steps_by_act, 1)
                    link(v.tensor_scalar(s_beta, s_beta, 1.0, None, ALU.add))
                    v.reciprocal(s_beta, s_beta)
                    link(v.scalar_tensor_tensor(s_y, s_y, 0.0, s_neg, ALU.max, ALU.add))
                    v.scalar_tensor_tensor(s_g.rearrange(hb, h=4), s_y.rearrange(hb, h=4), -1.0, bc(ealog, NB), ALU.mult, ALU.mult).then_inc(gate_steps_by_dve, 1)
                    for b in range(NB):
                        last = v.scalar_tensor_tensor(sm[:, b, 0:P], sm[:, b, 0:P], crs[:, b:b + 1], kvw, ALU.mult, ALU.mult)
                    last.then_inc(gate_steps_by_dve, 1)
                elif k == "gate_sums":
                    dve.wait_ge(*filled(e))
                    v.tensor_copy(s_G, ps(e)[:, 0:32])
                    v.tensor_copy(s_Gt, ps(e)[:, 32:64]).then_inc(release_of(e), 1)
                    dve.wait_ge(*released(e))
                    v.tensor_scalar(s_nG, s_G, -1.0, None, ALU.mult)
                    v.tensor_tensor(s_dG, s_Gt, s_G, ALU.subtract).then_inc(gate_steps_by_dve, 1)
                elif k == "memT" and e[1] % 2:
                    dve.wait_ge(*filled(e))
                    v.tensor_copy(memT[:, 4:8, (e[1] // 2) * P:(e[1] // 2 + 1) * P], quad(ps(e)[:, :])).then_inc(release_of(e), 1)
                elif k == "cT" and e[1] == 1:
                    dve.wait_ge(*filled(e))
                    v.tensor_copy(cT[:, 512:1024], ps(e)[:, :]).then_inc(release_of(e), 1)
                elif k == "conv":
                    h, part, t = e[1:]
                    dve.wait_ge(*released(("proj", h, part, t)))
                    if h and t == 0:
                        dve.wait_ge(*filled(("tok", h - 1, 1, part)))
                    y = qkv[:, part, t * 512:(t + 1) * 512]
                    tap = [cw[:, j * 12 + part * 4 + h:j * 12 + part * 4 + h + 1] for j in range(4)]
                    shifted = [hbuf[:, j + t * 512:j + (t + 1) * 512] for j in range(4)]
                    link(v.tensor_scalar(y, shifted[3], tap[3], None, ALU.mult))
                    link(v.scalar_tensor_tensor(y, shifted[2], tap[2], y, ALU.mult, ALU.add))
                    link(v.scalar_tensor_tensor(y, shifted[1], tap[1], y, ALU.mult, ALU.add))
                    v.scalar_tensor_tensor(y, shifted[0], tap[0], y, ALU.mult, ALU.add).then_inc(conv_done, 1)
                elif k == "norms":
                    h = e[1]
                    dve.wait_ge(inverse_norms_ready, h + 1)
                    dve.wait_ge(gate_steps_by_act, 2)
                    hh = slice(h * NB, (h + 1) * NB)
                    v.tensor_tensor(sc_of["kb"], rs_k, s_beta[:, hh], ALU.mult)
                    link(v.tensor_scalar(sc_of["q"], rs_q, DND ** -0.5, None, ALU.mult))
                    link(v.tensor_tensor(sc_of["qd"], sc_of["q"], s_eG[:, hh], ALU.mult))
                elif k == "tok":
                    h, a, part = e[1:]
                    if (h, a, part) == (0, 0, 1):
                        dve.wait_ge(scores_summed, seen["idx"])
                    dve.wait_ge(*filled(e))
                    src = quad(ps(e)[:, :])
                    qs_ = slice(4 * a, 4 * a + 4)
                    what = {1: ((R_KHAT, rs_k), (R_KB, sc_of["kb"])),
                            0: ((R_QHAT, sc_of["q"]), (R_QDEC, sc_of["qd"])),
                            2: ((R_VB, s_beta[:, h * NB:(h + 1) * NB]),)}[part]
                    for r, s in what:
                        last = v.tensor_tensor(quad(row(a, r)), src, bc(s[:, qs_], P), ALU.mult)
                    last.then_inc(release_of(e), 1)
                elif k == "GB":
                    h, a = e[1:]
                    dve.wait_ge(*filled(e))
                    v.tensor_tensor(quad(row(a, R_DARG)), quad(ps(e)[:, :]), rep(cst[:, C_NEG:C_NEG + P], 4), ALU.add).then_inc(release_of(e), 1)
                elif k in ("U", "At"):
                    h, a = e[1:]
                    dve.wait_ge(*filled(e))
                    dve.wait_ge(decays_ready, 2 * h + a + 1)
                    v.tensor_tensor(row(a, R_U if k == "U" else R_ATT), ps(e)[:, :], row(a, R_DEC), ALU.mult).then_inc(release_of(e), 1)
                elif k == "lv1":
                    h, a = e[1:]
                    dve.wait_ge(*filled(e))
                    v.tensor_tensor(quad(row(a, R_X)), rep(ident, 4), quad(ps(e)[:, :]), ALU.subtract).then_inc(release_of(e), 1)
                elif k == "XY":
                    h, a, s = e[1:]
                    w = 1 << s
                    dve.wait_ge(*filled(e))
                    halves = "p (n t) -> p n t"
                    if s < NLEV - 1:
                        xh = row(a, R_X).rearrange(halves, t=2 * w)[:, :, 0:w]
                        v.tensor_tensor(xh, xh, ps(e)[:, 0:256].rearrange(halves, t=w), ALU.subtract)
                    yh = row(a, R_Y).rearrange(halves, t=2 * w)[:, :, w:2 * w]
                    v.tensor_tensor(yh, yh, ps(e)[:, 256:512].rearrange(halves, t=w), ALU.subtract).then_inc(release_of(e), 1)
                elif k == "scanV":
                    h, b = e[1:]
                    key = ("V", h, b)
                    dve.wait_ge(*filled(key))
                    v.tensor_copy(vnew[:, (b % 2) * P:(b % 2 + 1) * P], ps(key)[:, 0:P]).then_inc(release_of(key), 1)
                elif k == "scanS" and e[2] < NB - 1:
                    h, b = e[1:]
                    key = ("S", h, b)
                    dve.wait_ge(*filled(key))
                    new = dn_s[:, ((b + 1) % 2) * P:((b + 1) % 2 + 1) * P]
                    if b == 0:
                        last = v.tensor_copy(new, ps(key)[:, 0:P])
                    else:
                        last = v.scalar_tensor_tensor(new, dn_s[:, (b % 2) * P:(b % 2 + 1) * P], s_gl[:, h * NB + b:h * NB + b + 1],
                                                      ps(key)[:, 0:P], ALU.mult, ALU.add)
                    last.then_inc(release_of(key), 1)
                elif k == "finals":
                    dve.wait_ge(kt_sem, 16)
                    v.tensor_tensor(dm01[:, 0:P], cst[:, C_KT + 7 * P:C_KT + 8 * P], cst[:, C_CAUS:C_CAUS + P], ALU.add)
                    v.tensor_copy(dm01[:, P:2 * P], cst[:, C_KT + 6 * P:C_KT + 7 * P])
                    link(v.tensor_tensor(dm01[:, 2 * P:3 * P], cst[:, C_KT + 7 * P:C_KT + 8 * P], cst[:, C_CAUS:C_CAUS + P], ALU.add))
                elif k == "dm":
                    b, stage_ = e[1:]
                    w = (b + 1) * P
                    one = slice(b - 2, b - 1)
                    d = score[:, score_at(b):score_at(b + 1)]
                    above, ties, rank = picked_above[:, 0:w], picked_ties[:, 0:w], tie_rank[:, 0:w]
                    if stage_ == 0:
                        link(v.tensor_scalar(above, d, candidate[:, one], 0.0, ALU.is_gt, ALU.add, accum_out=n_low[:, one]))
                    elif stage_ == 1:
                        link(v.tensor_scalar(ties, d, candidate[:, one], None, ALU.is_equal))
                    elif stage_ == 2:
                        v.tensor_scalar(n_off[:, one], n_low[:, one], -1.0, TOPK + 0.5, ALU.mult, ALU.add)
                        link(v.tensor_tensor_scan(rank, ties, ties, 0.0, ALU.add, ALU.max))
                    elif stage_ == 3:
                        link(v.scalar_tensor_tensor(ties, rank, n_off[:, one], ties, ALU.is_le, ALU.mult))
                    elif stage_ == 4:
                        link(v.scalar_tensor_tensor(ties, above, -1.0, ties, ALU.add, ALU.add))
                    else:
                        dve.wait_ge(kt_sem, 16)
                        kt0 = C_KT + (7 - b) * P
                        v.scalar_tensor_tensor(d, ties, BIG, cst[:, kt0:kt0 + w], ALU.mult, ALU.add).then_inc(keys_selected, 1)
                elif k == "sc":
                    b, h, c = e[1:]
                    lo, hi = idx_chunks(b)[c]
                    d = dm01[:, b * P:(2 * b + 1) * P] if b < 2 else score[:, score_at(b):score_at(b + 1)]
                    if (b, h, c) == (BLOCK_ORDER[0], 0, 0):
                        dve.wait_ge(keys_selected, N_SEL)
                    dve.wait_ge(*filled(e))
                    v.tensor_tensor_reduce(xs_of(b)[:, h, lo:hi], d[:, lo:hi], ps(e)[:, 0:hi - lo], 1.0, -3.0e38, ALU.add, ALU.max,
                                                   mxp[:, 2 * h + c:2 * h + c + 1]).then_inc(release_of(e), 1)
                    if c == len(idx_chunks(b)) - 1:
                        dve.wait_ge(*released(e))
                        if c:
                            link(v.tensor_tensor(mxp[:, 2 * h:2 * h + 1], mxp[:, 2 * h:2 * h + 1], mxp[:, 2 * h + 1:2 * h + 2], ALU.max))
                        v.tensor_scalar(nmx[:, h:h + 1], mxp[:, 2 * h:2 * h + 1], -SLOPES[h], None, ALU.mult).then_inc(head_max_ready, 1)
                elif k == "msc":
                    b, i = e[1:]
                    dve.wait_ge(*filled(e))
                    link(v.tensor_reduce(mmx[:, 2 * i:2 * i + 2], ps(e)[:, :].rearrange("p (h n) -> p h n", h=2), AX, ALU.max))
                    v.tensor_scalar(mmx[:, 2 * i:2 * i + 2], mmx[:, 2 * i:2 * i + 2], -0.125, None, ALU.mult).then_inc(mem_max_ready, 1)
                elif k == "pT" and e[2] % 2:
                    dve.wait_ge(*filled(e))
                    v.tensor_copy(pTb[(order[e] - 1) % 3], ps(e)[:, :]).then_inc(release_of(e), 1)
                elif k == "mpT" and e[2] == 1:
                    dve.wait_ge(*filled(e))
                    v.tensor_copy(mpT[1], ps(e)[:, :]).then_inc(release_of(e), 1)
                elif k == "rinv":
                    b = e[1]
                    dve.wait_ge(exps_ready, SAH * (PLACE[b] + 1))
                    dve.wait_ge(*released(("msc", b, 0)))
                    dve.wait_ge(*released(("msc", b, 1)))
                    if PLACE[b]:
                        dve.wait_ge(*released(("o", BLOCK_ORDER[PLACE[b] - 1])))
                    link(v.reciprocal(rinv, sums))
                elif k == "o":
                    b = e[1]
                    dve.wait_ge(*filled(e))
                    h8 = "p (h d) -> p h d"
                    v.tensor_tensor(mix[:, 512:1024].rearrange(h8, h=8), ps(e)[:, :].rearrange(h8, h=8), bc(rinv, 64), ALU.mult).then_inc(release_of(e), 1)
                elif k == "mix_split":
                    b = e[1]
                    dve.wait_ge(mix_hi_ready, PLACE[b] + 1)
                    v.tensor_tensor(mix_lo[:, :], av(MIXT_AT, DM), mix_hi[:, :].bitcast(F32), ALU.subtract).then_inc(mix_split, 1)
                elif k == "mixT":
                    b, i = e[1:]
                    dve.wait_ge(*filled(e))
                    dve.wait_ge(gates_back[PLACE[b] % 2], 16 * (PLACE[b] // 2 + 1))
                    gate = zgT[:, PLACE[b] % 2, 4 * i:4 * i + 4, :]
                    if i == 0:
                        v.scalar_tensor_tensor(quad(mixT[0]), quad(ps(e)[:, :]), nrmw, gate, ALU.mult, ALU.mult).then_inc(release_of(e), 1)
                    else:
                        v.tensor_tensor(quad(mixT[1]), quad(ps(e)[:, :]), gate, ALU.mult).then_inc(release_of(e), 1)
                elif k == "y":
                    b, i = e[1:]
                    if i == 0:
                        dve.wait_ge(xr_sem, 16 * (PLACE[b] + 1))
                        if PLACE[b]:
                            dve.wait_ge(st_sem, 16 * PLACE[b])
                    dve.wait_ge(*filled(e))
                    yh = yres[:, i * 512:(i + 1) * 512]
                    v.scalar_tensor_tensor(yh, xres[:, i * 512:(i + 1) * 512], ALPHA, ps(e)[:, :], ALU.mult, ALU.add).then_inc(release_of(e), 1)
                    dve.wait_ge(*released(e))
                    link(v.bn_stats(bst[:, 6 * i:6 * i + 6], yh))
                    if i == 1:
                        v.bn_aggr(mv, bst).then_inc(ln_stats_ready, 1)
                elif k == "ln":
                    b = e[1]
                    dve.wait_ge(ln_rstd_refined, PLACE[b] + 1)
                    v.tensor_scalar(yres, yres, mv[:, 0:1], rstd, ALU.subtract, ALU.mult).then_inc(ln_scaled, 1)
                    if b == BLOCK_ORDER[-1]:
                        dve.wait_ge(ln_scaled, NB)
                        dve.wait_ge(ln_sem, 32)
                        link(v.tensor_tensor(yres, yres, lng, ALU.mult))
                        v.tensor_tensor(yres, yres, lnb, ALU.add).then_inc(row_finished, 1)

        @block.scalar
        def _(act):
            sc = nc.scalar
            act_chain = ctx.enter_context(nc.semaphore("act_chain"))
            steps = [0]

            def link(ins):
                steps[0] += 1
                ins.then_inc(act_chain, 1)
                act.wait_ge(act_chain, steps[0])

            def copy(dst, src, scale=1.0):
                return sc.activation(dst, src, ACT.Copy, scale=scale)

            silu_loaded = [False]

            def exp_ln_table():
                if silu_loaded[0]:
                    sc.preload_act_table_set("natural_log_exp_and_others")
                    silu_loaded[0] = False

            sc.preload_act_table_set("natural_log_exp_and_others")
            act.wait_ge(small_constants_set, 1)
            for e in plan:
                k = e[0]
                if k in ("silu", "side"):
                    silu_loaded[0] = silu_loaded[0] or k == "silu" or e[1] >= 4 and e[3] == 3
                elif k in ("gates", "norms", "GB", "finals"):
                    exp_ln_table()
                if k == "xT":
                    half = 4 * (e[1] % 2)
                    act.wait_ge(*filled(e))
                    copy(x_hi[:, e[1] // 2, half:half + 4, :], ps(e)[:, :].rearrange("p (k t) -> p k t", k=4)).then_inc(x_hi_ready, 1)
                elif k == "split":
                    name = e[1]
                    if name[:3] == "out":
                        act.wait_ge(w_sem[int(name[3:]) // 4], 16)
                        copy(out_piece(wout_hi, name), out_piece(wout, name)).then_inc(weights_hi_ready, 1)
                    elif name == "small":
                        act.wait_ge(small_w_sem, 48)
                        copy(w_hi(name), small_raw).then_inc(weights_hi_ready, 1)
                    else:
                        act.wait_ge(loaded_sem[place_of[name] % N_SLOTS], load_need[name])
                        copy(w_hi(name), raw(name)).then_inc(weights_hi_ready, 1)
                elif k == "kiT":
                    act.wait_ge(*filled(e))
                    copy(khi[:, e[1] * 512:(e[1] + 1) * 512], ps(e)[:, :]).then_inc(key_hi_ready, 1)
                elif k == "qiT":
                    m, t = e[1:]
                    act.wait_ge(*filled(e))
                    for odd in range(2):
                        last = copy(q2[0:64, 2 * m + odd, t * 512:(t + 1) * 512], ps(e)[64 * odd:64 * odd + 64, :])
                    last.then_inc(query_hi_ready, 1)
                elif k == "side" and e[1] >= 4 and e[3] == 3:
                    key = e[:3]
                    act.wait_ge(*filled(key))
                    act.wait_ge(side_stored, 16 * staged_at[e])
                    sc.activation(stage[:, :], ps(key)[:, :], ACT.Silu).then_inc(release_of(key), 1)
                elif k in ("wukT", "kmT", "vm"):
                    act.wait_ge(*filled(e))
                    if staged_at[e]:
                        act.wait_ge(side_stored, 16 * staged_at[e])
                    n = 256 if k == "wukT" else 512
                    copy(stage[:, 0:n], ps(e)[:, 0:n]).then_inc(release_of(e), 1)
                elif k == "idx":
                    b, j, c = e[1:]
                    lo, hi = idx_chunks(b)[c]
                    act.wait_ge(*filled(e))
                    if order[e] > 3:
                        act.wait_ge(scores_summed, order[e] - 3)
                    sc.activation(rbuf[(order[e] - 1) % 3][:, 0:hi - lo], ps(e)[:, 0:hi - lo], ACT.Relu, scale=IXD ** -0.5).then_inc(release_of(e), 1)
                elif k == "count":
                    it, b = e[1:]
                    w = (b + 1) * P
                    if it == 0:
                        act.wait_ge(scores_summed, order["idx", b, IXH - 1, len(idx_chunks(b)) - 1])
                    else:
                        act.wait_ge(candidates_ready, it)
                    if order[e] > 2:
                        act.wait_ge(keys_counted, order[e] - 2)
                    sc.activation(signs[order[e] % 2][:, 0:w], score[:, score_at(b):score_at(b + 1)], ACT.Sign, scale=-1.0,
                                  bias=candidate[:, b - 2:b - 1], accum_out=n_low[:, b - 2:b - 1]).then_inc(keys_counted, 1)
                elif k == "gates":
                    act.wait_ge(gate_steps_by_dve, 1)
                    for b in range(NB):
                        link(sc.activation(junk[:, :], sm[:, b, 0:P], ACT.Square, accum_out=css[:, b:b + 1]))
                    sc.activation(s_beta.rearrange("p (h b) -> p h b", h=4), sm[:, :, 128:132].rearrange("p b h -> p h b"), ACT.Exp, scale=-1.0)
                    act.wait_ge(r_sem, 64)
                    sc.activation(ealog, alog, ACT.Exp)
                    link(sc.activation(s_neg, s_neg, ACT.Exp))
                    sc.activation(s_neg, s_neg, ACT.Ln, bias=one1)
                    link(sc.activation(crs, css, ACT.Ln, bias=eps_rms, scale=1.0 / RANK))
                    sc.activation(crs, crs, ACT.Exp, scale=-0.5).then_inc(gate_steps_by_act, 1)
                elif k == "gate_sums":
                    act.wait_ge(gate_steps_by_dve, 4)
                    sc.activation(s_eG, s_G, ACT.Exp)
                    sc.activation(s_eD, s_dG, ACT.Exp)
                    sc.activation(s_gl, s_Gt, ACT.Exp).then_inc(gate_steps_by_act, 1)
                elif k == "memT" and e[1] % 2 == 0:
                    act.wait_ge(*filled(e))
                    copy(memT[:, 0:4, (e[1] // 2) * P:(e[1] // 2 + 1) * P], ps(e)[:, :].rearrange("p (k t) -> p k t", k=4)).then_inc(release_of(e), 1)
                elif k == "cT" and e[1] == 0:
                    act.wait_ge(*filled(e))
                    copy(cT[:, 0:512], ps(e)[:, :]).then_inc(release_of(e), 1)
                elif k == "proj" and e[4] == 3:
                    h, part, t = e[1:4]
                    key = ("proj", h, part, t)
                    n = h * 3 + (1, 0, 2).index(part)
                    act.wait_ge(*filled(key))
                    if n and t == 0:
                        act.wait_ge(conv_done, 2 * n)
                        if part == 0:
                            act.wait_ge(k_squares_summed, h + 1)
                        if part == 2:
                            act.wait_ge(*filled(("ss", h)))
                    copy(hbuf[:, 3 + t * 512:3 + (t + 1) * 512], ps(key)[:, :]).then_inc(release_of(key), 1)
                elif k == "silu":
                    h, part = e[1:]
                    n = h * 3 + (1, 0, 2).index(part)
                    act.wait_ge(conv_done, 2 * n + 2)
                    sc.activation(qkv[:, part, :], qkv[:, part, :], ACT.Silu).then_inc(silu_done, 1)
                    if part < 2:
                        act.wait_ge(silu_done, n + 1)
                        sc.activation(hbuf[:, 3:3 + SEQ], qkv[:, part, :], ACT.Square).then_inc(squares_ready, 1)
                elif k == "norms":
                    h = e[1]
                    key = ("ss", h)
                    act.wait_ge(*filled(key))
                    if h:
                        act.wait_ge(*released(("tok", h - 1, 1, 1)))
                    rs = hsc[:, 16:32]
                    sc.activation(rs, ps(key)[:, 0:2 * NB], ACT.Ln, bias=eps_rms).then_inc(release_of(key), 1)
                    act.wait_ge(*released(key))
                    sc.activation(rs, rs, ACT.Exp, scale=-0.5).then_inc(inverse_norms_ready, 1)
                elif k == "bT":
                    h, a, w = e[1:]
                    act.wait_ge(*filled(e))
                    copy(row(a, (R_KHATT, R_KBT, R_QHATT, R_QDECT)[w]), ps(e)[:, :]).then_inc(release_of(e), 1)
                elif k == "GB":
                    h, a = e[1:]
                    act.wait_ge(*released(e))
                    for i in range(4):
                        col = h * NB + 4 * a + i
                        d = blk(row(a, R_DEC), i)
                        last = sc.activation(d, d, ACT.Exp, bias=s_nG[:, col:col + 1])
                    last.then_inc(decays_ready, 1)
                elif k == "M":
                    h, a, s = e[1:]
                    act.wait_ge(*filled(e))
                    copy(row(a, R_M1), ps(e)[:, :]).then_inc(release_of(e), 1)
                elif k == "nw":
                    h, a = e[1:]
                    act.wait_ge(*filled(e))
                    copy(row(a, R_NW), ps(e)[:, :], -1.0).then_inc(release_of(e), 1)
                elif k == "scanS":
                    h, b = e[1:]
                    key = ("O", h, b)
                    act.wait_ge(*filled(key))
                    copy(oall[:, b, h, :], ps(key)[:, 0:P])
                    if b or h:
                        act.wait_ge(*released(("O", h, b - 1) if b else ("O", h - 1, NB - 1)))
                    sc.activation(junk[:, :], ps(key)[:, 0:P], ACT.Square, accum_out=s_oss[:, b * 4 + h:b * 4 + h + 1]).then_inc(release_of(key), 1)
                elif k == "finals":
                    act.wait_ge(*released(("O", DNH - 1, NB - 1)))
                    link(sc.activation(s_orn, s_oss, ACT.Ln, bias=eps_rms, scale=1.0 / DND))
                    sc.activation(s_orn, s_orn, ACT.Exp, scale=-0.5).then_inc(output_norms_ready, 1)
                elif k == "qabs":
                    for odd in range(2):
                        key = (*e, odd)
                        act.wait_ge(*filled(key))
                        for m in range(2):
                            h = 2 * m + odd
                            last = copy(qab[:, h * P:(h + 1) * P], ps(key)[:, m * P:(m + 1) * P], SAD ** -0.5 / SLOPES[h])
                        last.then_inc(release_of(key), 1)
                elif k == "sc":
                    b, h, c = e[1:]
                    if c == len(idx_chunks(b)) - 1:
                        act.wait_ge(head_max_ready, SAH * PLACE[b] + h + 1)
                        p_ = xs_of(b)[:, h, :]
                        sc.activation(p_, p_, ACT.Exp, scale=SLOPES[h], bias=nmx[:, h:h + 1], accum_out=sums[:, h:h + 1]).then_inc(exps_ready, 1)
                elif k == "msc":
                    b, i = e[1:]
                    act.wait_ge(mem_max_ready, 2 * PLACE[b] + i + 1)
                    for m in range(2):
                        g = 2 * m + i
                        last = sc.activation(mp[:, g * 256:(g + 1) * 256], ps(e)[:, m * 256:(m + 1) * 256], ACT.Exp, scale=0.125,
                                             bias=mmx[:, 2 * i + m:2 * i + m + 1], accum_out=sums[:, 4 + g:5 + g])
                    last.then_inc(release_of(e), 1)
                elif k == "pT" and e[2] % 2 == 0:
                    act.wait_ge(*filled(e))
                    copy(pTb[(order[e] - 1) % 3], ps(e)[:, :]).then_inc(release_of(e), 1)
                elif k == "lat" and e[2] == e[1]:
                    key = ("lat", e[1])
                    act.wait_ge(*filled(key))
                    copy(latT, ps(key)[:, :]).then_inc(release_of(key), 1)
                elif k == "mpT" and e[2] == 0:
                    act.wait_ge(*filled(e))
                    copy(mpT[0], ps(e)[:, :]).then_inc(release_of(e), 1)
                elif k == "mixT" and e[2] == 1:
                    b = e[1]
                    act.wait_ge(*released(("mixT", b, 0)))
                    act.wait_ge(*released(("mixT", b, 1)))
                    copy(mix_hi[:, :], av(MIXT_AT, DM)).then_inc(mix_hi_ready, 1)
                elif k == "rstd":
                    b = e[1]
                    act.wait_ge(ln_stats_ready, PLACE[b] + 1)
                    link(sc.activation(rstd, mv[:, 1:2], ACT.Ln, bias=eps_ln))
                    sc.activation(rstd, rstd, ACT.Exp, scale=-0.5).then_inc(ln_rstd_ready, 1)

        @block.gpsimd
        def _(pool):
            g = nc.gpsimd
            pool_chain = ctx.enter_context(nc.semaphore("pool_chain"))
            steps = [0]

            def link(ins):
                steps[0] += 1
                ins.then_inc(pool_chain, 1)
                pool.wait_ge(pool_chain, steps[0])

            def rep(ap, n):
                return ap.unsqueeze(1).broadcast_to([P, n, ap.shape[1]])

            def quad(ap):
                return ap.rearrange("p (b t) -> p b t", b=4)

            def bc(ap, n):
                return ap.unsqueeze(2).broadcast_to([P, ap.shape[1], n])

            def refine(root, x, scratch):
                link(g.tensor_tensor(scratch, root, root, ALU.mult))
                link(g.tensor_tensor(scratch, scratch, x, ALU.mult))
                link(g.tensor_scalar(scratch, scratch, -0.5, 1.5, ALU.mult, ALU.add))
                return g.tensor_tensor(root, root, scratch, ALU.mult)

            pool.wait_ge(c_sem, 16)
            for e in plan:
                k = e[0]
                if k == "tok" and e[3] == 1:
                    h, a = e[1:3]
                    cols = slice(h * NB + 4 * a, h * NB + 4 * a + 4)
                    pool.wait_ge(*released(e))
                    pool.wait_ge(gate_steps_by_act, 2)
                    g.tensor_tensor(quad(row(a, R_KBG)), quad(row(a, R_KB)), bc(s_eG[:, cols], P), ALU.mult)
                    g.tensor_tensor(quad(row(a, R_KD)), quad(row(a, R_KHAT)), bc(s_eD[:, cols], P), ALU.mult).then_inc(keys_decayed, 1)
                elif k in ("lv1", "M"):
                    h, a = e[1:3]
                    s = e[3] if k == "M" else 0
                    if s == 0:
                        pool.wait_ge(*released(("U", h, a)))
                        pool.wait_ge(keys_decayed, 2 * h + a + 1)
                    elif s == 2:
                        pool.wait_ge(*filled(("lv1", h, a)))
                        pool.wait_ge(y_started, 2 * h + a + 1)
                    elif s > 2:
                        pool.wait_ge(*filled(("M", h, a, s - 2)))
                    uo = row(a, R_UO[s % 2])
                    g.tensor_tensor(quad(uo), quad(row(a, R_U)), rep(cst[:, C_LEV + s * P:C_LEV + (s + 1) * P], 4),
                                    ALU.mult).then_inc(level_masked, 1)
                    if s == 0:
                        pool.wait_ge(*released(("At", h, a)))
                        pool.wait_ge(level_masked, (h * NLEV) * 2 + a + 1)
                        g.tensor_tensor(quad(row(a, R_Y)), rep(ident, 4), quad(uo), ALU.subtract).then_inc(y_started, 1)
                elif k == "finals":
                    pool.wait_ge(output_norms_ready, 1)
                    link(g.tensor_scalar(s_y, s_oss, 1.0 / DND, RMS_EPS, ALU.mult, ALU.add))
                    link(refine(s_orn, s_y, s_tmp))
                elif k == "rstd":
                    b = e[1]
                    pool.wait_ge(ln_rstd_ready, PLACE[b] + 1)
                    link(g.tensor_scalar(s_y[:, 0:1], mv[:, 1:2], LN_EPS, None, ALU.add))
                    refine(rstd, s_y[:, 0:1], s_tmp[:, 0:1]).then_inc(ln_rstd_refined, 1)
                elif k == "deltanet_scale":
                    b = e[1]
                    if PLACE[b]:
                        pool.wait_ge(*filled(("mixT", BLOCK_ORDER[PLACE[b] - 1], 0)))
                    m = mix[:, 0:512].rearrange("p (h d) -> p h d", h=4)
                    g.tensor_tensor(m, oall[:, b, :, :], s_orn[:, 4 * b:4 * b + 4].unsqueeze(2).broadcast_to([P, 4, P]), ALU.mult).then_inc(deltanet_scaled, 1)
                elif k == "ln" and e[1] != BLOCK_ORDER[-1]:
                    b = e[1]
                    pool.wait_ge(ln_scaled, PLACE[b] + 1)
                    if PLACE[b] == 0:
                        pool.wait_ge(ln_sem, 32)
                    link(g.tensor_tensor(yres, yres, lng, ALU.mult))
                    g.tensor_tensor(yres, yres, lnb, ALU.add).then_inc(row_finished, 1)


_INS = ["x", "mem", "w_in", "conv_w", "dn_a_log", "dn_dt_bias", "dn_norm_w", "kv_norm_w", "w_uk", "w_uv", "w_mem_kv",
        "w_out", "ln_g", "ln_b"]


def kernel(**inputs):
    import numpy as _np
    import concourse.bacc as _bacc
    from concourse import mybir as _mybir
    from concourse.bass_utils import run_bass_kernel_spmd as _run

    nc = _bacc.Bacc("TRN2", target_bir_lowering=False, num_devices=1)
    arrays, args = {}, []
    for name in _INS:
        a = _np.ascontiguousarray(inputs[name])
        arrays[f"in_{name}"] = a
        args.append(nc.dram_tensor(f"in_{name}", a.shape, _mybir.dt.from_np(a.dtype), kind="ExternalInput").ap())
    consts = shape_constants()
    arrays["in_consts"] = consts
    args.append(nc.dram_tensor("in_consts", consts.shape, _mybir.dt.float32, kind="ExternalInput").ap())
    for name, shape in (("side_q", (4, P, SEQ)), ("side_z", (KT, P, SEQ)), ("side_mem", (3, P, 2 * NMEM))):
        args.append(nc.dram_tensor(name, shape, _mybir.dt.float32, kind="Internal").ap())
    args.append(nc.dram_tensor("out_y", (1, SEQ, DM), _mybir.dt.float32, kind="ExternalOutput").ap())
    build(nc, *args)
    r = _run(nc, [arrays], core_ids=[0])
    return r.results[0]["out_y"]
```
